# Optimizing a Trainium2 kernel written in Bass

```python
import jax, jax.numpy as jnp
from jax import lax
import numpy as np
import math

D_MODEL = 1024
BATCH = 1
SEQ = 512
DEPTH = 1

N_META = 16
MIX_WIDTH = D_MODEL
POOL_WIDTH = MIX_WIDTH // 2
POOL_WINDOWS = (2, 4, 8, 16)
N_POOL_GROUPS = 4
POOL_GROUP = POOL_WIDTH // N_POOL_GROUPS
GLA_HEADS = 4
GLA_VDIM = MIX_WIDTH - POOL_WIDTH
GLA_HEAD_V = GLA_VDIM // GLA_HEADS
GLA_KDIM = GLA_VDIM // 2
GLA_HEAD_K = GLA_KDIM // GLA_HEADS
GATE_RANK = 16
GATE_NORMALIZER = 16.0
CHUNK = 64
N_GROUPS = 4
EXPERTS_PER_GROUP = 4
N_EXPERTS = N_GROUPS * EXPERTS_PER_GROUP
TOP_K_IN_GROUP = 2
EXPERT_HIDDEN = D_MODEL // 4
EPS = 1e-6
IN_COLS = POOL_WIDTH + 2 * GLA_KDIM + 2 * GLA_VDIM + GATE_RANK
SPLIT_POINTS = (POOL_WIDTH,
                POOL_WIDTH + GLA_KDIM,
                POOL_WIDTH + 2 * GLA_KDIM,
                POOL_WIDTH + 2 * GLA_KDIM + GLA_VDIM,
                POOL_WIDTH + 2 * GLA_KDIM + 2 * GLA_VDIM)


def rmsnorm(x, w):
    xf = x.astype(jnp.float32)
    y = xf * lax.rsqrt(jnp.mean(xf * xf, axis=-1, keepdims=True) + EPS)
    return (y * w.astype(jnp.float32)).astype(x.dtype)

def pool_mixer(u, pool_w, pool_scale):
    B, L, _ = u.shape
    uf = u.astype(jnp.float32).reshape(B, L, N_POOL_GROUPS, POOL_GROUP)
    cs = jnp.concatenate([jnp.zeros((B, 1, N_POOL_GROUPS, POOL_GROUP), jnp.float32),
                          jnp.cumsum(uf, axis=1)], axis=1)
    t = jnp.arange(L)
    outs = []
    for g, w in enumerate(POOL_WINDOWS):
        lo = jnp.maximum(t + 1 - w, 0)
        cs_g = cs[:, :, g]
        win_sum = cs_g[:, 1:] - cs_g[:, lo]
        cnt = (t + 1 - lo).astype(jnp.float32)[None, :, None]
        outs.append(win_sum / cnt - uf[:, :, g])
    pooled = jnp.stack(outs, axis=2)
    mixed = jnp.einsum('blgc,gcd->blgd', pooled, pool_w.astype(jnp.float32))
    y = mixed.reshape(B, L, POOL_WIDTH) * pool_scale.astype(jnp.float32)
    return y.astype(u.dtype)

def gla_mixer(q, k, v, r, g_lr, w_gate_up, b_gate, gla_norm_w):
    B, L, _ = q.shape
    f32 = jnp.float32
    log_a = jax.nn.log_sigmoid(g_lr.astype(f32) @ w_gate_up.astype(f32)
                               + b_gate.astype(f32)) / GATE_NORMALIZER
    pad = CHUNK - N_META

    def heads(a, dh):
        a = jnp.pad(a.astype(f32), ((0, 0), (pad, 0), (0, 0)))
        return a.reshape(B, -1, CHUNK, GLA_HEADS, dh).transpose(0, 3, 1, 2, 4)

    qh = heads(q, GLA_HEAD_K) * (GLA_HEAD_K ** -0.5)
    kh = heads(k, GLA_HEAD_K)
    vh = heads(v, GLA_HEAD_V)
    gh = heads(log_a, GLA_HEAD_K)
    b = jnp.cumsum(gh, axis=3)
    b_last = b[:, :, :, -1:, :]
    q_t = qh * jnp.exp(b)
    k_t = kh * jnp.exp(-b)
    k_end = kh * jnp.exp(b_last - b)
    causal = jnp.tril(jnp.ones((CHUNK, CHUNK), dtype=bool))
    scores = jnp.where(causal, jnp.einsum('bhncd,bhnsd->bhncs', q_t, k_t), 0.0)
    o_intra = jnp.einsum('bhncs,bhnsv->bhncv', scores, vh)
    dS = jnp.einsum('bhncd,bhncv->bhndv', k_end, vh)
    decay = jnp.exp(b_last[:, :, :, 0, :])

    def step(S, inp):
        dS_n, dec_n = inp
        return dec_n[..., None] * S + dS_n, S

    S0 = jnp.zeros((B, GLA_HEADS, GLA_HEAD_K, GLA_HEAD_V), f32)
    _, S_start = lax.scan(step, S0, (jnp.moveaxis(dS, 2, 0), jnp.moveaxis(decay, 2, 0)))
    S_start = jnp.moveaxis(S_start, 0, 2)
    o_inter = jnp.einsum('bhncd,bhndv->bhncv', q_t, S_start)
    o = (o_intra + o_inter).transpose(0, 2, 3, 1, 4).reshape(B, -1, GLA_HEADS, GLA_HEAD_V)[:, pad:]
    o = o * lax.rsqrt(jnp.mean(o * o, axis=-1, keepdims=True) + EPS) * gla_norm_w.astype(f32)
    o = o.reshape(B, L, GLA_VDIM) * jax.nn.silu(r.astype(f32))
    return o.astype(q.dtype)

def hier_moe(x, w_rg, b_rg, w_re, b_re, w_gate, w_up, w_down):
    B, L, D = x.shape
    f32 = jnp.float32
    xt = x.reshape(-1, D)
    xf = xt.astype(f32)
    g_logits = xf @ w_rg.astype(f32) + b_rg.astype(f32)
    g_prob = jax.nn.softmax(g_logits, axis=-1)
    g_sel = jnp.argmax(g_logits, axis=-1)
    p_g = jnp.take_along_axis(g_prob, g_sel[:, None], axis=-1)
    e_logits = (xf @ w_re.astype(f32) + b_re.astype(f32)).reshape(-1, N_GROUPS, EXPERTS_PER_GROUP)
    e_logits = jnp.take_along_axis(e_logits, g_sel[:, None, None], axis=1)[:, 0]
    e_prob = jax.nn.softmax(e_logits, axis=-1)
    top_p, top_i = lax.top_k(e_prob, TOP_K_IN_GROUP)
    top_p = top_p / jnp.sum(top_p, axis=-1, keepdims=True)
    weights = p_g * top_p
    expert_id = g_sel[:, None] * EXPERTS_PER_GROUP + top_i
    combine = jnp.sum(jax.nn.one_hot(expert_id, N_EXPERTS, dtype=f32) * weights[..., None], axis=1)
    y = jnp.zeros(xf.shape, f32)
    for e in range(N_EXPERTS):
        h = jax.nn.silu(xt @ w_gate[e]) * (xt @ w_up[e])
        y = y + combine[:, e:e + 1] * (h @ w_down[e]).astype(f32)
    return y.reshape(B, L, D).astype(x.dtype)

def first_inputs(seed: int = 0) -> dict:
    key = jax.random.key(seed)
    ks = jax.random.split(key, 20)
    n = jax.random.normal
    D = D_MODEL
    return {
        "x": n(ks[0], (BATCH, SEQ, D), jnp.float32),
        "meta_tokens": n(ks[1], (N_META, D), jnp.float32),
        "norm_mix_w": 1.0 + 0.05 * n(ks[2], (DEPTH, D), jnp.float32),
        "w_in": n(ks[3], (DEPTH, D, IN_COLS), jnp.float32) * D ** -0.5,
        "w_gate_up": n(ks[4], (DEPTH, GATE_RANK, GLA_KDIM), jnp.float32) * GATE_RANK ** -0.5,
        "b_gate": 0.1 * n(ks[5], (DEPTH, GLA_KDIM), jnp.float32),
        "gla_norm_w": 1.0 + 0.05 * n(ks[6], (DEPTH, GLA_HEAD_V), jnp.float32),
        "pool_w": n(ks[7], (DEPTH, N_POOL_GROUPS, POOL_GROUP, POOL_GROUP), jnp.float32) * POOL_GROUP ** -0.5,
        "pool_scale": 1.0 + 0.05 * n(ks[8], (DEPTH, POOL_WIDTH), jnp.float32),
        "w_out": n(ks[9], (DEPTH, MIX_WIDTH, D), jnp.float32) * MIX_WIDTH ** -0.5,
        "norm_ffn_w": 1.0 + 0.05 * n(ks[10], (DEPTH, D), jnp.float32),
        "w_router_group": n(ks[11], (DEPTH, D, N_GROUPS), jnp.float32) * D ** -0.5,
        "b_router_group": 0.01 * n(ks[12], (DEPTH, N_GROUPS), jnp.float32),
        "w_router_expert": n(ks[13], (DEPTH, D, N_EXPERTS), jnp.float32) * D ** -0.5,
        "b_router_expert": 0.01 * n(ks[14], (DEPTH, N_EXPERTS), jnp.float32),
        "w_expert_gate": n(ks[15], (DEPTH, N_EXPERTS, D, EXPERT_HIDDEN), jnp.float32) * D ** -0.5,
        "w_expert_up": n(ks[16], (DEPTH, N_EXPERTS, D, EXPERT_HIDDEN), jnp.float32) * D ** -0.5,
        "w_expert_down": n(ks[17], (DEPTH, N_EXPERTS, EXPERT_HIDDEN, D), jnp.float32) * EXPERT_HIDDEN ** -0.5,
        "final_norm_w": 1.0 + 0.05 * n(ks[18], (D,), jnp.float32),
    }

def first_block(x, meta_tokens, norm_mix_w, w_in, w_gate_up, b_gate, gla_norm_w, pool_w,
              pool_scale, w_out, norm_ffn_w, w_router_group, b_router_group,
              w_router_expert, b_router_expert, w_expert_gate, w_expert_up,
              w_expert_down, final_norm_w):
    B = x.shape[0]
    meta = jnp.broadcast_to(meta_tokens[None].astype(x.dtype), (B, N_META, D_MODEL))
    h = jnp.concatenate([meta, x], axis=1)
    for l in range(DEPTH):
        u = rmsnorm(h, norm_mix_w[l])
        proj = u @ w_in[l]
        pool_v, q, k, v, r, g_lr = jnp.split(proj, SPLIT_POINTS, axis=-1)
        y_pool = pool_mixer(pool_v, pool_w[l], pool_scale[l])
        y_gla = gla_mixer(q, k, v, r, g_lr, w_gate_up[l], b_gate[l], gla_norm_w[l])
        h = h + jnp.concatenate([y_pool, y_gla], axis=-1) @ w_out[l]
        h = h + hier_moe(rmsnorm(h, norm_ffn_w[l]), w_router_group[l], b_router_group[l],
                         w_router_expert[l], b_router_expert[l], w_expert_gate[l],
                         w_expert_up[l], w_expert_down[l])
    return rmsnorm(h, final_norm_w)[:, N_META:]


DEPTH_2 = 2

HEAD_DIM = 64
N_HEADS_TOTAL = D_MODEL // HEAD_DIM
N_SB_HEADS = N_HEADS_TOTAL // 4
DIL_GROUPS = ((128, 1), (512, 4), (2048, 16))
N_DIL_GROUPS = len(DIL_GROUPS)
HEADS_PER_GROUP = (N_HEADS_TOTAL - N_SB_HEADS) // N_DIL_GROUPS
N_DIL_HEADS = HEADS_PER_GROUP * N_DIL_GROUPS
D_DIL = N_DIL_HEADS * HEAD_DIM
D_DIL_OUT = HEADS_PER_GROUP * HEAD_DIM
D_SB = N_SB_HEADS * HEAD_DIM
D_IN = 3 * D_DIL + 3 * D_SB + 2 * D_MODEL
D_FF = 128 * ((8 * D_MODEL // 3 + 127) // 128)
ROPE_THETA = 500000.0
ROPE_DIM = HEAD_DIM // 4
Q_BLOCK = 128
RMS_EPS = 1e-6


def rms_norm(x, gain):
    xf = x.astype(jnp.float32)
    xf = xf * lax.rsqrt(jnp.mean(xf * xf, axis=-1, keepdims=True) + RMS_EPS)
    return (xf * gain.astype(jnp.float32)).astype(x.dtype)

def swiglu(x, w_gate, w_up, w_down):
    return (jax.nn.silu(x @ w_gate) * (x @ w_up)) @ w_down

def rope_tables(seq_len):
    pos = jnp.arange(seq_len, dtype=jnp.float32)
    inv_freq = ROPE_THETA ** (-jnp.arange(0, ROPE_DIM, 2, dtype=jnp.float32) / ROPE_DIM)
    ang = pos[:, None] * inv_freq[None, :]
    return jnp.cos(ang), jnp.sin(ang)

def apply_partial_rope(x, cos, sin):
    half = ROPE_DIM // 2
    x1 = x[..., :half]
    x2 = x[..., half:ROPE_DIM]
    c = cos.astype(x.dtype)
    s = sin.astype(x.dtype)
    return jnp.concatenate([x1 * c - x2 * s, x2 * c + x1 * s, x[..., ROPE_DIM:]], axis=-1)

def dilated_window_attention(q, k, v, window, dilation):
    B, H, T, dh = q.shape
    span = window // dilation
    unit = span * dilation
    t_pad = -(-T // unit) * unit
    n_sub = t_pad // dilation
    n_blk = n_sub // span

    def to_blocks(a):
        a = jnp.pad(a, ((0, 0), (0, 0), (0, t_pad - T), (0, 0)))
        a = a.reshape(B, H, n_sub, dilation, dh).transpose(0, 1, 3, 2, 4)
        return a.reshape(B, H, dilation, n_blk, span, dh)

    qb, kb, vb = to_blocks(q), to_blocks(k), to_blocks(v)

    def with_prev(a):
        prev = jnp.pad(a, ((0, 0), (0, 0), (0, 0), (1, 0), (0, 0), (0, 0)))[:, :, :, :-1]
        return jnp.concatenate([prev, a], axis=4)

    kw, vw = with_prev(kb), with_prev(vb)
    s = jnp.einsum('bhrnqd,bhrnkd->bhrnqk', qb, kw).astype(jnp.float32) * (dh ** -0.5)
    qi = jnp.arange(span)[:, None]
    kj = jnp.arange(2 * span)[None, :]
    dist = qi + span - kj
    band = (dist >= 0) & (dist <= span)
    blk = jnp.arange(n_blk)[:, None, None]
    valid = band[None] & ((blk > 0) | (kj >= span)[None])
    s = jnp.where(valid, s, -jnp.inf)
    m = jnp.max(s, axis=-1, keepdims=True)
    p = jnp.exp(s - m)
    denom = jnp.sum(p, axis=-1, keepdims=True)
    o = jnp.einsum('bhrnqk,bhrnkd->bhrnqd', p, vw.astype(jnp.float32)) / denom
    lse = (m + jnp.log(denom))[..., 0]
    o = o.reshape(B, H, dilation, n_sub, dh).transpose(0, 1, 3, 2, 4).reshape(B, H, t_pad, dh)[:, :, :T]
    lse = lse.reshape(B, H, dilation, n_sub).transpose(0, 1, 3, 2).reshape(B, H, t_pad)[:, :, :T]
    return o, lse

def stick_breaking_attention(q, k, v):
    B, H, T, dh = q.shape
    n_blk = T // Q_BLOCK
    qb = q.reshape(B, H, n_blk, Q_BLOCK, dh).transpose(2, 0, 1, 3, 4)
    kpos = jnp.arange(T)
    vf = v.astype(jnp.float32)

    def block(args):
        q_blk, b = args
        z = jnp.einsum('bhqd,bhkd->bhqk', q_blk, k).astype(jnp.float32) * (dh ** -0.5)
        qpos = b * Q_BLOCK + jnp.arange(Q_BLOCK)
        past = kpos[None, :] < qpos[:, None]
        log_beta = jax.nn.log_sigmoid(z)
        log_keep = jnp.where(past, jax.nn.log_sigmoid(-z), 0.0)
        after = lax.cumsum(log_keep, axis=3, reverse=True) - log_keep
        w = jnp.where(past, jnp.exp(log_beta + after), 0.0)
        return jnp.einsum('bhqk,bhkd->bhqd', w, vf)

    o = lax.map(block, (qb, jnp.arange(n_blk)))
    return o.transpose(1, 2, 0, 3, 4).reshape(B, H, T, dh).astype(q.dtype)

def hybrid_mixer(h, w_in, w_proj_dil, w_proj_sb, w_out, cos, sin):
    B, T, _ = h.shape
    proj = h @ w_in
    o1 = 3 * D_DIL
    o2 = o1 + 3 * D_SB
    o3 = o2 + D_MODEL
    qkv_d = proj[..., :o1].reshape(B, T, 3, N_DIL_HEADS, HEAD_DIM).transpose(2, 0, 3, 1, 4)
    q_d = apply_partial_rope(qkv_d[0], cos, sin)
    k_d = apply_partial_rope(qkv_d[1], cos, sin)
    v_d = qkv_d[2]
    outs, lses = [], []
    for g, (window, dilation) in enumerate(DIL_GROUPS):
        hs = slice(g * HEADS_PER_GROUP, (g + 1) * HEADS_PER_GROUP)
        o, lse = dilated_window_attention(q_d[:, hs], k_d[:, hs], v_d[:, hs], window, dilation)
        outs.append(o)
        lses.append(lse)
    w_grp = jax.nn.softmax(jnp.stack(lses, axis=0), axis=0)
    o_dil = jnp.sum(w_grp[..., None] * jnp.stack(outs, axis=0), axis=0).astype(h.dtype)
    o_dil = o_dil.transpose(0, 2, 1, 3).reshape(B, T, D_DIL_OUT)
    qkv_s = proj[..., o1:o2].reshape(B, T, 3, N_SB_HEADS, HEAD_DIM).transpose(2, 0, 3, 1, 4)
    o_sb = stick_breaking_attention(qkv_s[0], qkv_s[1], qkv_s[2])
    o_sb = o_sb.transpose(0, 2, 1, 3).reshape(B, T, D_SB)
    gate_dil = jax.nn.sigmoid(proj[..., o2:o3])
    gate_sb = jax.nn.sigmoid(proj[..., o3:])
    y = gate_dil * (o_dil @ w_proj_dil) + gate_sb * (o_sb @ w_proj_sb)
    return y @ w_out

def second_inputs(seed: int = 0) -> dict:
    key = jax.random.key(seed)
    ks = jax.random.split(key, 16)
    f32 = jnp.float32

    def dense(k, shape, fan_in):
        return jax.random.normal(k, shape, f32) * (fan_in ** -0.5)

    def gain(k, shape):
        return 1.0 + 0.05 * jax.random.normal(k, shape, f32)

    return {
        "x": jax.random.normal(ks[0], (BATCH, SEQ, D_MODEL), f32),
        "norm_ffn1": gain(ks[1], (DEPTH_2, D_MODEL)),
        "ffn1_w_gate": dense(ks[2], (DEPTH_2, D_MODEL, D_FF), D_MODEL),
        "ffn1_w_up": dense(ks[3], (DEPTH_2, D_MODEL, D_FF), D_MODEL),
        "ffn1_w_down": dense(ks[4], (DEPTH_2, D_FF, D_MODEL), D_FF),
        "norm_mix": gain(ks[5], (DEPTH_2, D_MODEL)),
        "w_in": dense(ks[6], (DEPTH_2, D_MODEL, D_IN), D_MODEL),
        "w_proj_dil": dense(ks[7], (DEPTH_2, D_DIL_OUT, D_MODEL), D_DIL_OUT),
        "w_proj_sb": dense(ks[8], (DEPTH_2, D_SB, D_MODEL), D_SB),
        "w_out": dense(ks[9], (DEPTH_2, D_MODEL, D_MODEL), D_MODEL),
        "norm_ffn2": gain(ks[10], (DEPTH_2, D_MODEL)),
        "ffn2_w_gate": dense(ks[11], (DEPTH_2, D_MODEL, D_FF), D_MODEL),
        "ffn2_w_up": dense(ks[12], (DEPTH_2, D_MODEL, D_FF), D_MODEL),
        "ffn2_w_down": dense(ks[13], (DEPTH_2, D_FF, D_MODEL), D_FF),
        "norm_final": gain(ks[14], (D_MODEL,)),
    }

def second_block(x, norm_ffn1, ffn1_w_gate, ffn1_w_up, ffn1_w_down, norm_mix, w_in,
              w_proj_dil, w_proj_sb, w_out, norm_ffn2, ffn2_w_gate, ffn2_w_up,
              ffn2_w_down, norm_final):
    T = x.shape[1]
    cos, sin = rope_tables(T)
    for l in range(DEPTH_2):
        x = x + 0.5 * swiglu(rms_norm(x, norm_ffn1[l]), ffn1_w_gate[l], ffn1_w_up[l], ffn1_w_down[l])
        x = x + hybrid_mixer(rms_norm(x, norm_mix[l]), w_in[l], w_proj_dil[l], w_proj_sb[l],
                             w_out[l], cos, sin)
        x = x + 0.5 * swiglu(rms_norm(x, norm_ffn2[l]), ffn2_w_gate[l], ffn2_w_up[l], ffn2_w_down[l])
    return rms_norm(x, norm_final)


def setup_inputs(seed=0):
    out = dict(first_inputs(seed))
    for name, value in second_inputs(seed + 1).items():
        if name != "x":
            out[name + "_2"] = value
    return out


def reference(
    x, meta_tokens, norm_mix_w, w_in, w_gate_up, b_gate, gla_norm_w, pool_w, pool_scale, w_out,
    norm_ffn_w, w_router_group, b_router_group, w_router_expert, b_router_expert, w_expert_gate,
    w_expert_up, w_expert_down, final_norm_w, norm_ffn1_2, ffn1_w_gate_2, ffn1_w_up_2,
    ffn1_w_down_2, norm_mix_2, w_in_2, w_proj_dil_2, w_proj_sb_2, w_out_2, norm_ffn2_2,
    ffn2_w_gate_2, ffn2_w_up_2, ffn2_w_down_2, norm_final_2,
):
    x = first_block(
        x, meta_tokens, norm_mix_w, w_in, w_gate_up, b_gate, gla_norm_w, pool_w, pool_scale,
        w_out, norm_ffn_w, w_router_group, b_router_group, w_router_expert, b_router_expert,
        w_expert_gate, w_expert_up, w_expert_down, final_norm_w,
    )
    return second_block(
        x, norm_ffn1_2, ffn1_w_gate_2, ffn1_w_up_2, ffn1_w_down_2, norm_mix_2, w_in_2,
        w_proj_dil_2, w_proj_sb_2, w_out_2, norm_ffn2_2, ffn2_w_gate_2, ffn2_w_up_2,
        ffn2_w_down_2, norm_final_2,
    )


_drawn_inputs = setup_inputs


def setup_inputs(seed=0):
    import zlib

    import numpy as np

    out = dict(_drawn_inputs(seed))
    spreads = {}
    factors = {'b_router_group': 4.066, 'b_router_expert': 6.707}
    for name, (base, spread) in spreads.items():
        noise = np.random.default_rng([zlib.crc32(name.encode()), seed]).standard_normal(out[name].shape)
        drawn = base * np.exp(spread * noise) if base else spread * noise
        out[name] = __import__('jax').numpy.asarray(drawn.astype(out[name].dtype))
    for name, factor in factors.items():
        out[name] = (out[name] * factor).astype(out[name].dtype)
    return out
```

```python
from contextlib import ExitStack

import numpy as np

import concourse.bass as bass
from concourse import mybir

F32 = mybir.dt.float32
F32R = mybir.dt.float32r
BF16 = mybir.dt.bfloat16
I32 = mybir.dt.int32
ALU = mybir.AluOpType
ACT = mybir.ActivationFunctionType
AX = mybir.AxisListType.X

P = 128
T = 512
D = 1024
DC = D // P
TB = T // P
META = 16
POOL_WINDOWS = (2, 4, 8, 16)
GATE_RANK = 16
GLA_HEADS, GLA_K, GLA_V, CHUNK = 4, 64, 128, 64
N_CHUNK = T // CHUNK
N_GROUPS, PER_GROUP = 4, 4
N_EXPERTS = N_GROUPS * PER_GROUP
ROUTES = N_GROUPS + N_EXPERTS
EPS = 1e-6
DEPTH_2 = 2
HEAD = 64
SLOTS = 4
DILATIONS = (1, 4, 16)
WINDOWS = (128, 512, 2048)
ROPE_DIM = HEAD // 4
ROPE_THETA = 500000.0
D_FF = 2816
FF_GROUPS = (8, 8, 6)
MASKED = -1e30

RAW = 3
SPLIT = 3
AHEAD = 2
PANEL = DC * P


def matrix_panels(rows, cols, k_groups=None, width=P):
    out, r = [], 0
    for kc in k_groups or (rows // P,):
        for c in range(0, cols, width):
            out.append((r, kc * P, c, min(width, cols - c)))
        r += kc * P
    return out


def weight_matrices():
    m = {
        "pool": matrix_panels(D, 512), "q": matrix_panels(D, 256), "k": matrix_panels(D, 256),
        "v": matrix_panels(D, 512), "r": matrix_panels(D, 512), "g": matrix_panels(D, GATE_RANK),
        "out": matrix_panels(D, D), "route": matrix_panels(D, ROUTES),
        "moe_gate": matrix_panels(D, 4096), "moe_up": matrix_panels(D, 4096),
        "moe_down": matrix_panels(4096, D, (8,) * 4),
    }
    for l in range(DEPTH_2):
        for f in (1, 2):
            m[f"ff{f}_gate_{l}"] = matrix_panels(D, D_FF)
            m[f"ff{f}_up_{l}"] = matrix_panels(D, D_FF)
            m[f"ff{f}_down_{l}"] = matrix_panels(D_FF, D, FF_GROUPS)
        m[f"in_{l}"] = matrix_panels(D, 5120)
        m[f"proj_dil_{l}"] = matrix_panels(256, D)
        m[f"proj_sb_{l}"] = matrix_panels(256, D)
        m[f"out_{l}"] = matrix_panels(D, D)
    return m


def ffn_order(gate, up, down, groups):
    out, j = [], 0
    for g, n in enumerate(groups):
        for i in range(n):
            out += [(gate, j), (up, j)]
            j += 1
        out += [(down, g * DC + m) for m in range(DC)]
    return out


def weight_order():
    o = [("g", 0)] + [("k", i) for i in range(2)] + [("v", i) for i in range(4)]
    o += [("q", i) for i in range(2)]
    for i in range(4):
        o += [("pool", i), ("r", i)]
    o += [("out", i) for i in range(DC)]
    o += [("route", 0)]
    o += ffn_order("moe_gate", "moe_up", "moe_down", (8,) * 4)
    for l in range(DEPTH_2):
        o += ffn_order(f"ff1_gate_{l}", f"ff1_up_{l}", f"ff1_down_{l}", FF_GROUPS)
        o += [(f"in_{l}", i) for i in range(40)]
        for m in range(DC):
            o += [(f"proj_dil_{l}", m), (f"proj_sb_{l}", m)]
        o += [(f"out_{l}", m) for m in range(DC)]
        o += ffn_order(f"ff2_gate_{l}", f"ff2_up_{l}", f"ff2_down_{l}", FF_GROUPS)
    return o


class Engine:

    def __init__(self, sem):
        self.sem, self.count, self.ops, self.reached = sem, 0, [], {}
        self.last = None

    def wait(self, *marks):
        for m in marks:
            if m is None:
                continue
            if isinstance(m, list):
                self.wait(*m)
                continue
            sem, value = m
            if self.reached.get(id(sem), 0) < value:
                self.reached[id(sem)] = value
                self.ops.append(lambda e, s=sem, v=value: e.wait_ge(s, v))

    def run(self, make, *marks):
        self.wait(*marks)
        self.ops.append(make)

    def do(self, make, *marks):
        self.wait(*marks)
        self.count += 1
        self.ops.append(lambda e: make(e).then_inc(self.sem, 1))
        self.last = (self.sem, self.count)
        return self.last


def build(nc, dram, out):
    matrices, order = weight_matrices(), weight_order()
    stack = ExitStack()
    with stack:
        def sb(where, name, shape, dt=F32):
            return where.enter_context(nc.sbuf_tensor(name, shape, dt))

        def sem(name):
            return stack.enter_context(nc.semaphore(name))

        pe, act, dve, pool = (Engine(sem(f"{n}_done")) for n in ("pe", "act", "dve", "pool"))
        sync = Engine(sem("sync_unused"))

        bank_l = [stack.enter_context(nc.psum_tensor(f"bank_l{i}", [P, 512], F32)) for i in range(2)]
        bank_s = stack.enter_context(nc.psum_tensor("bank_s", [P, 3, 512], F32))
        bank_t = [stack.enter_context(nc.psum_tensor(f"bank_t{i}", [P, 512], F32)) for i in range(2)]
        bank_o = stack.enter_context(nc.psum_tensor("bank_o", [P, 512], F32))
        free_l, free_s, free_t, free_o = [[], []], [[], [], []], [[], []], [[]]

        x = sb(stack, "x", [P, DC, T])
        xg_hi = sb(stack, "xg_hi", [P, DC, T], F32R)
        xg_lo = sb(stack, "xg_lo", [P, DC, T], F32R)
        rstd = sb(stack, "rstd", [P, T])
        squares = sb(stack, "squares", [P, 2, T])
        square_sum = sb(stack, "square_sum", [P, T])
        w_raw = sb(stack, "w_raw", [P, RAW, PANEL])
        w_hi = sb(stack, "w_hi", [P, SPLIT, PANEL], F32R)
        w_lo = sb(stack, "w_lo", [P, SPLIT, PANEL], F32R)
        n_gain = 3 + 3 * DEPTH_2 + 1
        gains = sb(stack, "gains", [P, n_gain * DC])
        ident = sb(stack, "ident", [P, P])
        ident_bf = sb(stack, "ident_bf", [P, P], BF16)
        ones = sb(stack, "ones", [P, P])

        loads = {}

        def load(name, dst, src):
            s = sem(f"load_{name}")
            sync.ops.append(lambda e: e.dma_start(dst, src).then_inc(s, 16))
            loads[name] = (s, 16)
            return loads[name]

        for c in range(DC):
            load(f"x{c}", x[:, c, :], dram["x_t"][:, c, :])
            if c == 0:
                load("gains", gains[:, :], dram["gains"])
                load("ones", ones[:, :], dram["ones"])
        load("ident", ident[:, :], dram["ident"])
        ident_bf_ready = act.do(lambda e: e.activation(ident_bf[:, :], ident[:, :], ACT.Copy),
                                loads["ident"])

        def gain(g, c):
            return gains[:, g * DC + c:g * DC + c + 1]

        raw_arrived = [sem(f"raw_arrived{i}") for i in range(RAW)]
        raw_split = [None] * RAW
        slot_used = [None] * SPLIT
        split_ready = {}
        stream = {"split": 0, "next": 0}

        def panel_shape(i):
            name, j = order[i]
            r, rows, c, cols = matrices[name][j]
            return rows // P, cols

        def split_panel():
            i = stream["split"]
            if i == len(order):
                return
            stream["split"] += 1
            name, j = order[i]
            at = sum(p[1] * p[3] for p in matrices[name][:j])
            kc, cols = panel_shape(i)
            n, raw, slot = kc * cols, i % RAW, i % SPLIT
            src = dram[name][at:at + P * n].rearrange("(p w) -> p w", p=P)
            sync.wait(raw_split[raw])
            sync.ops.append(lambda e: e.dma_start(w_raw[:, raw, 0:n], src).then_inc(raw_arrived[raw], 16))
            arrived = (raw_arrived[raw], 16 * (i // RAW + 1))
            rounded = act.do(lambda e: e.activation(w_hi[:, slot, 0:n], w_raw[:, raw, 0:n], ACT.Copy),
                             arrived, slot_used[slot], split_ready.get(i - SPLIT))
            split_ready[i] = dve.do(
                lambda e: e.tensor_tensor(w_lo[:, slot, 0:n], w_raw[:, raw, 0:n],
                                          w_hi[:, slot, 0:n].bitcast(F32), ALU.subtract),
                arrived, rounded, slot_used[slot])
            raw_split[raw] = split_ready[i]

        def product(name, hi, lo, outs, ready, bank_free):
            i = stream["next"]
            assert order[i][0] == name, (order[i], name)
            stream["next"] += 1
            while stream["split"] <= min(i + AHEAD, len(order) - 1):
                split_panel()
            kc, cols = panel_shape(i)
            slot = i % SPLIT
            pe.wait(split_ready[i])
            pe.wait(bank_free)
            parts = [(w_hi, 0), (w_hi, 1), (w_lo, 0)]
            for c in range(kc):
                pe.wait(ready[c] if ready else None)
                for n, (w, part) in enumerate(parts):
                    lhs = w[:, slot, c * cols:(c + 1) * cols]
                    for dst, src_hi, src_lo in [(outs, hi, lo)] if not isinstance(outs, list) else [
                            (o, h, g) for o, h, g in zip(outs, hi, lo)]:
                        src = (src_hi if part == 0 else src_lo)(c)
                        first, last = c == 0 and n == 0, c == kc - 1 and n == 2
                        op = (lambda e, d=dst, a=lhs, b=src, f=first, z=last:
                              e.matmul(d, a, b, start=f, stop=z))
                        if last and (not isinstance(outs, list) or dst is outs[-1]):
                            done = pe.do(op)
                        else:
                            pe.run(op)
            slot_used[slot] = done
            return done

        turn = {"l": 0, "t": 0, "s": 0}

        def next_l():
            turn["l"] ^= 1
            return turn["l"]

        def next_t():
            turn["t"] ^= 1
            return turn["t"]

        xg_ready = [None] * DC
        x_written = [None] * DC
        x_read = [None] * DC
        state = {"xg_used": None, "sum_used": None, "rstd": None, "rstd_read": None}
        square_read = [None, None]
        sum_mark = [None]

        def fence():
            marks = [e.last for e in (pe, act, dve, pool)]
            for e in (act, dve, pool):
                e.wait(*marks)

        def x_product(name, bank=None):
            b = next_l() if bank is None else bank
            kc, cols = panel_shape(stream["next"])
            done = product(name, lambda c: xg_hi[:, c, :], lambda c: xg_lo[:, c, :],
                           bank_l[b][0:cols, :], xg_ready, free_l[b])
            state["xg_used"] = done
            return b, done

        def add_square(c, written):
            if c == 0:
                sum_mark[0] = act.do(lambda e: e.activation(square_sum[:, :], x[:, 0, :], ACT.Square),
                                     written, state["sum_used"], sum_mark[0])
                x_read[0] = [sum_mark[0]]
                return
            half = c % 2
            squared = act.do(lambda e: e.activation(squares[:, half, :], x[:, c, :], ACT.Square),
                             written, square_read[half])
            sum_mark[0] = dve.do(lambda e: e.tensor_tensor(square_sum[:, :], square_sum[:, :],
                                                           squares[:, half, :], ALU.add),
                                 squared, sum_mark[0])
            square_read[half] = sum_mark[0]
            x_read[c] = [squared]

        def split_x(c, g, written):
            rounded = act.do(lambda e: e.activation(xg_hi[:, c, :], x[:, c, :], ACT.Copy, scale=gain(g, c)),
                             written, state["xg_used"], xg_ready[c], loads["gains"])
            xg_ready[c] = dve.do(
                lambda e: e.scalar_tensor_tensor(xg_lo[:, c, :], x[:, c, :], gain(g, c),
                                                 xg_hi[:, c, :].bitcast(F32), ALU.mult, ALU.subtract),
                written, rounded, state["xg_used"], loads["gains"])
            x_read[c] = (x_read[c] or []) + [rounded, xg_ready[c]]

        def token_rstd():
            summed = pe.do(lambda e: e.matmul(bank_o[:, :], ones[:, :], square_sum[:, :],
                                              start=True, stop=True),
                           sum_mark[0], free_o[0], loads["ones"])
            state["sum_used"] = summed
            logged = act.do(lambda e: e.activation(rstd[:, :], bank_o[:, :], ACT.Ln,
                                                   scale=1.0 / D, bias=eps_col[:, 0:1]),
                            summed, dve.last, eps_ready)
            free_o[0] = logged
            state["rstd"] = act.do(lambda e: e.activation(rstd[:, :], rstd[:, :], ACT.Exp, scale=-0.5), logged)

        eps_col = sb(stack, "eps_col", [P, 1])
        eps_ready = dve.do(lambda e: e.memset(eps_col[:, :], EPS))

        def add_to_x(c, bank, done, factor, g=None, stats=True):
            written = dve.do(
                lambda e: e.scalar_tensor_tensor(x[:, c, :], bank_l[bank][:, :], factor, x[:, c, :],
                                                 ALU.mult, ALU.add),
                done, x_read[c], x_written[c])
            free_l[bank] = written
            x_written[c] = written
            x_read[c] = None
            if stats:
                add_square(c, written)
            if g is not None:
                split_x(c, g, written)

        def split_value(hi, lo, value, marks, free=None):
            rounded = act.do(lambda e: e.activation(hi, value, ACT.Copy), marks, free)
            return dve.do(lambda e: e.tensor_tensor(lo, value, hi.bitcast(F32), ALU.subtract), rounded, free)

        def feed_forward(tag, gate, up, down, groups, factor, g, expert_scale=None, stats=True):
            fence()
            with ExitStack() as phase:
                hid_hi = sb(phase, f"hid_hi_{tag}", [P, 8, T], F32R)
                hid_lo = sb(phase, f"hid_lo_{tag}", [P, 8, T], F32R)
                gated = sb(phase, f"gated_{tag}", [P, 2, T])
                silu = sb(phase, f"silu_{tag}", [P, 2, T])
                val = sb(phase, f"val_{tag}", [P, 2, T])
                if expert_scale:
                    expert_scale = expert_scale(phase)
                hid_used, j = None, 0
                silu_read, val_read, gated_read = [None] * 2, [None] * 2, [None] * 2
                val_written = [None] * 2
                silu_w, gated_w = [None] * 2, [None] * 2
                for n_group, n in enumerate(groups):
                    hid_ready = [None] * n
                    for i in range(n):
                        h = j % 2
                        bg, gate_done = x_product(gate)
                        gated_w[h] = dve.do(lambda e, h=h, b=bg: e.tensor_tensor(
                            gated[:, h, :], bank_l[b][:, :], rstd[:, :], ALU.mult),
                            gate_done, state["rstd"], gated_read[h])
                        free_l[bg] = gated_w[h]
                        silu_w[h] = act.do(lambda e, h=h: e.activation(silu[:, h, :], gated[:, h, :], ACT.Silu),
                                           gated_w[h], silu_read[h])
                        gated_read[h] = silu_w[h]
                        scale, scale_mark = (rstd[:, :], state["rstd"]) if not expert_scale else expert_scale(j)
                        bu, up_done = x_product(up)
                        product_w = dve.do(lambda e, h=h, b=bu: e.tensor_tensor(
                            val[:, h, :], bank_l[b][:, :], silu[:, h, :], ALU.mult),
                            up_done, silu_w[h], val_read[h])
                        free_l[bu] = product_w
                        silu_read[h] = product_w
                        val_w = dve.do(lambda e, h=h, s=scale: e.tensor_tensor(
                            val[:, h, :], val[:, h, :], s, ALU.mult), product_w, scale_mark)
                        hid_ready[i] = split_value(hid_hi[:, i, :], hid_lo[:, i, :], val[:, h, :],
                                                   val_w, hid_used)
                        val_read[h] = hid_ready[i]
                        j += 1
                    last = n_group == len(groups) - 1
                    for m in range(DC):
                        b = next_l()
                        hid_used = product(down, lambda c: hid_hi[:, c, :], lambda c: hid_lo[:, c, :],
                                           bank_l[b][:, :], hid_ready, free_l[b])
                        add_to_x(m, b, hid_used, factor, g if last else None, stats and last)
                        if last and m == DC - 1:
                            token_rstd()

        def transpose_to(dst, src, n_out, n_in, t, at, marks):
            return pe.do(lambda e: e.transpose(bank_t[t][0:n_out, at:at + n_in], src, ident[0:n_in, 0:n_in]),
                         marks, loads["ident"])

        def mixer_1():
            L = META + T
            with ExitStack() as phase:
                meta = sb(phase, "meta", [P, DC, META])
                meta_hi = sb(phase, "meta_hi", [P, DC, META], F32R)
                meta_lo = sb(phase, "meta_lo", [P, DC, META], F32R)
                meta_sq = sb(phase, "meta_sq", [P, DC, META])
                meta_sum = sb(phase, "meta_sum", [P, META])
                meta_rstd = sb(phase, "meta_rstd", [P, META])
                meta_g = sb(phase, "meta_g", [P, DC, META])
                gate_up = sb(phase, "gate_up", [GATE_RANK, 256])
                vecs = sb(phase, "vecs", [P, 2 + 4 + 1])
                pool_w = sb(phase, "pool_w", [P, 4, P])
                resets = sb(phase, "resets", [P, L])
                gla_mask = sb(phase, "gla_mask", [P, T], I32)
                y_hi = sb(phase, "y1_hi", [P, DC, T], F32R)
                y_lo = sb(phase, "y1_lo", [P, DC, T], F32R)
                load("meta", meta[:, :, :], dram["meta_t"])
                load("gate_up", gate_up[:, :], dram["w_gate_up"])
                load("vecs", vecs[:, :], dram["vecs"])
                load("resets", resets[:, :], dram["resets"])
                load("gla_mask", gla_mask[:, :], dram["gla_mask"])
                load("pool_w", pool_w[:, :, :], dram["pool_w"])

                sq = act.do(lambda e: e.activation(meta_sq[:, :, :], meta[:, :, :], ACT.Square), loads["meta"])
                sm = dve.do(lambda e: e.tensor_reduce(meta_sum[:, :], meta_sq[:, :, :].rearrange("p c t -> p t c"),
                                                      AX, ALU.add), sq)
                mm = pe.do(lambda e: e.matmul(bank_t[0][:, 0:META], ones[:, :], meta_sum[:, :],
                                              start=True, stop=True), sm, loads["ones"])
                lg = act.do(lambda e: e.activation(meta_rstd[:, :], bank_t[0][:, 0:META], ACT.Ln,
                                                   scale=1.0 / D, bias=eps_col[:, 0:1]), mm, eps_ready)
                free_t[0] = lg
                meta_rstd_w = act.do(lambda e: e.activation(meta_rstd[:, :], meta_rstd[:, :], ACT.Exp,
                                                            scale=-0.5), lg)
                mg = dve.do(lambda e: e.tensor_tensor(
                    meta_g[:, :, :], meta[:, :, :],
                    gains[:, 0:DC].rearrange("p (c o) -> p c o", o=1).to_broadcast([P, DC, META]), ALU.mult),
                    loads["meta"], loads["gains"])
                meta_ready = split_value(meta_hi[:, :, :], meta_lo[:, :, :], meta_g[:, :, :], mg)

                for c in range(DC):
                    add_square(c, loads[f"x{c}"])
                    split_x(c, 0, loads[f"x{c}"])
                token_rstd()

                def both(name, dst, dst_free=None):
                    b, t = next_l(), next_t()
                    kc, cols = panel_shape(stream["next"])
                    done = product(name, [lambda c: xg_hi[:, c, :], lambda c: meta_hi[:, c, :]],
                                   [lambda c: xg_lo[:, c, :], lambda c: meta_lo[:, c, :]],
                                   [bank_l[b][0:cols, :], bank_t[t][0:cols, 0:META]],
                                   [[r, meta_ready] for r in xg_ready], [free_l[b], free_t[t]])
                    state["xg_used"] = done
                    free_l[b] = dve.do(lambda e: e.tensor_tensor(dst[0:cols, META:], bank_l[b][0:cols, :],
                                                                 rstd[0:cols, :], ALU.mult),
                                       done, state["rstd"], dst_free)
                    free_t[t] = dve.do(lambda e: e.tensor_tensor(dst[0:cols, 0:META],
                                                                 bank_t[t][0:cols, 0:META],
                                                                 meta_rstd[0:cols, :], ALU.mult),
                                       done, meta_rstd_w, dst_free)
                    return [free_l[b], free_t[t]]

                with ExitStack() as gla:
                    g_low = sb(gla, "g_low", [GATE_RANK, L])
                    k_f = sb(gla, "k_f", [P, 2, L])
                    q_f = sb(gla, "q_f", [P, 2, T])
                    v_f = sb(gla, "v_f", [P, L])
                    v_tok = sb(gla, "v_tok", [P, TB, 512])
                    v_meta = sb(gla, "v_meta", [META, 512])
                    la = sb(gla, "la", [P, 2, L])
                    e1 = sb(gla, "e1", [P, L])
                    bsum = sb(gla, "bsum", [P, 2, L])
                    k_end = sb(gla, "k_end", [P, 2, L])
                    ke_tok = sb(gla, "ke_tok", [P, TB, 256])
                    ke_meta = sb(gla, "ke_meta", [META, 256])
                    decay = sb(gla, "decay", [P, 2, N_CHUNK])
                    carry = sb(gla, "carry", [P, 2, N_CHUNK, GLA_V])
                    scores = sb(gla, "scores", [P, 2, T])
                    pool_u = sb(gla, "pool_u", [P, L])
                    pool_s = sb(gla, "pool_s", [P, 2, L])

                    g_ready = both("g", g_low)
                    la_w = []
                    for hp in range(2):
                        t = next_t()
                        b = next_l()
                        w = gate_up[:, hp * P:(hp + 1) * P]
                        pe.run(lambda e, b=b, w=w: e.matmul(bank_l[b][:, :], w, g_low[:, META:], start=True, stop=True),
                               g_ready, free_l[b], loads["gate_up"])
                        m = pe.do(lambda e, t=t, w=w: e.matmul(bank_t[t][:, 0:META], w, g_low[:, 0:META],
                                                               start=True, stop=True), free_t[t])
                        bias = vecs[:, hp:hp + 1]
                        w1 = dve.do(lambda e, b=b, hp=hp, s=bias: e.tensor_scalar(
                            la[:, hp, META:], bank_l[b][:, :], s, None, ALU.add), m, loads["vecs"])
                        free_l[b] = w1
                        w2 = dve.do(lambda e, t=t, hp=hp, s=bias: e.tensor_scalar(
                            la[:, hp, 0:META], bank_t[t][:, 0:META], s, None, ALU.add), m)
                        free_t[t] = w2
                        a = act.do(lambda e, hp=hp: e.activation(e1[:, :], la[:, hp, :], ACT.Abs), w1, w2,
                                   la_w[-1] if la_w else None)
                        a = act.do(lambda e: e.activation(e1[:, :], e1[:, :], ACT.Exp, scale=-1.0), a)
                        a = act.do(lambda e: e.activation(e1[:, :], e1[:, :], ACT.Ln, bias=1.0), a)
                        la_w.append(dve.do(lambda e, hp=hp: e.scalar_tensor_tensor(
                            la[:, hp, :], la[:, hp, :], 0.0, e1[:, :], ALU.min, ALU.subtract), a))
                    sums = [dve.do(lambda e, hp=hp: e.tensor_tensor_scan(
                        bsum[:, hp, :], resets[:, :], la[:, hp, :], 0.0, ALU.mult, ALU.add),
                        la_w[hp], loads["resets"]) for hp in range(2)]

                    k_w = [both("k", k_f[:, hp, :]) for hp in range(2)]

                    ke_w, decay_w = [], []
                    for hp in range(2):
                        blocks = bsum[:, hp, META:].rearrange("p (n c) -> p n c", c=CHUNK)
                        a1 = dve.do(lambda e, hp=hp, v=blocks: e.tensor_tensor(
                            k_end[:, hp, META:].rearrange("p (n c) -> p n c", c=CHUNK),
                            v[:, :, CHUNK - 1:CHUNK].to_broadcast([P, N_CHUNK, CHUNK]), v, ALU.subtract), sums[hp])
                        a2 = dve.do(lambda e, hp=hp: e.tensor_scalar(
                            k_end[:, hp, 0:META], bsum[:, hp, 0:META], bsum[:, hp, META - 1:META], -1.0,
                            ALU.subtract, ALU.mult), sums[hp])
                        ex = act.do(lambda e, hp=hp: e.activation(k_end[:, hp, :], k_end[:, hp, :], ACT.Exp,
                                                                  scale=1.0 / 16), a1, a2)
                        decay_w.append(act.do(lambda e, hp=hp, v=blocks: e.activation(
                            decay[:, hp, :], v[:, :, CHUNK - 1], ACT.Exp, scale=1.0 / 16), sums[hp]))
                        ke_w.append(dve.do(lambda e, hp=hp: e.tensor_tensor(
                            k_end[:, hp, :], k_end[:, hp, :], k_f[:, hp, :], ALU.mult), ex, k_w[hp]))
                    exps = []
                    for hp in range(2):
                        p1 = act.do(lambda e, hp=hp: e.activation(la[:, hp, :], bsum[:, hp, :], ACT.Exp,
                                                                  scale=1.0 / 16), sums[hp])
                        p2 = act.do(lambda e, hp=hp: e.activation(bsum[:, hp, :], bsum[:, hp, :], ACT.Exp,
                                                                  scale=-1.0 / 16), p1, decay_w[hp], ke_w[hp])
                        exps.append((p1, p2))
                    kt_w = [dve.do(lambda e, hp=hp: e.tensor_tensor(k_f[:, hp, :], k_f[:, hp, :],
                                                                    bsum[:, hp, :], ALU.mult), exps[hp][1], ke_w[hp])
                            for hp in range(2)]

                    def to_tokens(src, dst, dst_meta, col, marks):
                        t = next_t()
                        for blk in range(TB):
                            m = pe.do(lambda e, blk=blk: e.transpose(
                                bank_t[t][:, blk * P:(blk + 1) * P],
                                src[:, META + blk * P:META + (blk + 1) * P], ident[:, :]),
                                marks, free_t[t], loads["ident"])
                        free_t[t] = act.do(lambda e: e.activation(
                            dst[:, :, col:col + P], bank_t[t][:, :].rearrange("p (b c) -> p b c", c=P), ACT.Copy), m)
                        r1 = free_t[t]
                        t2 = next_t()
                        m = pe.do(lambda e: e.transpose(bank_t[t2][0:META, 0:P], src[:, 0:META], ident[:, :]),
                                  free_t[t2])
                        free_t[t2] = act.do(lambda e: e.activation(dst_meta[:, col:col + P],
                                                                   bank_t[t2][0:META, 0:P], ACT.Copy), m)
                        return [r1, free_t[t2]], m

                    v_w, v_read = [], None
                    for i in range(4):
                        w = both("v", v_f[:, :], v_read)
                        r, v_read = to_tokens(v_f, v_tok, v_meta, i * P, w)
                        v_w += r
                    ke_ready = []
                    for hp in range(2):
                        r, _ = to_tokens(k_end[:, hp, :], ke_tok, ke_meta, hp * P, ke_w[hp])
                        ke_ready += r

                    carry_w = [[None] * N_CHUNK, [None] * N_CHUNK]
                    for n in range(-1, N_CHUNK - 1):
                        s = (n + 1) % 3
                        po = 64 * (n % 2)
                        for h in range(GLA_HEADS):
                            if n < 0:
                                lhs, rhs = ke_meta[:, h * 64:(h + 1) * 64], v_meta[:, h * P:(h + 1) * P]
                            else:
                                lhs = ke_tok[po:po + 64, n // 2, h * 64:(h + 1) * 64]
                                rhs = v_tok[po:po + 64, n // 2, h * P:(h + 1) * P]
                            d = bank_s[64 * (h % 2):64 * (h % 2) + 64, s, (h // 2) * P:(h // 2 + 1) * P]
                            m = pe.do(lambda e, d=d, a=lhs, b=rhs, h=h: e.matmul(
                                d, a, b, start=(h < 2), stop=True, skip_group_check=True),
                                ke_ready, v_w, free_s[s])
                        for hp in range(2):
                            src = bank_s[:, s, hp * P:(hp + 1) * P]
                            if n < 0:
                                carry_w[hp][0] = dve.do(lambda e, hp=hp, v=src: e.tensor_copy(
                                    carry[:, hp, 0, :], v), m)
                            else:
                                carry_w[hp][n + 1] = dve.do(lambda e, hp=hp, v=src, n=n: e.scalar_tensor_tensor(
                                    carry[:, hp, n + 1, :], carry[:, hp, n, :], decay[:, hp, n:n + 1], v,
                                    ALU.mult, ALU.add), m, carry_w[hp][n], decay_w[hp])
                            free_s[s] = carry_w[hp][n + 1]

                    qt_w = []
                    for hp in range(2):
                        b, done = x_product("q")
                        w = dve.do(lambda e, b=b, hp=hp: e.scalar_tensor_tensor(
                            q_f[:, hp, :], bank_l[b][:, :], GLA_K ** -0.5, rstd[:, :], ALU.mult, ALU.mult),
                            done, state["rstd"])
                        free_l[b] = w
                        qt_w.append(dve.do(lambda e, hp=hp: e.tensor_tensor(
                            q_f[:, hp, :], q_f[:, hp, :], la[:, hp, META:], ALU.mult), w, exps[hp][0]))
                    zeroed = pool.do(lambda e: e.memset(scores[:, :, :], 0.0))

                    y_w = [None] * DC
                    scores_read, scores_w = [None, None], [zeroed, zeroed]
                    u_read, s_read, p_read = None, None, None
                    post_read = None
                    for h in range(GLA_HEADS):
                        u_w = both("pool", pool_u[:, :], u_read)
                        width, src, cur = 1, pool_u[:, :], u_w
                        flip = 0
                        while width < POOL_WINDOWS[h]:
                            dst = pool_s[:, flip, :]
                            cur = pool.do(lambda e, d=dst, s=src, w=width: e.tensor_tensor(
                                d[:, 2 * w - 1:L], s[:, 2 * w - 1:L], s[:, w - 1:L - w], ALU.add),
                                cur, p_read, zeroed)
                            src, width, flip = dst, 2 * width, flip ^ 1
                        dst = pool_s[:, flip, META:L]
                        pooled = dve.do(lambda e, d=dst, s=src, h=h: e.scalar_tensor_tensor(
                            d, s[:, META:L], 1.0 / POOL_WINDOWS[h], pool_u[:, META:L], ALU.mult, ALU.subtract),
                            cur, u_w)
                        b = next_l()
                        m = pe.do(lambda e, b=b, d=dst, h=h: e.matmul(bank_l[b][:, :], pool_w[:, h, :], d,
                                                                      start=True, stop=True),
                                  pooled, free_l[b], loads["pool_w"])
                        u_read, p_read = pooled, m
                        sc = vecs[:, 2 + h:3 + h]
                        hi = act.do(lambda e, b=b, h=h, s=sc: e.activation(y_hi[:, h, :], bank_l[b][:, :],
                                                                           ACT.Copy, scale=s), m, loads["vecs"])
                        y_w[h] = free_l[b] = dve.do(lambda e, b=b, h=h, s=sc: e.scalar_tensor_tensor(
                            y_lo[:, h, :], bank_l[b][:, :], s, y_hi[:, h, :].bitcast(F32),
                            ALU.mult, ALU.subtract), hi)

                        hp, po, t, z = h // 2, 64 * (h % 2), next_t(), h % 2
                        for blk in range(TB):
                            lo_, hi_ = blk * P, (blk + 1) * P
                            m = pe.do(lambda e, a=lo_, b=hi_, hp=hp, po=po, t=t: e.matmul(
                                bank_t[t][:, a:b], k_f[po:po + 64, hp, META + a:META + b],
                                q_f[po:po + 64, hp, a:b], start=True, stop=True),
                                kt_w[hp], qt_w[hp], free_t[t])
                        scores_w[z] = free_t[t] = dve.do(lambda e, z=z, t=t: e.copy_predicated(
                            scores[:, z, :], gla_mask[:, :], bank_t[t][:, :]),
                            m, zeroed, scores_read[z], loads["gla_mask"])
                        for blk in range(TB):
                            pe.run(lambda e, blk=blk, h=h, z=z: e.matmul(
                                bank_o[:, blk * P:(blk + 1) * P], v_tok[:, blk, h * P:(h + 1) * P],
                                scores[:, z, blk * P:(blk + 1) * P], start=(blk == 0), stop=False,
                                skip_group_check=True), scores_w[z], free_o[0], v_w)
                        for n in range(N_CHUNK):
                            m = pe.do(lambda e, n=n, hp=hp, po=po: e.matmul(
                                bank_o[:, n * CHUNK:(n + 1) * CHUNK], carry[po:po + 64, hp, n, :],
                                q_f[po:po + 64, hp, n * CHUNK:(n + 1) * CHUNK], start=False,
                                stop=(n == N_CHUNK - 1), skip_group_check=True), carry_w[hp][n])
                        scores_read[z] = m
                        o_sb, sq_sb, rs_sb = squares[:, 0, :], squares[:, 1, :], square_sum[:, :]
                        a = act.do(lambda e, d=o_sb: e.activation(d, bank_o[:, :], ACT.Copy), m,
                                   post_read, square_read, sum_mark[0], state["sum_used"])
                        a2 = act.do(lambda e, d=sq_sb: e.activation(d, bank_o[:, :], ACT.Square), m)
                        free_o[0] = a2
                        t = next_t()
                        m = pe.do(lambda e, t=t, s=sq_sb: e.matmul(bank_t[t][:, :], ones[:, :], s,
                                                                   start=True, stop=True), a2, free_t[t])
                        a3 = act.do(lambda e, t=t, d=rs_sb: e.activation(d, bank_t[t][:, :], ACT.Ln,
                                                                         scale=1.0 / GLA_V, bias=eps_col[:, 0:1]), m)
                        free_t[t] = a3
                        a3 = act.do(lambda e, d=rs_sb: e.activation(d, d, ACT.Exp, scale=-0.5), a3)
                        v1 = dve.do(lambda e, d=o_sb, r=rs_sb: e.scalar_tensor_tensor(
                            d, d, vecs[:, 6:7], r, ALU.mult, ALU.mult), a3, a)
                        b, done = x_product("r")
                        v2 = free_l[b] = dve.do(lambda e, b=b, r=rs_sb: e.tensor_tensor(
                            r, bank_l[b][:, :], rstd[:, :], ALU.mult), done, v1, state["rstd"])
                        a4 = act.do(lambda e, r=rs_sb: e.activation(r, r, ACT.Silu), v2)
                        v3 = dve.do(lambda e, d=o_sb, r=rs_sb: e.tensor_tensor(d, d, r, ALU.mult), a4, v1)
                        y_w[4 + h] = split_value(y_hi[:, 4 + h, :], y_lo[:, 4 + h, :], o_sb, v3)
                        post_read = y_w[4 + h]
                    square_read[0] = square_read[1] = post_read
                    sum_mark[0] = v3
                for m in range(DC):
                    b = next_l()
                    done = product("out", lambda c: y_hi[:, c, :], lambda c: y_lo[:, c, :],
                                   bank_l[b][:, :], y_w, free_l[b])
                    add_to_x(m, b, done, 1.0, 1)
                token_rstd()

        comb_t = sb(stack, "comb_t", [N_EXPERTS, T])
        router_bias = sb(stack, "router_bias", [ROUTES, 1])
        load("router_bias", router_bias[:, :], dram["router_bias"])
        comb = {}

        def router():
            fence()
            with ExitStack() as phase:
                lt = sb(phase, "logits_t", [ROUTES, T])
                lg = sb(phase, "logits", [P, TB, ROUTES])
                rank = sb(phase, "rank", [P, TB, 4])
                hot = sb(phase, "hot", [P, TB, 4])
                tmp4 = sb(phase, "tmp4", [P, TB, 4])
                tmp16 = sb(phase, "tmp16", [P, TB, 4, 4])
                el = sb(phase, "el", [P, TB, 4])
                pick = sb(phase, "pick", [P, TB, 4])
                wsum = sb(phase, "wsum", [P, TB, 4])
                col = sb(phase, "col", [P, 8, TB, 1])
                combine = sb(phase, "combine", [P, TB, N_EXPERTS])
                load("rank", rank[:, :, :], dram["rank"])
                b, done = x_product("route")
                m = free_l[b] = dve.do(lambda e: e.tensor_tensor(lt[:, :], bank_l[b][0:ROUTES, :],
                                                                 rstd[0:ROUTES, :], ALU.mult), done, state["rstd"])
                m = dve.do(lambda e: e.tensor_scalar(lt[:, :], lt[:, :], router_bias[:, 0:1], None, ALU.add),
                           m, loads["router_bias"])
                t = next_t()
                for blk in range(TB):
                    p = pe.do(lambda e, blk=blk: e.transpose(bank_t[t][:, blk * 32:blk * 32 + ROUTES],
                                                             lt[:, blk * P:(blk + 1) * P],
                                                             ident[0:ROUTES, 0:ROUTES]), m, free_t[t])
                m = free_t[t] = dve.do(lambda e: e.tensor_copy(
                    lg[:, :, :], bank_t[t][:, 0:TB * 32].rearrange("p (b r) -> p b r", r=32)[:, :, 0:ROUTES]), p)

                def chain(make, *marks):
                    return dve.do(make, dve.last, *marks)

                def wide(v):
                    return v.to_broadcast([P, TB, 4])

                def first_of(values, peak, dst):
                    chain(lambda e: e.tensor_tensor(tmp4[:, :, :], values, wide(peak), ALU.is_equal))
                    chain(lambda e: e.tensor_tensor(tmp4[:, :, :], tmp4[:, :, :], rank[:, :, :], ALU.mult),
                          loads["rank"])
                    chain(lambda e: e.tensor_reduce(col[:, 7, :, :], tmp4[:, :, :], AX, ALU.max))
                    chain(lambda e: e.tensor_tensor(dst, tmp4[:, :, :], wide(col[:, 7, :, :]), ALU.is_equal))

                g_l = lg[:, :, 0:N_GROUPS]
                chain(lambda e: e.tensor_reduce(col[:, 0, :, :], g_l, AX, ALU.max))
                first_of(g_l, col[:, 0, :, :], hot[:, :, :])
                m = chain(lambda e: e.tensor_tensor(tmp4[:, :, :], g_l, wide(col[:, 0, :, :]), ALU.subtract))
                m = act.do(lambda e: e.activation(tmp4[:, :, :], tmp4[:, :, :], ACT.Exp), m)
                chain(lambda e: e.tensor_reduce(col[:, 1, :, :], tmp4[:, :, :], AX, ALU.add), m)
                e_l = lg[:, :, N_GROUPS:].rearrange("p b (g e) -> p b g e", e=4)
                for g in range(N_GROUPS):
                    chain(lambda e, g=g: e.tensor_tensor(
                        tmp16[:, :, g, :], e_l[:, :, g, :], wide(hot[:, :, g:g + 1]), ALU.mult))
                chain(lambda e: e.tensor_tensor(tmp4[:, :, :], tmp16[:, :, 0, :], tmp16[:, :, 1, :], ALU.add))
                chain(lambda e: e.tensor_tensor(el[:, :, :], tmp16[:, :, 2, :], tmp16[:, :, 3, :], ALU.add))
                chain(lambda e: e.tensor_tensor(el[:, :, :], el[:, :, :], tmp4[:, :, :], ALU.add))
                chain(lambda e: e.tensor_reduce(col[:, 2, :, :], el[:, :, :], AX, ALU.max))
                first_of(el[:, :, :], col[:, 2, :, :], wsum[:, :, :])
                m = chain(lambda e: e.tensor_tensor(pick[:, :, :], el[:, :, :], wide(col[:, 2, :, :]), ALU.subtract))
                m = act.do(lambda e: e.activation(pick[:, :, :], pick[:, :, :], ACT.Exp), m)
                chain(lambda e: e.scalar_tensor_tensor(el[:, :, :], wsum[:, :, :], -3e38, el[:, :, :],
                                                       ALU.mult, ALU.add))
                chain(lambda e: e.tensor_reduce(col[:, 3, :, :], el[:, :, :], AX, ALU.max))
                first_of(el[:, :, :], col[:, 3, :, :], el[:, :, :])
                chain(lambda e: e.tensor_tensor(wsum[:, :, :], wsum[:, :, :], el[:, :, :], ALU.add))
                chain(lambda e: e.tensor_tensor(wsum[:, :, :], wsum[:, :, :], pick[:, :, :], ALU.mult), m)
                chain(lambda e: e.tensor_reduce(col[:, 4, :, :], wsum[:, :, :], AX, ALU.add))
                chain(lambda e: e.tensor_tensor(col[:, 5, :, :], col[:, 4, :, :], col[:, 1, :, :], ALU.mult))
                chain(lambda e: e.reciprocal(col[:, 6, :, :], col[:, 5, :, :]))
                chain(lambda e: e.tensor_tensor(wsum[:, :, :], wsum[:, :, :], wide(col[:, 6, :, :]), ALU.mult))
                for g in range(N_GROUPS):
                    m = chain(lambda e, g=g: e.tensor_tensor(
                        combine[:, :, 4 * g:4 * g + 4], wsum[:, :, :], wide(hot[:, :, g:g + 1]), ALU.mult))
                t2 = next_t()
                for blk in range(TB):
                    p = pe.do(lambda e, blk=blk: e.transpose(
                        bank_t[t2][0:N_EXPERTS, blk * P:(blk + 1) * P], combine[:, blk, :], ident[:, :]),
                        m, free_t[t2])
                comb["ready"] = free_t[t2] = dve.do(lambda e: e.tensor_copy(comb_t[:, :],
                                                                           bank_t[t2][0:N_EXPERTS, :]), p)

        def expert_scales(phase):
            picks = sb(phase, "picks", [N_EXPERTS, N_EXPERTS, P])
            scale = sb(phase, "expert_scale", [P, 2, T])
            load("picks", picks[:, :, :], dram["picks"])
            marks = {}

            def of_chunk(j):
                ex = j // 2
                if ex not in marks:
                    m = pe.do(lambda e: e.matmul(bank_o[:, :], picks[:, ex, :], comb_t[:, :],
                                                 start=True, stop=True),
                              comb["ready"], free_o[0], loads["picks"])
                    marks[ex] = free_o[0] = dve.do(lambda e: e.tensor_tensor(
                        scale[:, ex % 2, :], bank_o[:, :], rstd[:, :], ALU.mult), m, dve.last)
                return scale[:, ex % 2, :], marks[ex]
            return of_chunk

        def normalise(g, g_next=None, store=False):
            for c in range(DC):
                w = x_written[c] = dve.do(lambda e, c=c: e.scalar_tensor_tensor(
                    x[:, c, :], x[:, c, :], gain(g, c), rstd[:, :], ALU.mult, ALU.mult),
                    state["rstd"], x_read[c], x_written[c])
                x_read[c] = None
                if store:
                    sync.wait(w)
                    sync.ops.append(lambda e, c=c: e.dma_start(out[:, c, :], x[:, c, :]).then_inc(stored, 16))
                else:
                    add_square(c, w)
                    split_x(c, g_next, w)
            if not store:
                token_rstd()

        stored = sem("stored")

        rotate = sb(stack, "rotate", [P, P])
        suffix = sb(stack, "suffix", [P, P])
        minus = sb(stack, "minus", [P, P])
        strict = sb(stack, "strict", [P, P])
        masks_f = sb(stack, "masks_bf", [P, 2 * P + 4 * P + 4 * P + P], BF16)
        load("rotate", rotate[:, :], dram["rotate"])
        load("suffix", suffix[:, :], dram["suffix"])
        load("minus", minus[:, :], dram["minus"])
        load("strict", strict[:, :], dram["strict"])
        load("masks", masks_f[:, :], dram["masks"])
        MASK_END = (2 * P, 6 * P, 10 * P)

        def mixer_2(l):
            g_out = 3 + 3 * l + 2
            name = f"in_{l}"
            fence()
            with ExitStack() as phase:
                o_f = sb(phase, f"o_f_{l}", [P, 4, T])
                gates = sb(phase, f"gates_{l}", [P, 16, T])
                att = ExitStack()
                qk = sb(att, f"qk_{l}", [P, 16, T])
                v_tok = sb(att, f"vt_{l}", [P, TB, D])
                rope = ExitStack()
                cos = sb(rope, f"cos_{l}", [P, T])
                sin = sb(rope, f"sin_{l}", [P, T])
                rot = sb(rope, f"rot_{l}", [P, 2, T])
                sync.wait(*[e.last for e in (pe, act, dve, pool)])
                load(f"cos_{l}", cos[:, :], dram["cos"])
                load(f"sin_{l}", sin[:, :], dram["sin"])
                rot_read = [None, None]
                qk_w = [None] * 16
                for i in range(12):
                    b, done = x_product(name)
                    scale = HEAD ** -0.5 if i < 6 else 1.0
                    w = free_l[b] = dve.do(lambda e, b=b, i=i, s=scale: e.scalar_tensor_tensor(
                        qk[:, i, :], bank_l[b][:, :], s, rstd[:, :], ALU.mult, ALU.mult), done, state["rstd"])
                    t, r = next_t(), i % 2
                    m = pe.do(lambda e, t=t, i=i: e.matmul(bank_t[t][:, :], rotate[:, :], qk[:, i, :],
                                                           start=True, stop=True), w, free_t[t], loads["rotate"])
                    free_t[t] = dve.do(lambda e, t=t, r=r: e.tensor_tensor(
                        rot[:, r, :], bank_t[t][:, :], sin[:, :], ALU.mult), m, rot_read[r], loads[f"sin_{l}"])
                    a = pool.do(lambda e, i=i: e.tensor_tensor(qk[:, i, :], qk[:, i, :], cos[:, :], ALU.mult),
                                w, m, loads[f"cos_{l}"])
                    qk_w[i] = rot_read[r] = pool.do(lambda e, i=i, r=r: e.tensor_tensor(
                        qk[:, i, :], qk[:, i, :], rot[:, r, :], ALU.add), a, free_t[t])
                v_w = []
                vt_read = [None, None]

                def value_panel(i):
                    b, done = x_product(name)
                    r = i % 2
                    w = free_l[b] = dve.do(lambda e: e.tensor_tensor(rot[:, r, :], bank_l[b][:, :],
                                                                     rstd[:, :], ALU.mult),
                                           done, state["rstd"], vt_read[r], rot_read[r])
                    t = next_t()
                    for blk in range(TB):
                        m = pe.do(lambda e, blk=blk: e.transpose(
                            bank_t[t][:, blk * P:(blk + 1) * P], rot[:, r, blk * P:(blk + 1) * P], ident[:, :]),
                            w, free_t[t])
                    vt_read[r] = m
                    free_t[t] = act.do(lambda e: e.activation(
                        v_tok[:, :, i * P:(i + 1) * P], bank_t[t][:, :].rearrange("p (b c) -> p b c", c=P),
                        ACT.Copy), m)
                    v_w.append(free_t[t])

                for i in range(6):
                    value_panel(i)
                for i in range(12, 16):
                    b, done = x_product(name)
                    scale = HEAD ** -0.5 if i < 14 else 1.0
                    qk_w[i] = free_l[b] = dve.do(lambda e, b=b, i=i, s=scale: e.scalar_tensor_tensor(
                        qk[:, i, :], bank_l[b][:, :], s, rstd[:, :], ALU.mult, ALU.mult), done)
                for i in range(6, 8):
                    value_panel(i)
                fence()
                rope.close()

                work = ExitStack()
                prob = sb(work, f"prob_{l}", [P, 2, 1280])
                prob_t = sb(work, f"prob_t_{l}", [P, 2, T])
                diag = sb(work, f"diag_{l}", [P, 2, P])
                stat = sb(work, f"stat_{l}", [P, 2, 8])
                prob_read, pt_read = [None, None], [None, None]
                diag_read = [None, None]
                pt = {"n": 0}
                o_w = []
                gate_n = {"i": 0}

                def gate_panel():
                    i = gate_n["i"]
                    if i == 16:
                        return
                    gate_n["i"] += 1
                    b, done = x_product(name)
                    free_l[b] = gate_w[i] = dve.do(lambda e: e.tensor_tensor(
                        gates[:, i, :], bank_l[b][:, :], rstd[:, :], ALU.mult), done)

                gate_w = [None] * 16

                def dilated_scores(u, s, blk):
                    z, po = u % 2, 64 * (s % 2)
                    first = max(blk - 1, 0)
                    k0 = (first, 0, 0)
                    width = [(blk + 1 - k) * P for k in k0]
                    for g in range(3):
                        ch = (g * SLOTS + s) // 2
                        pe.run(lambda e, g=g: e.matmul(
                            bank_s[:, g, 0:width[g]], ident_bf[:, :], masks_f[:, MASK_END[g] - width[g]:MASK_END[g]],
                            start=True, stop=False), free_s[g], ident_bf_ready, loads["masks"])
                        m = pe.do(lambda e, g=g, ch=ch: e.matmul(
                            bank_s[:, g, 0:width[g]], qk[po:po + 64, ch, blk * P:(blk + 1) * P],
                            qk[po:po + 64, 6 + ch, k0[g] * P:(blk + 1) * P], start=False, stop=True),
                            qk_w[ch], qk_w[6 + ch])
                    w0, w1 = width[0], width[1]
                    st = stat[:, z, :]
                    r1 = dve.do(lambda e: e.tensor_reduce(st[:, 0:1], bank_s[:, 0, 0:w0], AX, ALU.max),
                                m, diag_read[z])
                    r2 = dve.do(lambda e: e.tensor_reduce(st[:, 1:3], bank_s[:, 1:3, 0:w1], AX, ALU.max), m)
                    r = dve.do(lambda e: e.tensor_reduce(st[:, 3:4], st[:, 0:3], AX, ALU.max), r1, r2)
                    r = dve.do(lambda e: e.tensor_scalar(st[:, 4:5], st[:, 3:4], -1.0, None, ALU.mult), r)
                    a1 = act.do(lambda e: e.activation(prob[:, z, 0:w0], bank_s[:, 0, 0:w0], ACT.Exp,
                                                       bias=st[:, 4:5], accum_out=st[:, 5:6]), r, prob_read[z])
                    a2 = act.do(lambda e: e.activation(
                        prob[:, z, 256:256 + 2 * w1].rearrange("p (g k) -> p g k", g=2), bank_s[:, 1:3, 0:w1],
                        ACT.Exp, bias=st[:, 4:5], accum_out=st[:, 6:7]), r)
                    free_s[0] = [a1]
                    free_s[1] = free_s[2] = [a2]
                    r = dve.do(lambda e: e.tensor_tensor(st[:, 7:8], st[:, 5:6], st[:, 6:7], ALU.add), a1, a2)
                    r = dve.do(lambda e: e.reciprocal(st[:, 7:8], st[:, 7:8]), r)
                    return dve.do(lambda e: e.tensor_scalar(diag[:, z, :], ident[:, :], st[:, 7:8], None,
                                                            ALU.mult), r)

                def dilated_values(u, s, blk, diag_w):
                    z, po = u % 2, 64 * (s % 2)
                    first = max(blk - 1, 0)
                    batches = [(1, 0, 256), (2, 0, 256 + (blk + 1) * P), (0, first, 0)]
                    total = sum(blk + 1 - k0 for _, k0, _ in batches)
                    n = 0
                    for g, k0, at in batches:
                        t, nb, y = next_t(), blk + 1 - k0, pt["n"] % 2
                        pt["n"] += 1
                        for j in range(nb):
                            m = pe.do(lambda e, t=t, j=j, a=at: e.matmul(
                                bank_t[t][:, j * P:(j + 1) * P], prob[:, z, a + j * P:a + (j + 1) * P],
                                diag[:, z, :], start=True, stop=True), diag_w, free_t[t])
                        copy_on = act if g == 1 else dve
                        if g == 1:
                            w = act.do(lambda e, t=t, y=y, nb=nb: e.activation(
                                prob_t[:, y, 0:nb * P], bank_t[t][:, 0:nb * P], ACT.Copy), m, pt_read[y])
                        else:
                            w = dve.do(lambda e, t=t, y=y, nb=nb: e.tensor_copy(
                                prob_t[:, y, 0:nb * P], bank_t[t][:, 0:nb * P]), m, pt_read[y])
                        free_t[t] = w
                        head = (g * SLOTS + s) * HEAD
                        for j in range(nb):
                            n += 1
                            m2 = pe.do(lambda e, j=j, y=y, k0=k0, h=head, n=n: e.matmul(
                                bank_o[po:po + 64, 0:P], v_tok[:, k0 + j, h:h + HEAD],
                                prob_t[:, y, j * P:(j + 1) * P], start=(n == 1), stop=(n == total)),
                                w, v_w, free_o[0])
                        pt_read[y] = m2
                    prob_read[z] = diag_read[z] = m
                    free_o[0] = dve.do(lambda e: e.tensor_copy(o_f[po:po + 64, s // 2, blk * P:(blk + 1) * P],
                                                               bank_o[po:po + 64, 0:P]), m2)
                    o_w.append(free_o[0])

                units = [(s, blk) for blk in range(TB) for s in range(SLOTS)]
                marks = {}
                for u in range(len(units) + 1):
                    if u < len(units):
                        marks[u] = dilated_scores(u, *units[u])
                        if u < 12:
                            gate_panel()
                    if u:
                        dilated_values(u - 1, *units[u - 1], marks[u - 1])

                place = [(0, 0), (1, 0), (2, 0), (1, 384)]
                flat = [0, 512, 1024, 896]

                def stick_scores(h):
                    z, po, ch = h % 2, 64 * (h % 2), h // 2
                    for kb in range(TB):
                        bk, c0 = place[kb]
                        w = T - kb * P
                        m = pe.do(lambda e, bk=bk, c0=c0, w=w, kb=kb: e.matmul(
                            bank_s[:, bk, c0:c0 + w], qk[po:po + 64, 14 + ch, kb * P:(kb + 1) * P],
                            qk[po:po + 64, 12 + ch, kb * P:T], start=(c0 == 0), stop=False,
                            skip_group_check=True), qk_w[12 + ch], qk_w[14 + ch], free_s[bk])
                    sizes = (512, 512, 256)
                    for bk, n in enumerate(sizes):
                        a = act.do(lambda e, bk=bk, n=n: e.activation(
                            prob[:, z, bk * 512:bk * 512 + n], bank_s[:, bk, 0:n], ACT.Abs), m, prob_read[z])
                    a = act.do(lambda e: e.activation(prob[:, z, :], prob[:, z, :], ACT.Exp, scale=-1.0), a)
                    a = act.do(lambda e: e.activation(prob[:, z, :], prob[:, z, :], ACT.Ln, bias=1.0), a)
                    done = []
                    for bk, n in enumerate(sizes):
                        done.append(dve.do(lambda e, bk=bk, n=n: e.scalar_tensor_tensor(
                            prob[:, z, bk * 512:bk * 512 + n], bank_s[:, bk, 0:n], 0.0,
                            prob[:, z, bk * 512:bk * 512 + n], ALU.max, ALU.add), a))
                    for kb in range(TB):
                        done.append(dve.do(lambda e, f=flat[kb]: e.tensor_tensor(
                            prob[:, z, f:f + P], prob[:, z, f:f + P], strict[:, :], ALU.mult),
                            done[0:3], loads["strict"]))
                    return done

                def stick_weights(h, nlk):
                    z = h % 2
                    for kb in range(TB):
                        bk, c0 = place[kb]
                        w = T - kb * P
                        pe.run(lambda e, bk=bk, c0=c0: e.matmul(
                            bank_s[:, bk, c0:c0 + P], ident_bf[:, :], masks_f[:, 10 * P:11 * P],
                            start=False, stop=False, skip_group_check=True), nlk)
                        pe.run(lambda e, bk=bk, c0=c0, w=w, f=flat[kb]: e.matmul(
                            bank_s[:, bk, c0:c0 + w], suffix[:, :], prob[:, z, f:f + w],
                            start=False, stop=False, skip_group_check=True), loads["suffix"], loads["minus"])
                        for k2 in range(kb + 1, TB):
                            w2, f2 = T - k2 * P, flat[k2]
                            c2 = c0 + (k2 - kb) * P
                            pe.run(lambda e, bk=bk, c=c2, w=w2, f=f2: e.matmul(
                                bank_s[:, bk, c:c + w], minus[:, :], prob[:, z, f:f + w],
                                start=False, stop=False, skip_group_check=True))
                    m = pe.do(lambda e: e.matmul(bank_s[:, 2, 0:1], ident_bf[:, :], masks_f[:, 0:1], start=False,
                                                 stop=True, skip_group_check=True))
                    for bk, n in enumerate((512, 512, 256)):
                        a = act.do(lambda e, bk=bk, n=n: e.activation(
                            prob[:, z, bk * 512:bk * 512 + n], bank_s[:, bk, 0:n], ACT.Exp), m)
                        free_s[bk] = a
                    return a

                def stick_values(h, weights):
                    z, po = h % 2, 64 * (h % 2)
                    for kb in range(TB):
                        f, w = flat[kb], T - kb * P
                        m = pe.do(lambda e, kb=kb, f=f, w=w: e.matmul(
                            bank_o[po:po + 64, kb * P:T], v_tok[:, kb, 768 + h * HEAD:768 + (h + 1) * HEAD],
                            prob[:, z, f:f + w], start=(kb == 0), stop=(kb == TB - 1),
                            skip_group_check=True), weights, free_o[0], v_w)
                    prob_read[z] = m
                    free_o[0] = dve.do(lambda e: e.tensor_copy(o_f[po:po + 64, 2 + h // 2, :],
                                                               bank_o[po:po + 64, :]), m)
                    o_w.append(free_o[0])

                prev = None
                for h in range(4):
                    nlk = stick_scores(h)
                    gate_panel()
                    if prev:
                        stick_values(*prev)
                    prev = (h, stick_weights(h, nlk))
                stick_values(*prev)
                fence()
                work.close()
                att.close()

                o_hi = sb(phase, f"o_hi_{l}", [P, 4, T], F32R)
                o_lo = sb(phase, f"o_lo_{l}", [P, 4, T], F32R)
                y_hi = sb(phase, f"y_hi_{l}", [P, DC, T], F32R)
                y_lo = sb(phase, f"y_lo_{l}", [P, DC, T], F32R)
                part = sb(phase, f"part_{l}", [P, 2, 2, T])
                o_ready = [split_value(o_hi[:, c, :], o_lo[:, c, :], o_f[:, c, :], o_w) for c in range(4)]
                part_read = [None, None]
                y_w = [None] * DC
                for m in range(DC):
                    for f in range(2):
                        sg = act.do(lambda e, i=8 * f + m: e.activation(gates[:, i, :], gates[:, i, :], ACT.Sigmoid),
                                    gate_w[8 * f + m])
                        b = next_l()
                        done = product(f"proj_{('dil', 'sb')[f]}_{l}", lambda c, f=f: o_hi[:, 2 * f + c, :],
                                       lambda c, f=f: o_lo[:, 2 * f + c, :], bank_l[b][:, :],
                                       o_ready[2 * f:2 * f + 2], free_l[b])
                        z = m % 2
                        free_l[b] = dve.do(lambda e, b=b, z=z, f=f, i=8 * f + m: e.tensor_tensor(
                            part[:, z, f, :], bank_l[b][:, :], gates[:, i, :], ALU.mult),
                            done, sg, part_read[z])
                    w = pool.do(lambda e, z=z: e.tensor_tensor(part[:, z, 0, :], part[:, z, 0, :],
                                                               part[:, z, 1, :], ALU.add), dve.last)
                    y_w[m] = part_read[z] = split_value(y_hi[:, m, :], y_lo[:, m, :], part[:, z, 0, :], w)
                for m in range(DC):
                    b = next_l()
                    done = product(f"out_{l}", lambda c: y_hi[:, c, :], lambda c: y_lo[:, c, :],
                                   bank_l[b][:, :], y_w, free_l[b])
                    add_to_x(m, b, done, 1.0, g_out)
                token_rstd()

        mixer_1()
        router()
        feed_forward("moe", "moe_gate", "moe_up", "moe_down", (8,) * 4, 1.0, None, expert_scales)
        normalise(2, 3)
        for l in range(DEPTH_2):
            feed_forward(f"ff1_{l}", f"ff1_gate_{l}", f"ff1_up_{l}", f"ff1_down_{l}", FF_GROUPS, 0.5, 4 + 3 * l)
            mixer_2(l)
            last = l == DEPTH_2 - 1
            feed_forward(f"ff2_{l}", f"ff2_gate_{l}", f"ff2_up_{l}", f"ff2_down_{l}", FF_GROUPS, 0.5,
                         None if last else 3 + 3 * (l + 1))
        normalise(3 + 3 * DEPTH_2, store=True)
        sync.wait((stored, 16 * DC))

        block = stack.enter_context(nc.Block())

        def body(engine):
            def emit(e):
                for op in engine.ops:
                    op(e)
            return emit
        block.sync(body(sync))
        block.scalar(body(act))
        block.gpsimd(body(pool))
        block.vector(body(dve))
        block.tensor(body(pe))


def constants():
    i = np.arange(P)
    causal = i[:, None] >= i[None, :]
    masks = []
    for w, d in zip(WINDOWS, DILATIONS):
        near = (i[:, None] - i[None, :]) % d == 0
        diag = near & causal
        far = near & (i[:, None] + P - i[None, :] <= w) if w == P else near
        masks += [far] * (1 if w == P else 3) + [diag]
    masks.append(~(i[:, None] < i[None, :]) == False)
    masks = np.where(np.concatenate(masks, 1), 0.0, MASKED)
    pos = np.arange(T, dtype=np.float32)
    inv = np.float32(ROPE_THETA) ** (-np.arange(0, ROPE_DIM, 2, dtype=np.float32) / np.float32(ROPE_DIM))
    ang = (pos[:, None] * inv[None, :]).astype(np.float32)
    half = ROPE_DIM // 2
    cos, sin = np.ones((P, T), np.float32), np.zeros((P, T), np.float32)
    rotate = np.zeros((P, P), np.float32)
    for h in range(0, P, HEAD):
        cos[h:h + half] = cos[h + half:h + ROPE_DIM] = np.cos(ang).T
        sin[h:h + half], sin[h + half:h + ROPE_DIM] = -np.sin(ang).T, np.sin(ang).T
        for a in range(half):
            rotate[h + a, h + half + a] = rotate[h + half + a, h + a] = 1.0
    resets = np.ones((P, META + T), np.float32)
    resets[:, META::CHUNK] = 0.0
    same = (i[:, None] // CHUNK) == (i[None, :] // CHUNK)
    gla_mask = np.tile((same & (i[:, None] <= i[None, :])).astype(np.int32), (1, TB))
    picks = np.zeros((N_EXPERTS, N_EXPERTS, P), np.float32)
    picks[np.arange(N_EXPERTS), np.arange(N_EXPERTS)] = 1.0
    return {
        "ident": np.eye(P, dtype=np.float32), "ones": np.ones((P, P), np.float32),
        "rotate": rotate, "cos": cos, "sin": sin,
        "suffix": np.where(i[:, None] >= i[None, :], -1.0, 0.0).astype(np.float32),
        "minus": np.full((P, P), -1.0, np.float32),
        "strict": (i[:, None] < i[None, :]).astype(np.float32),
        "masks": masks, "resets": resets, "gla_mask": gla_mask, "picks": picks,
        "rank": np.broadcast_to(np.arange(4, 0, -1, dtype=np.float32), (P, TB, 4)).copy(),
    }


def kernel(**a):
    import ml_dtypes
    import concourse.bacc as bacc
    from concourse.bass_utils import run_bass_kernel_spmd

    a = {k: np.asarray(v) for k, v in a.items()}

    def chunks(v):
        return v.reshape(-1, P).T

    def feature_major(v):
        return np.ascontiguousarray(v.T.reshape(DC, P, -1).transpose(1, 0, 2))

    w_in = a["w_in"][0]
    source = {
        "pool": w_in[:, 0:512], "q": w_in[:, 512:768], "k": w_in[:, 768:1024], "v": w_in[:, 1024:1536],
        "r": w_in[:, 1536:2048], "g": w_in[:, 2048:2064], "out": a["w_out"][0],
        "route": np.concatenate([a["w_router_group"][0], a["w_router_expert"][0]], 1),
        "moe_gate": a["w_expert_gate"][0].transpose(1, 0, 2).reshape(D, 4096),
        "moe_up": a["w_expert_up"][0].transpose(1, 0, 2).reshape(D, 4096),
        "moe_down": a["w_expert_down"][0].reshape(4096, D),
    }
    for l in range(DEPTH_2):
        for f in (1, 2):
            for part in ("gate", "up", "down"):
                source[f"ff{f}_{part}_{l}"] = a[f"ffn{f}_w_{part}_2"][l]
        source[f"in_{l}"] = a["w_in_2"][l]
        source[f"proj_dil_{l}"] = a["w_proj_dil_2"][l]
        source[f"proj_sb_{l}"] = a["w_proj_sb_2"][l]
        source[f"out_{l}"] = a["w_out_2"][l]
    arrays = {}
    for name, panels in weight_matrices().items():
        w = source[name]
        arrays[name] = np.concatenate([
            w[r:r + rows, c:c + cols].reshape(rows // P, P, cols).transpose(1, 0, 2).ravel()
            for r, rows, c, cols in panels])
    gains = [a["norm_mix_w"][0], a["norm_ffn_w"][0], a["final_norm_w"]]
    for l in range(DEPTH_2):
        gains += [a["norm_ffn1_2"][l], a["norm_mix_2"][l], a["norm_ffn2_2"][l]]
    gains.append(a["norm_final_2"])
    arrays.update(constants())
    arrays["masks"] = arrays["masks"].astype(ml_dtypes.bfloat16)
    arrays.update({
        "x_t": feature_major(a["x"][0]), "meta_t": feature_major(a["meta_tokens"]),
        "gains": np.ascontiguousarray(np.concatenate([chunks(g) for g in gains], 1)),
        "w_gate_up": a["w_gate_up"][0],
        "vecs": np.ascontiguousarray(np.concatenate(
            [chunks(a["b_gate"][0]), chunks(a["pool_scale"][0]), chunks(a["gla_norm_w"][0])], 1)),
        "pool_w": np.ascontiguousarray(a["pool_w"][0].transpose(1, 0, 2)),
        "router_bias": np.concatenate([a["b_router_group"][0], a["b_router_expert"][0]])[:, None].copy(),
    })

    nc = bacc.Bacc("TRN2", target_bir_lowering=False, num_devices=1)
    dram = {n: nc.dram_tensor(f"in_{n}", v.shape, mybir.dt.from_np(v.dtype), kind="ExternalInput").ap()
            for n, v in arrays.items()}
    out = nc.dram_tensor("out_t", (P, DC, T), F32, kind="ExternalOutput").ap()
    build(nc, dram, out)
    r = run_bass_kernel_spmd(nc, [{f"in_{n}": v for n, v in arrays.items()}], core_ids=[0])
    got = r.results[0]["out_t"]
    return got.transpose(2, 1, 0).reshape(1, T, D)
```

```python
from contextlib import ExitStack

import numpy as np

import concourse.bass as bass
from concourse import mybir

F32 = mybir.dt.float32
F32R = mybir.dt.float32r
BF16 = mybir.dt.bfloat16
I32 = mybir.dt.int32
ALU = mybir.AluOpType
ACT = mybir.ActivationFunctionType
AX = mybir.AxisListType.X

P = 128
T = 512
D = 1024
DC = D // P
TB = T // P
META = 16
L = META + T
POOL_WINDOWS = (2, 4, 8, 16)
GATE_RANK = 16
GLA_HEADS, GLA_K, GLA_V, CHUNK = 4, 64, 128, 64
N_CHUNK = T // CHUNK
N_GROUPS, PER_GROUP = 4, 4
N_EXPERTS = N_GROUPS * PER_GROUP
ROUTES = N_GROUPS + N_EXPERTS
EPS = 1e-6
DEPTH_2 = 2
HEAD = 64
SLOTS = 4
DILATIONS = (1, 4, 16)
WINDOWS = (128, 512, 2048)
ROPE_DIM = HEAD // 4
ROPE_THETA = 500000.0
D_FF = 2816
FF_GROUPS = (8, 8, 6)
MASKED = -1e30

RAW = 3
SPLIT = 3
AHEAD = 2
PANEL = DC * P


def matrix_panels(rows, cols, k_groups=None, width=P):
    out, r = [], 0
    for kc in k_groups or (rows // P,):
        for c in range(0, cols, width):
            out.append((r, kc * P, c, min(width, cols - c)))
        r += kc * P
    return out


def weight_matrices():
    m = {
        "pool": matrix_panels(D, 512), "q": matrix_panels(D, 256), "k": matrix_panels(D, 256),
        "v": matrix_panels(D, 512), "r": matrix_panels(D, 512), "g": matrix_panels(D, P),
        "out": matrix_panels(D, D), "route": matrix_panels(D, P),
        "moe_gate": matrix_panels(D, 4096), "moe_up": matrix_panels(D, 4096),
        "moe_down": matrix_panels(4096, D, (8,) * 4),
    }
    for l in range(DEPTH_2):
        for f in (1, 2):
            m[f"ff{f}_gate_{l}"] = matrix_panels(D, D_FF)
            m[f"ff{f}_up_{l}"] = matrix_panels(D, D_FF)
            m[f"ff{f}_down_{l}"] = matrix_panels(D_FF, D, FF_GROUPS)
        m[f"in_{l}"] = matrix_panels(D, 5120)
        m[f"proj_dil_{l}"] = matrix_panels(256, D)
        m[f"proj_sb_{l}"] = matrix_panels(256, D)
        m[f"out_{l}"] = matrix_panels(D, D)
    return m


def ffn_order(gate, up, down, groups):
    out, j = [], 0
    for g, n in enumerate(groups):
        for i in range(n):
            out += [(gate, j), (up, j)]
            j += 1
        out += [(down, g * DC + m) for m in range(DC)]
    return out


def weight_order():
    o = [("g", 0)] + [("k", i) for i in range(2)] + [("v", i) for i in range(4)]
    o += [("q", i) for i in range(2)]
    for i in range(4):
        o += [("pool", i), ("r", i)]
    o += [("out", i) for i in range(DC)]
    o += [("route", 0)]
    o += ffn_order("moe_gate", "moe_up", "moe_down", (8,) * 4)
    for l in range(DEPTH_2):
        o += ffn_order(f"ff1_gate_{l}", f"ff1_up_{l}", f"ff1_down_{l}", FF_GROUPS)
        o += [(f"in_{l}", i) for i in range(40)]
        for m in range(DC):
            o += [(f"proj_dil_{l}", m), (f"proj_sb_{l}", m)]
        o += [(f"out_{l}", m) for m in range(DC)]
        o += ffn_order(f"ff2_gate_{l}", f"ff2_up_{l}", f"ff2_down_{l}", FF_GROUPS)
    return o


class Engine:

    def __init__(self, sem):
        self.sem, self.count, self.ops, self.reached = sem, 0, [], {}
        self.last = None

    def wait(self, *marks):
        for m in marks:
            if m is None:
                continue
            if isinstance(m, list):
                self.wait(*m)
                continue
            sem, value = m
            if self.reached.get(id(sem), 0) < value:
                self.reached[id(sem)] = value
                self.ops.append(lambda e, s=sem, v=value: e.wait_ge(s, v))

    def run(self, make, *marks):
        self.wait(*marks)
        self.ops.append(make)

    def do(self, make, *marks):
        self.wait(*marks)
        self.count += 1
        self.ops.append(lambda e: make(e).then_inc(self.sem, 1))
        self.last = (self.sem, self.count)
        return self.last


def build(nc, dram, out):
    matrices, order = weight_matrices(), weight_order()
    stack = ExitStack()
    with stack:
        def sb(where, name, shape, dt=F32):
            return where.enter_context(nc.sbuf_tensor(name, shape, dt))

        def sem(name):
            return stack.enter_context(nc.semaphore(name))

        pe, act, dve, pool = (Engine(sem(f"{n}_done")) for n in ("pe", "act", "dve", "pool"))
        sync = Engine(sem("sync_unused"))

        bank_l = [stack.enter_context(nc.psum_tensor(f"bank_l{i}", [P, 512], F32)) for i in range(2)]
        bank_s = stack.enter_context(nc.psum_tensor("bank_s", [P, 3, 512], F32))
        bank_t = [stack.enter_context(nc.psum_tensor(f"bank_t{i}", [P, 512], F32)) for i in range(2)]
        bank_o = stack.enter_context(nc.psum_tensor("bank_o", [P, 512], F32))
        free_l, free_s, free_t, free_o = [[], []], [[], [], []], [[], []], [[]]

        x = sb(stack, "x", [P, DC, T])
        xg_hi = sb(stack, "xg_hi", [P, DC, L], F32R)
        xg_lo = sb(stack, "xg_lo", [P, DC, L], F32R)
        rstd = sb(stack, "rstd", [P, T])
        squares = sb(stack, "squares", [P, 2, T])
        square_sum = sb(stack, "square_sum", [P, T])
        w_raw = sb(stack, "w_raw", [P, RAW, PANEL])
        w_hi = sb(stack, "w_hi", [P, SPLIT, PANEL], F32R)
        w_lo = sb(stack, "w_lo", [P, SPLIT, PANEL], F32R)
        n_gain = 3 + 3 * DEPTH_2 + 1
        gains = sb(stack, "gains", [P, n_gain * DC])
        ident = sb(stack, "ident", [P, P])
        ident_bf = sb(stack, "ident_bf", [P, P], BF16)
        ones = sb(stack, "ones", [P, P])

        loads = {}

        def load(name, dst, src):
            s = sem(f"load_{name}")
            sync.ops.append(lambda e: e.dma_start(dst, src).then_inc(s, 16))
            loads[name] = (s, 16)
            return loads[name]

        for c in range(DC):
            load(f"x{c}", x[:, c, :], dram["x_t"][:, c, :])
            if c == 0:
                load("gains", gains[:, :], dram["gains"])
                load("ones", ones[:, :], dram["ones"])
        load("ident", ident[:, :], dram["ident"])
        ident_bf_ready = act.do(lambda e: e.activation(ident_bf[:, :], ident[:, :], ACT.Copy),
                                loads["ident"])

        def gain(g, c):
            return gains[:, g * DC + c:g * DC + c + 1]

        raw_arrived = [sem(f"raw_arrived{i}") for i in range(RAW)]
        raw_split = [None] * RAW
        slot_used = [None] * SPLIT
        split_ready = {}
        stream = {"split": 0, "next": 0}

        def panel_shape(i):
            name, j = order[i]
            r, rows, c, cols = matrices[name][j]
            return rows // P, cols

        def split_panel():
            i = stream["split"]
            if i == len(order):
                return
            stream["split"] += 1
            name, j = order[i]
            at = sum(p[1] * p[3] for p in matrices[name][:j])
            kc, cols = panel_shape(i)
            n, raw, slot = kc * cols, i % RAW, i % SPLIT
            src = dram[name][at:at + P * n].rearrange("(p w) -> p w", p=P)
            sync.wait(raw_split[raw])
            sync.ops.append(lambda e: e.dma_start(w_raw[:, raw, 0:n], src).then_inc(raw_arrived[raw], 16))
            arrived = (raw_arrived[raw], 16 * (i // RAW + 1))
            rounded = act.do(lambda e: e.activation(w_hi[:, slot, 0:n], w_raw[:, raw, 0:n], ACT.Copy),
                             arrived, slot_used[slot], split_ready.get(i - SPLIT))
            split_ready[i] = dve.do(
                lambda e: e.tensor_tensor(w_lo[:, slot, 0:n], w_raw[:, raw, 0:n],
                                          w_hi[:, slot, 0:n].bitcast(F32), ALU.subtract),
                arrived, rounded, slot_used[slot])
            raw_split[raw] = split_ready[i]

        def product(name, hi, lo, outs, ready, bank_free):
            i = stream["next"]
            assert order[i][0] == name, (order[i], name)
            stream["next"] += 1
            while stream["split"] <= min(i + AHEAD, len(order) - 1):
                split_panel()
            kc, cols = panel_shape(i)
            slot = i % SPLIT
            pe.wait(split_ready[i])
            pe.wait(bank_free)
            parts = [(w_hi, 0), (w_hi, 1), (w_lo, 0)]
            for c in range(kc):
                pe.wait(ready[c] if ready else None)
                for n, (w, part) in enumerate(parts):
                    lhs = w[:, slot, c * cols:(c + 1) * cols]
                    for dst, src_hi, src_lo in [(outs, hi, lo)] if not isinstance(outs, list) else [
                            (o, h, g) for o, h, g in zip(outs, hi, lo)]:
                        src = (src_hi if part == 0 else src_lo)(c)
                        first, last = c == 0 and n == 0, c == kc - 1 and n == 2
                        op = (lambda e, d=dst, a=lhs, b=src, f=first, z=last:
                              e.matmul(d, a, b, start=f, stop=z))
                        if last and (not isinstance(outs, list) or dst is outs[-1]):
                            done = pe.do(op)
                        else:
                            pe.run(op)
            slot_used[slot] = done
            return done

        turn = {"l": 0, "t": 0, "s": 0}

        def next_l():
            turn["l"] ^= 1
            return turn["l"]

        def next_t():
            turn["t"] ^= 1
            return turn["t"]

        xg_ready = [None] * DC
        x_written = [None] * DC
        x_read = [None] * DC
        state = {"xg_used": None, "sum_used": None, "rstd": None, "rstd_read": None}
        square_read = [None, None]
        sum_mark = [None]

        def fence():
            marks = [e.last for e in (pe, act, dve, pool)]
            for e in (act, dve, pool):
                e.wait(*marks)

        def x_product(name, bank=None):
            b = next_l() if bank is None else bank
            kc, cols = panel_shape(stream["next"])
            done = product(name, lambda c: xg_hi[:, c, META:], lambda c: xg_lo[:, c, META:],
                           bank_l[b][0:cols, :], xg_ready, free_l[b])
            state["xg_used"] = done
            return b, done

        def add_square(c, written):
            if c == 0:
                sum_mark[0] = act.do(lambda e: e.activation(square_sum[:, :], x[:, 0, :], ACT.Square),
                                     written, state["sum_used"], sum_mark[0])
                x_read[0] = [sum_mark[0]]
                return
            half = c % 2
            squared = act.do(lambda e: e.activation(squares[:, half, :], x[:, c, :], ACT.Square),
                             written, square_read[half])
            sum_mark[0] = dve.do(lambda e: e.tensor_tensor(square_sum[:, :], square_sum[:, :],
                                                           squares[:, half, :], ALU.add),
                                 squared, sum_mark[0])
            square_read[half] = sum_mark[0]
            x_read[c] = [squared]

        def split_x(c, g, written):
            rounded = act.do(lambda e: e.activation(xg_hi[:, c, META:], x[:, c, :], ACT.Copy, scale=gain(g, c)),
                             written, state["xg_used"], xg_ready[c], loads["gains"])
            xg_ready[c] = dve.do(
                lambda e: e.scalar_tensor_tensor(xg_lo[:, c, META:], x[:, c, :], gain(g, c),
                                                 xg_hi[:, c, META:].bitcast(F32), ALU.mult, ALU.subtract),
                written, rounded, state["xg_used"], loads["gains"])
            x_read[c] = (x_read[c] or []) + [rounded, xg_ready[c]]

        def token_rstd():
            summed = pe.do(lambda e: e.matmul(bank_o[:, :], ones[:, :], square_sum[:, :],
                                              start=True, stop=True),
                           sum_mark[0], free_o[0], loads["ones"])
            state["sum_used"] = summed
            logged = act.do(lambda e: e.activation(rstd[:, :], bank_o[:, :], ACT.Ln,
                                                   scale=1.0 / D, bias=eps_col[:, 0:1]),
                            summed, dve.last, eps_ready)
            free_o[0] = logged
            state["rstd"] = act.do(lambda e: e.activation(rstd[:, :], rstd[:, :], ACT.Exp, scale=-0.5), logged)

        eps_col = sb(stack, "eps_col", [P, 1])
        eps_ready = dve.do(lambda e: e.memset(eps_col[:, :], EPS))

        def add_to_x(c, bank, done, factor, g=None, stats=True):
            written = dve.do(
                lambda e: e.scalar_tensor_tensor(x[:, c, :], bank_l[bank][:, :], factor, x[:, c, :],
                                                 ALU.mult, ALU.add),
                done, x_read[c], x_written[c])
            free_l[bank] = written
            x_written[c] = written
            x_read[c] = None
            if stats:
                add_square(c, written)
            if g is not None:
                split_x(c, g, written)

        def split_value(hi, lo, value, marks, free=None):
            rounded = act.do(lambda e: e.activation(hi, value, ACT.Copy), marks, free)
            return dve.do(lambda e: e.tensor_tensor(lo, value, hi.bitcast(F32), ALU.subtract), rounded, free)

        def feed_forward(tag, gate, up, down, groups, factor, g, expert_scale=None, stats=True):
            fence()
            with ExitStack() as phase:
                hid_hi = sb(phase, f"hid_hi_{tag}", [P, 8, T], F32R)
                hid_lo = sb(phase, f"hid_lo_{tag}", [P, 8, T], F32R)
                gated = sb(phase, f"gated_{tag}", [P, 2, T])
                silu = sb(phase, f"silu_{tag}", [P, 2, T])
                val = sb(phase, f"val_{tag}", [P, 2, T])
                if expert_scale:
                    expert_scale = expert_scale(phase)
                hid_used, j = None, 0
                silu_read, val_read, gated_read = [None] * 2, [None] * 2, [None] * 2
                val_written = [None] * 2
                silu_w, gated_w = [None] * 2, [None] * 2
                for n_group, n in enumerate(groups):
                    hid_ready = [None] * n
                    for i in range(n):
                        h = j % 2
                        bg, gate_done = x_product(gate)
                        gated_w[h] = dve.do(lambda e, h=h, b=bg: e.tensor_tensor(
                            gated[:, h, :], bank_l[b][:, :], rstd[:, :], ALU.mult),
                            gate_done, state["rstd"], gated_read[h])
                        free_l[bg] = gated_w[h]
                        silu_w[h] = act.do(lambda e, h=h: e.activation(silu[:, h, :], gated[:, h, :], ACT.Silu),
                                           gated_w[h], silu_read[h])
                        gated_read[h] = silu_w[h]
                        scale, scale_mark = (rstd[:, :], state["rstd"]) if not expert_scale else expert_scale(j)
                        bu, up_done = x_product(up)
                        product_w = dve.do(lambda e, h=h, b=bu: e.tensor_tensor(
                            val[:, h, :], bank_l[b][:, :], silu[:, h, :], ALU.mult),
                            up_done, silu_w[h], val_read[h])
                        free_l[bu] = product_w
                        silu_read[h] = product_w
                        val_w = dve.do(lambda e, h=h, s=scale: e.tensor_tensor(
                            val[:, h, :], val[:, h, :], s, ALU.mult), product_w, scale_mark)
                        hid_ready[i] = split_value(hid_hi[:, i, :], hid_lo[:, i, :], val[:, h, :],
                                                   val_w, hid_used)
                        val_read[h] = hid_ready[i]
                        j += 1
                    last = n_group == len(groups) - 1
                    for m in range(DC):
                        b = next_l()
                        hid_used = product(down, lambda c: hid_hi[:, c, :], lambda c: hid_lo[:, c, :],
                                           bank_l[b][:, :], hid_ready, free_l[b])
                        add_to_x(m, b, hid_used, factor, g if last else None, stats and last)
                        if last and m == DC - 1:
                            token_rstd()

        def transpose_to(dst, src, n_out, n_in, t, at, marks):
            return pe.do(lambda e: e.transpose(bank_t[t][0:n_out, at:at + n_in], src, ident[0:n_in, 0:n_in]),
                         marks, loads["ident"])

        def mixer_1():
            with ExitStack() as phase:
                meta = sb(phase, "meta", [P, DC, META])
                meta_sq = sb(phase, "meta_sq", [P, DC, META])
                meta_sum = sb(phase, "meta_sum", [P, META])
                all_rstd = sb(phase, "all_rstd", [P, L])
                meta_g = sb(phase, "meta_g", [P, DC, META])
                gate_up = sb(phase, "gate_up", [GATE_RANK, 256])
                vecs = sb(phase, "vecs", [P, 2 + 4 + 1])
                pool_w = sb(phase, "pool_w", [P, 4, P])
                resets = sb(phase, "resets", [P, L])
                gla_mask = sb(phase, "gla_mask", [P, T], I32)
                y_hi = sb(phase, "y1_hi", [P, DC, T], F32R)
                y_lo = sb(phase, "y1_lo", [P, DC, T], F32R)
                load("meta", meta[:, :, :], dram["meta_t"])
                load("gate_up", gate_up[:, :], dram["w_gate_up"])
                load("vecs", vecs[:, :], dram["vecs"])
                load("resets", resets[:, :], dram["resets"])
                load("gla_mask", gla_mask[:, :], dram["gla_mask"])
                load("pool_w", pool_w[:, :, :], dram["pool_w"])

                sq = act.do(lambda e: e.activation(meta_sq[:, :, :], meta[:, :, :], ACT.Square), loads["meta"])
                sm = dve.do(lambda e: e.tensor_reduce(meta_sum[:, :], meta_sq[:, :, :].rearrange("p c t -> p t c"),
                                                      AX, ALU.add), sq)
                mm = pe.do(lambda e: e.matmul(bank_t[0][:, 0:META], ones[:, :], meta_sum[:, :],
                                              start=True, stop=True), sm, loads["ones"])
                lg = act.do(lambda e: e.activation(all_rstd[:, 0:META], bank_t[0][:, 0:META], ACT.Ln,
                                                   scale=1.0 / D, bias=eps_col[:, 0:1]), mm, eps_ready)
                free_t[0] = lg
                meta_rstd_w = act.do(lambda e: e.activation(all_rstd[:, 0:META], all_rstd[:, 0:META], ACT.Exp,
                                                            scale=-0.5), lg)
                mg = dve.do(lambda e: e.tensor_tensor(
                    meta_g[:, :, :], meta[:, :, :],
                    gains[:, 0:DC].rearrange("p (c o) -> p c o", o=1).to_broadcast([P, DC, META]), ALU.mult),
                    loads["meta"], loads["gains"])
                meta_ready = split_value(xg_hi[:, :, 0:META], xg_lo[:, :, 0:META], meta_g[:, :, :], mg)

                for c in range(DC):
                    add_square(c, loads[f"x{c}"])
                    split_x(c, 0, loads[f"x{c}"])
                token_rstd()
                rstd_copied = dve.do(lambda e: e.tensor_copy(all_rstd[:, META:], rstd[:, :]),
                                     state["rstd"], meta_rstd_w)

                half = L // 2

                def both(name, dst, rows=P, dst_free=None):
                    b, t = next_l(), next_t()
                    done = product(name, [lambda c: xg_hi[:, c, 0:half], lambda c: xg_hi[:, c, half:]],
                                   [lambda c: xg_lo[:, c, 0:half], lambda c: xg_lo[:, c, half:]],
                                   [bank_l[b][:, 0:half], bank_t[t][:, 0:half]],
                                   [[r, meta_ready] for r in xg_ready], [free_l[b], free_t[t]])
                    state["xg_used"] = done
                    free_l[b] = dve.do(lambda e: e.tensor_tensor(dst[0:rows, 0:half], bank_l[b][0:rows, 0:half],
                                                                 all_rstd[0:rows, 0:half], ALU.mult),
                                       done, rstd_copied, dst_free)
                    free_t[t] = dve.do(lambda e: e.tensor_tensor(dst[0:rows, half:], bank_t[t][0:rows, 0:half],
                                                                 all_rstd[0:rows, half:], ALU.mult),
                                       done, rstd_copied, dst_free)
                    return [free_l[b], free_t[t]]

                with ExitStack() as gla:
                    g_low = sb(gla, "g_low", [GATE_RANK, L])
                    k_f = sb(gla, "k_f", [P, 2, L])
                    q_f = sb(gla, "q_f", [P, 2, T])
                    v_f = sb(gla, "v_f", [P, 2, L])
                    v_tok = sb(gla, "v_tok", [P, TB, 512])
                    v_meta = sb(gla, "v_meta", [META, 512])
                    la = sb(gla, "la", [P, 2, L])
                    e1 = sb(gla, "e1", [P, L])
                    bsum = sb(gla, "bsum", [P, 2, L])
                    k_end = sb(gla, "k_end", [P, 2, L])
                    ke_tok = sb(gla, "ke_tok", [P, TB, 256])
                    ke_meta = sb(gla, "ke_meta", [META, 256])
                    decay = sb(gla, "decay", [P, 2, N_CHUNK])
                    carry = sb(gla, "carry", [P, 2, N_CHUNK, GLA_V])
                    scores = sb(gla, "scores", [P, 2, T])
                    pool_u = sb(gla, "pool_u", [P, L])
                    pool_s = sb(gla, "pool_s", [P, 2, L])
                    o_f, o_square, head_rstd, r_f = (k_end[:, :, 0:T], e1[:, 0:T], v_f[:, 0, 0:T],
                                                     bsum[:, :, 0:T])

                    g_ready = both("g", g_low, GATE_RANK)
                    k_w = [both("k", k_f[:, 0, :])]
                    la_w = []
                    for hp in range(2):
                        t = next_t()
                        b = next_l()
                        w = gate_up[:, hp * P:(hp + 1) * P]
                        pe.run(lambda e, b=b, w=w: e.matmul(bank_l[b][:, :], w, g_low[:, META:], start=True, stop=True),
                               g_ready, free_l[b], loads["gate_up"])
                        m = pe.do(lambda e, t=t, w=w: e.matmul(bank_t[t][:, 0:META], w, g_low[:, 0:META],
                                                               start=True, stop=True), free_t[t])
                        bias = vecs[:, hp:hp + 1]
                        w1 = dve.do(lambda e, b=b, hp=hp, s=bias: e.tensor_scalar(
                            la[:, hp, META:], bank_l[b][:, :], s, None, ALU.add), m, loads["vecs"])
                        free_l[b] = w1
                        w2 = dve.do(lambda e, t=t, hp=hp, s=bias: e.tensor_scalar(
                            la[:, hp, 0:META], bank_t[t][:, 0:META], s, None, ALU.add), m)
                        free_t[t] = w2
                        a = act.do(lambda e, hp=hp: e.activation(e1[:, :], la[:, hp, :], ACT.Abs), w1, w2,
                                   la_w[-1] if la_w else None)
                        a = act.do(lambda e: e.activation(e1[:, :], e1[:, :], ACT.Exp, scale=-1.0), a)
                        a = act.do(lambda e: e.activation(e1[:, :], e1[:, :], ACT.Ln, bias=1.0), a)
                        la_w.append(dve.do(lambda e, hp=hp: e.scalar_tensor_tensor(
                            la[:, hp, :], la[:, hp, :], 0.0, e1[:, :], ALU.min, ALU.subtract), a))
                    sums = [dve.do(lambda e, hp=hp: e.tensor_tensor_scan(
                        bsum[:, hp, :], resets[:, :], la[:, hp, :], 0.0, ALU.mult, ALU.add),
                        la_w[hp], loads["resets"]) for hp in range(2)]

                    k_w.append(both("k", k_f[:, 1, :]))

                    ke_w, decay_w = [], []
                    for hp in range(2):
                        blocks = bsum[:, hp, META:].rearrange("p (n c) -> p n c", c=CHUNK)
                        a1 = dve.do(lambda e, hp=hp, v=blocks: e.tensor_tensor(
                            k_end[:, hp, META:].rearrange("p (n c) -> p n c", c=CHUNK),
                            v[:, :, CHUNK - 1:CHUNK].to_broadcast([P, N_CHUNK, CHUNK]), v, ALU.subtract), sums[hp])
                        a2 = dve.do(lambda e, hp=hp: e.tensor_scalar(
                            k_end[:, hp, 0:META], bsum[:, hp, 0:META], bsum[:, hp, META - 1:META], -1.0,
                            ALU.subtract, ALU.mult), sums[hp])
                        ex = act.do(lambda e, hp=hp: e.activation(k_end[:, hp, :], k_end[:, hp, :], ACT.Exp,
                                                                  scale=1.0 / 16), a1, a2)
                        decay_w.append(act.do(lambda e, hp=hp, v=blocks: e.activation(
                            decay[:, hp, :], v[:, :, CHUNK - 1], ACT.Exp, scale=1.0 / 16), sums[hp]))
                        ke_w.append(dve.do(lambda e, hp=hp: e.tensor_tensor(
                            k_end[:, hp, :], k_end[:, hp, :], k_f[:, hp, :], ALU.mult), ex, k_w[hp]))
                    exps = []
                    for hp in range(2):
                        p1 = act.do(lambda e, hp=hp: e.activation(la[:, hp, :], bsum[:, hp, :], ACT.Exp,
                                                                  scale=1.0 / 16), sums[hp])
                        p2 = act.do(lambda e, hp=hp: e.activation(bsum[:, hp, :], bsum[:, hp, :], ACT.Exp,
                                                                  scale=-1.0 / 16), p1, decay_w[hp], ke_w[hp])
                        exps.append((p1, p2))
                    kt_w = [dve.do(lambda e, hp=hp: e.tensor_tensor(k_f[:, hp, :], k_f[:, hp, :],
                                                                    bsum[:, hp, :], ALU.mult), exps[hp][1], ke_w[hp])
                            for hp in range(2)]

                    def to_tokens(src, dst, dst_meta, col, marks):
                        t = next_t()
                        for blk in range(TB):
                            m = pe.do(lambda e, blk=blk: e.transpose(
                                bank_t[t][:, blk * P:(blk + 1) * P],
                                src[:, META + blk * P:META + (blk + 1) * P], ident[:, :]),
                                marks, free_t[t], loads["ident"])
                        free_t[t] = act.do(lambda e: e.activation(
                            dst[:, :, col:col + P], bank_t[t][:, :].rearrange("p (b c) -> p b c", c=P), ACT.Copy), m)
                        r1 = free_t[t]
                        t2 = next_t()
                        m = pe.do(lambda e: e.transpose(bank_t[t2][0:META, 0:P], src[:, 0:META], ident[:, :]),
                                  free_t[t2])
                        free_t[t2] = act.do(lambda e: e.activation(dst_meta[:, col:col + P],
                                                                   bank_t[t2][0:META, 0:P], ACT.Copy), m)
                        return [r1, free_t[t2]], m

                    v_w, v_read, w = [], [None, None], None
                    for i in range(4):
                        w_next = both("v", v_f[:, i % 2, :], dst_free=v_read[i % 2])
                        if i:
                            r, v_read[(i - 1) % 2] = to_tokens(v_f[:, (i - 1) % 2, :], v_tok, v_meta, (i - 1) * P, w)
                            v_w += r
                        w = w_next
                    to_q = x_product("q")
                    r, _ = to_tokens(v_f[:, 1, :], v_tok, v_meta, 3 * P, w)
                    v_w += r
                    ke_ready = []
                    for hp in range(2):
                        r, _ = to_tokens(k_end[:, hp, :], ke_tok, ke_meta, hp * P, ke_w[hp])
                        ke_ready += r

                    qt_w = []

                    def scale_q(hp, b, done):
                        w = free_l[b] = dve.do(lambda e: e.scalar_tensor_tensor(
                            q_f[:, hp, :], bank_l[b][:, :], GLA_K ** -0.5, rstd[:, :], ALU.mult, ALU.mult),
                            done, state["rstd"])
                        qt_w.append(dve.do(lambda e: e.tensor_tensor(
                            q_f[:, hp, :], q_f[:, hp, :], la[:, hp, META:], ALU.mult), w, exps[hp][0]))

                    scale_q(0, *to_q)

                    carry_w = [[None] * N_CHUNK, [None] * N_CHUNK]

                    def carry_step(n):
                        s = (n + 1) % 3
                        po = 64 * (n % 2)
                        for h in range(GLA_HEADS):
                            if n < 0:
                                lhs, rhs = ke_meta[:, h * 64:(h + 1) * 64], v_meta[:, h * P:(h + 1) * P]
                            else:
                                lhs = ke_tok[po:po + 64, n // 2, h * 64:(h + 1) * 64]
                                rhs = v_tok[po:po + 64, n // 2, h * P:(h + 1) * P]
                            d = bank_s[64 * (h % 2):64 * (h % 2) + 64, s, (h // 2) * P:(h // 2 + 1) * P]
                            m = pe.do(lambda e, d=d, a=lhs, b=rhs, h=h: e.matmul(
                                d, a, b, start=(h < 2), stop=True, skip_group_check=True),
                                ke_ready, v_w, free_s[s])
                        for hp in range(2):
                            src = bank_s[:, s, hp * P:(hp + 1) * P]
                            if n < 0:
                                carry_w[hp][0] = dve.do(lambda e, hp=hp, v=src: e.tensor_copy(
                                    carry[:, hp, 0, :], v), m)
                            else:
                                carry_w[hp][n + 1] = dve.do(lambda e, hp=hp, v=src: e.scalar_tensor_tensor(
                                    carry[:, hp, n + 1, :], carry[:, hp, n, :], decay[:, hp, n:n + 1], v,
                                    ALU.mult, ALU.add), m, carry_w[hp][n], decay_w[hp])
                            free_s[s] = carry_w[hp][n + 1]

                    for n in range(-1, 2):
                        carry_step(n)
                    to_q = x_product("q")
                    for n in range(2, 5):
                        carry_step(n)
                    scale_q(1, *to_q)
                    for n in range(5, N_CHUNK - 1):
                        carry_step(n)
                    zeroed = pool.do(lambda e: e.memset(scores[:, :, :], 0.0))

                    y_w = [None] * DC
                    scores_read = [None, None]
                    o_read, r_read, sq_read = [ke_ready, ke_ready], [kt_w, kt_w], la_w
                    u_read, p_read = None, None

                    def finish_head(h, o_w, o_sq, r_w):
                        z, t = h % 2, next_t()
                        m = pe.do(lambda e: e.matmul(bank_t[t][:, :], ones[:, :], o_square[:, :],
                                                     start=True, stop=True), o_sq, free_t[t])
                        a = act.do(lambda e: e.activation(head_rstd[:, :], bank_t[t][:, :], ACT.Ln,
                                                          scale=1.0 / GLA_V, bias=eps_col[:, 0:1]), m, marks["norm"])
                        free_t[t] = a
                        a = act.do(lambda e: e.activation(head_rstd[:, :], head_rstd[:, :], ACT.Exp, scale=-0.5), a)
                        v = dve.do(lambda e: e.scalar_tensor_tensor(
                            o_f[:, z, :], o_f[:, z, :], vecs[:, 6:7], head_rstd[:, :], ALU.mult, ALU.mult), a, o_w)
                        marks["norm"] = v
                        v = dve.do(lambda e: e.tensor_tensor(o_f[:, z, :], o_f[:, z, :], r_f[:, z, :], ALU.mult),
                                   v, r_w)
                        r_read[z] = v
                        y_w[4 + h] = o_read[z] = split_value(y_hi[:, 4 + h, :], y_lo[:, 4 + h, :], o_f[:, z, :], v)
                        return m

                    marks = {"norm": v_w}
                    pending = None
                    for h in range(GLA_HEADS):
                        hp, po, z = h // 2, 64 * (h % 2), h % 2
                        u_w = both("pool", pool_u[:, :], dst_free=u_read)
                        width, src, cur, flip = 1, pool_u[:, :], u_w, 0
                        while width < POOL_WINDOWS[h]:
                            dst = pool_s[:, flip, :]
                            cur = (pool if width < 4 else dve).do(lambda e, d=dst, s=src, w=width: e.tensor_tensor(
                                d[:, 2 * w - 1:L], s[:, 2 * w - 1:L], s[:, w - 1:L - w], ALU.add),
                                cur, p_read, zeroed)
                            src, width, flip = dst, 2 * width, flip ^ 1
                        dst = pool_s[:, flip, META:L]
                        pooled = dve.do(lambda e, d=dst, s=src, h=h: e.scalar_tensor_tensor(
                            d, s[:, META:L], 1.0 / POOL_WINDOWS[h], pool_u[:, META:L], ALU.mult, ALU.subtract),
                            cur, u_w)

                        t = next_t()
                        for blk in range(TB):
                            m = pe.do(lambda e, a=blk * P, b=(blk + 1) * P, hp=hp, po=po, t=t: e.matmul(
                                bank_t[t][:, a:b], k_f[po:po + 64, hp, META + a:META + b],
                                q_f[po:po + 64, hp, a:b], start=True, stop=True),
                                kt_w[hp], qt_w[hp], free_t[t])
                        scores_w = free_t[t] = dve.do(lambda e, z=z, t=t: e.copy_predicated(
                            scores[:, z, :], gla_mask[:, :], bank_t[t][:, :]),
                            m, zeroed, scores_read[z], loads["gla_mask"])
                        if pending:
                            sq_read = finish_head(*pending)

                        b, done = x_product("r")
                        r_w = free_l[b] = dve.do(lambda e, b=b, z=z: e.tensor_tensor(
                            r_f[:, z, :], bank_l[b][:, :], rstd[:, :], ALU.mult), done, state["rstd"], r_read[z])
                        r_w = act.do(lambda e, z=z: e.activation(r_f[:, z, :], r_f[:, z, :], ACT.Silu), r_w)

                        b = next_l()
                        m = pe.do(lambda e, b=b, d=dst, h=h: e.matmul(bank_l[b][:, :], pool_w[:, h, :], d,
                                                                      start=True, stop=True),
                                  pooled, free_l[b], loads["pool_w"])
                        u_read, p_read = pooled, m
                        sc = vecs[:, 2 + h:3 + h]
                        hi = act.do(lambda e, b=b, h=h, s=sc: e.activation(y_hi[:, h, :], bank_l[b][:, :],
                                                                           ACT.Copy, scale=s), m, loads["vecs"])
                        y_w[h] = free_l[b] = dve.do(lambda e, b=b, h=h, s=sc: e.scalar_tensor_tensor(
                            y_lo[:, h, :], bank_l[b][:, :], s, y_hi[:, h, :].bitcast(F32),
                            ALU.mult, ALU.subtract), hi)

                        for blk in range(TB):
                            pe.run(lambda e, blk=blk, h=h, z=z: e.matmul(
                                bank_o[:, blk * P:(blk + 1) * P], v_tok[:, blk, h * P:(h + 1) * P],
                                scores[:, z, blk * P:(blk + 1) * P], start=(blk == 0), stop=False,
                                skip_group_check=True), scores_w, free_o[0], v_w)
                        for n in range(N_CHUNK):
                            m = pe.do(lambda e, n=n, hp=hp, po=po: e.matmul(
                                bank_o[:, n * CHUNK:(n + 1) * CHUNK], carry[po:po + 64, hp, n, :],
                                q_f[po:po + 64, hp, n * CHUNK:(n + 1) * CHUNK], start=False,
                                stop=(n == N_CHUNK - 1), skip_group_check=True), carry_w[hp][n])
                        scores_read[z] = m
                        o_w = act.do(lambda e, z=z: e.activation(o_f[:, z, :], bank_o[:, :], ACT.Copy), m, o_read[z])
                        o_sq = free_o[0] = act.do(lambda e: e.activation(o_square[:, :], bank_o[:, :], ACT.Square),
                                                  m, sq_read)
                        pending = (h, o_w, o_sq, r_w)
                    finish_head(*pending)
                for m in range(DC):
                    b = next_l()
                    done = product("out", lambda c: y_hi[:, c, :], lambda c: y_lo[:, c, :],
                                   bank_l[b][:, :], y_w, free_l[b])
                    add_to_x(m, b, done, 1.0, 1)
                token_rstd()

        comb_t = sb(stack, "comb_t", [N_EXPERTS, T])
        router_bias = sb(stack, "router_bias", [ROUTES, 1])
        load("router_bias", router_bias[:, :], dram["router_bias"])
        comb = {}

        def router():
            fence()
            with ExitStack() as phase:
                lt = sb(phase, "logits_t", [ROUTES, T])
                lg = sb(phase, "logits", [P, TB, ROUTES])
                rank = sb(phase, "rank", [P, TB, 4])
                hot = sb(phase, "hot", [P, TB, 4])
                tmp4 = sb(phase, "tmp4", [P, TB, 4])
                tmp16 = sb(phase, "tmp16", [P, TB, 4, 4])
                el = sb(phase, "el", [P, TB, 4])
                pick = sb(phase, "pick", [P, TB, 4])
                wsum = sb(phase, "wsum", [P, TB, 4])
                col = sb(phase, "col", [P, 8, TB, 1])
                combine = sb(phase, "combine", [P, TB, N_EXPERTS])
                load("rank", rank[:, :, :], dram["rank"])
                b, done = x_product("route")
                m = free_l[b] = dve.do(lambda e: e.tensor_tensor(lt[:, :], bank_l[b][0:ROUTES, :],
                                                                 rstd[0:ROUTES, :], ALU.mult), done, state["rstd"])
                m = dve.do(lambda e: e.tensor_scalar(lt[:, :], lt[:, :], router_bias[:, 0:1], None, ALU.add),
                           m, loads["router_bias"])
                t = next_t()
                for blk in range(TB):
                    p = pe.do(lambda e, blk=blk: e.transpose(bank_t[t][:, blk * 32:blk * 32 + ROUTES],
                                                             lt[:, blk * P:(blk + 1) * P],
                                                             ident[0:ROUTES, 0:ROUTES]), m, free_t[t])
                m = free_t[t] = dve.do(lambda e: e.tensor_copy(
                    lg[:, :, :], bank_t[t][:, 0:TB * 32].rearrange("p (b r) -> p b r", r=32)[:, :, 0:ROUTES]), p)

                def chain(make, *marks):
                    return dve.do(make, dve.last, *marks)

                def wide(v):
                    return v.to_broadcast([P, TB, 4])

                def first_of(values, peak, dst):
                    chain(lambda e: e.tensor_tensor(tmp4[:, :, :], values, wide(peak), ALU.is_equal))
                    chain(lambda e: e.tensor_tensor(tmp4[:, :, :], tmp4[:, :, :], rank[:, :, :], ALU.mult),
                          loads["rank"])
                    chain(lambda e: e.tensor_reduce(col[:, 7, :, :], tmp4[:, :, :], AX, ALU.max))
                    chain(lambda e: e.tensor_tensor(dst, tmp4[:, :, :], wide(col[:, 7, :, :]), ALU.is_equal))

                g_l = lg[:, :, 0:N_GROUPS]
                chain(lambda e: e.tensor_reduce(col[:, 0, :, :], g_l, AX, ALU.max))
                first_of(g_l, col[:, 0, :, :], hot[:, :, :])
                m = chain(lambda e: e.tensor_tensor(tmp4[:, :, :], g_l, wide(col[:, 0, :, :]), ALU.subtract))
                m = act.do(lambda e: e.activation(tmp4[:, :, :], tmp4[:, :, :], ACT.Exp), m)
                chain(lambda e: e.tensor_reduce(col[:, 1, :, :], tmp4[:, :, :], AX, ALU.add), m)
                e_l = lg[:, :, N_GROUPS:].rearrange("p b (g e) -> p b g e", e=4)
                for g in range(N_GROUPS):
                    chain(lambda e, g=g: e.tensor_tensor(
                        tmp16[:, :, g, :], e_l[:, :, g, :], wide(hot[:, :, g:g + 1]), ALU.mult))
                chain(lambda e: e.tensor_tensor(tmp4[:, :, :], tmp16[:, :, 0, :], tmp16[:, :, 1, :], ALU.add))
                chain(lambda e: e.tensor_tensor(el[:, :, :], tmp16[:, :, 2, :], tmp16[:, :, 3, :], ALU.add))
                chain(lambda e: e.tensor_tensor(el[:, :, :], el[:, :, :], tmp4[:, :, :], ALU.add))
                chain(lambda e: e.tensor_reduce(col[:, 2, :, :], el[:, :, :], AX, ALU.max))
                first_of(el[:, :, :], col[:, 2, :, :], wsum[:, :, :])
                m = chain(lambda e: e.tensor_tensor(pick[:, :, :], el[:, :, :], wide(col[:, 2, :, :]), ALU.subtract))
                m = act.do(lambda e: e.activation(pick[:, :, :], pick[:, :, :], ACT.Exp), m)
                chain(lambda e: e.scalar_tensor_tensor(el[:, :, :], wsum[:, :, :], -3e38, el[:, :, :],
                                                       ALU.mult, ALU.add))
                chain(lambda e: e.tensor_reduce(col[:, 3, :, :], el[:, :, :], AX, ALU.max))
                first_of(el[:, :, :], col[:, 3, :, :], el[:, :, :])
                chain(lambda e: e.tensor_tensor(wsum[:, :, :], wsum[:, :, :], el[:, :, :], ALU.add))
                chain(lambda e: e.tensor_tensor(wsum[:, :, :], wsum[:, :, :], pick[:, :, :], ALU.mult), m)
                chain(lambda e: e.tensor_reduce(col[:, 4, :, :], wsum[:, :, :], AX, ALU.add))
                chain(lambda e: e.tensor_tensor(col[:, 5, :, :], col[:, 4, :, :], col[:, 1, :, :], ALU.mult))
                chain(lambda e: e.reciprocal(col[:, 6, :, :], col[:, 5, :, :]))
                chain(lambda e: e.tensor_tensor(wsum[:, :, :], wsum[:, :, :], wide(col[:, 6, :, :]), ALU.mult))
                for g in range(N_GROUPS):
                    m = chain(lambda e, g=g: e.tensor_tensor(
                        combine[:, :, 4 * g:4 * g + 4], wsum[:, :, :], wide(hot[:, :, g:g + 1]), ALU.mult))
                t2 = next_t()
                for blk in range(TB):
                    p = pe.do(lambda e, blk=blk: e.transpose(
                        bank_t[t2][0:N_EXPERTS, blk * P:(blk + 1) * P], combine[:, blk, :], ident[:, :]),
                        m, free_t[t2])
                comb["ready"] = free_t[t2] = dve.do(lambda e: e.tensor_copy(comb_t[:, :],
                                                                           bank_t[t2][0:N_EXPERTS, :]), p)

        def expert_scales(phase):
            picks = sb(phase, "picks", [N_EXPERTS, N_EXPERTS, P])
            scale = sb(phase, "expert_scale", [P, 2, T])
            load("picks", picks[:, :, :], dram["picks"])
            marks = {}

            def of_chunk(j):
                ex = j // 2
                if ex not in marks:
                    m = pe.do(lambda e: e.matmul(bank_o[:, :], picks[:, ex, :], comb_t[:, :],
                                                 start=True, stop=True),
                              comb["ready"], free_o[0], loads["picks"])
                    marks[ex] = free_o[0] = dve.do(lambda e: e.tensor_tensor(
                        scale[:, ex % 2, :], bank_o[:, :], rstd[:, :], ALU.mult), m, dve.last)
                return scale[:, ex % 2, :], marks[ex]
            return of_chunk

        def normalise(g, g_next=None, store=False):
            for c in range(DC):
                w = x_written[c] = dve.do(lambda e, c=c: e.scalar_tensor_tensor(
                    x[:, c, :], x[:, c, :], gain(g, c), rstd[:, :], ALU.mult, ALU.mult),
                    state["rstd"], x_read[c], x_written[c])
                x_read[c] = None
                if store:
                    sync.wait(w)
                    sync.ops.append(lambda e, c=c: e.dma_start(out[:, c, :], x[:, c, :]).then_inc(stored, 16))
                else:
                    add_square(c, w)
                    split_x(c, g_next, w)
            if not store:
                token_rstd()

        stored = sem("stored")

        rotate = sb(stack, "rotate", [P, P])
        suffix = sb(stack, "suffix", [P, P])
        minus = sb(stack, "minus", [P, P])
        strict = sb(stack, "strict", [P, P])
        masks_f = sb(stack, "masks_bf", [P, 2 * P + 4 * P + 4 * P + P], BF16)
        load("rotate", rotate[:, :], dram["rotate"])
        load("suffix", suffix[:, :], dram["suffix"])
        load("minus", minus[:, :], dram["minus"])
        load("strict", strict[:, :], dram["strict"])
        load("masks", masks_f[:, :], dram["masks"])
        MASK_END = (2 * P, 6 * P, 10 * P)

        def mixer_2(l):
            g_out = 3 + 3 * l + 2
            name = f"in_{l}"
            fence()
            with ExitStack() as phase:
                o_f = sb(phase, f"o_f_{l}", [P, 4, T])
                gates = sb(phase, f"gates_{l}", [P, 16, T])
                att = ExitStack()
                qk = sb(att, f"qk_{l}", [P, 16, T])
                v_tok = sb(att, f"vt_{l}", [P, TB, D])
                rope = ExitStack()
                cos = sb(rope, f"cos_{l}", [P, T])
                sin = sb(rope, f"sin_{l}", [P, T])
                rot = sb(rope, f"rot_{l}", [P, 2, T])
                val = sb(rope, f"values_{l}", [P, 2, T])
                sync.wait(*[e.last for e in (pe, act, dve, pool)])
                load(f"cos_{l}", cos[:, :], dram["cos"])
                load(f"sin_{l}", sin[:, :], dram["sin"])
                rot_read = [None, None]
                qk_w = [None] * 16
                pending = {"do": None}

                def next_panel():
                    b, done = x_product(name)
                    if pending["do"]:
                        pending["do"]()
                    pending["do"] = None
                    return b, done

                def rotated_panel(i):
                    b, done = next_panel()
                    scale = HEAD ** -0.5 if i < 6 else 1.0
                    w = free_l[b] = dve.do(lambda e: e.scalar_tensor_tensor(
                        qk[:, i, :], bank_l[b][:, :], scale, rstd[:, :], ALU.mult, ALU.mult), done, state["rstd"])

                    def rest():
                        t, r = next_t(), i % 2
                        m = pe.do(lambda e: e.matmul(bank_t[t][:, :], rotate[:, :], qk[:, i, :],
                                                     start=True, stop=True), w, free_t[t], loads["rotate"])
                        free_t[t] = dve.do(lambda e: e.tensor_tensor(
                            rot[:, r, :], bank_t[t][:, :], sin[:, :], ALU.mult), m, rot_read[r], loads[f"sin_{l}"])
                        a = pool.do(lambda e: e.tensor_tensor(qk[:, i, :], qk[:, i, :], cos[:, :], ALU.mult),
                                    w, m, loads[f"cos_{l}"])
                        qk_w[i] = rot_read[r] = pool.do(lambda e: e.tensor_tensor(
                            qk[:, i, :], qk[:, i, :], rot[:, r, :], ALU.add), a, free_t[t])
                    pending["do"] = rest

                v_w = []

                def value_panel(i):
                    b, done = next_panel()
                    r = i % 2
                    w = free_l[b] = dve.do(lambda e: e.tensor_tensor(val[:, r, :], bank_l[b][:, :],
                                                                     rstd[:, :], ALU.mult),
                                           done, state["rstd"], val_read[r])

                    def rest():
                        t = next_t()
                        for blk in range(TB):
                            m = pe.do(lambda e, blk=blk: e.transpose(
                                bank_t[t][:, blk * P:(blk + 1) * P], val[:, r, blk * P:(blk + 1) * P], ident[:, :]),
                                w, free_t[t])
                        val_read[r] = m
                        free_t[t] = act.do(lambda e: e.activation(
                            v_tok[:, :, i * P:(i + 1) * P], bank_t[t][:, :].rearrange("p (b c) -> p b c", c=P),
                            ACT.Copy), m)
                        v_w.append(free_t[t])
                    pending["do"] = rest

                val_read = [None, None]
                for i in range(12):
                    rotated_panel(i)
                for i in range(6):
                    value_panel(i)
                for i in range(12, 16):
                    b, done = next_panel()
                    scale = HEAD ** -0.5 if i < 14 else 1.0
                    qk_w[i] = free_l[b] = dve.do(lambda e, b=b, i=i, s=scale: e.scalar_tensor_tensor(
                        qk[:, i, :], bank_l[b][:, :], s, rstd[:, :], ALU.mult, ALU.mult), done)
                for i in range(6, 8):
                    value_panel(i)
                pending["do"]()
                fence()
                rope.close()

                work = ExitStack()
                prob = sb(work, f"prob_{l}", [P, 2, 1280])
                prob_t = sb(work, f"prob_t_{l}", [P, 2, T])
                stat = sb(work, f"stat_{l}", [P, 2, 8])
                prob_read, pt_read = [None, None], [None, None]
                pt = {"n": 0}
                o_w = []
                gate_n = {"i": 0}

                def gate_panel():
                    i = gate_n["i"]
                    if i == 16:
                        return
                    gate_n["i"] += 1
                    b, done = x_product(name)
                    free_l[b] = gate_w[i] = dve.do(lambda e: e.tensor_tensor(
                        gates[:, i, :], bank_l[b][:, :], rstd[:, :], ALU.mult), done)

                gate_w = [None] * 16

                def dilated_scores(u, s, blk):
                    z, po = u % 2, 64 * (s % 2)
                    first = max(blk - 1, 0)
                    k0 = (first, 0, 0)
                    width = [(blk + 1 - k) * P for k in k0]
                    for g in range(3):
                        ch = (g * SLOTS + s) // 2
                        pe.run(lambda e, g=g: e.matmul(
                            bank_s[:, g, 0:width[g]], ident_bf[:, :], masks_f[:, MASK_END[g] - width[g]:MASK_END[g]],
                            start=True, stop=False), free_s[g], ident_bf_ready, loads["masks"])
                        m = pe.do(lambda e, g=g, ch=ch: e.matmul(
                            bank_s[:, g, 0:width[g]], qk[po:po + 64, ch, blk * P:(blk + 1) * P],
                            qk[po:po + 64, 6 + ch, k0[g] * P:(blk + 1) * P], start=False, stop=True),
                            qk_w[ch], qk_w[6 + ch])
                    w0, w1 = width[0], width[1]
                    st = stat[:, z, :]
                    r1 = dve.do(lambda e: e.tensor_reduce(st[:, 0:1], bank_s[:, 0, 0:w0], AX, ALU.max),
                                m)
                    r2 = dve.do(lambda e: e.tensor_reduce(st[:, 1:3], bank_s[:, 1:3, 0:w1], AX, ALU.max), m)
                    r = dve.do(lambda e: e.tensor_reduce(st[:, 3:4], st[:, 0:3], AX, ALU.max), r1, r2)
                    r = dve.do(lambda e: e.tensor_scalar(st[:, 4:5], st[:, 3:4], -1.0, None, ALU.mult), r)
                    a1 = act.do(lambda e: e.activation(prob[:, z, 0:w0], bank_s[:, 0, 0:w0], ACT.Exp,
                                                       bias=st[:, 4:5], accum_out=st[:, 5:6]), r, prob_read[z])
                    a2 = act.do(lambda e: e.activation(
                        prob[:, z, w0:w0 + 2 * w1].rearrange("p (g k) -> p g k", g=2), bank_s[:, 1:3, 0:w1],
                        ACT.Exp, bias=st[:, 4:5], accum_out=st[:, 6:7]), r)
                    free_s[0] = [a1]
                    free_s[1] = free_s[2] = [a2]
                    r = dve.do(lambda e: e.tensor_tensor(st[:, 7:8], st[:, 5:6], st[:, 6:7], ALU.add), a1, a2)
                    r = dve.do(lambda e: e.reciprocal(st[:, 7:8], st[:, 7:8]), r)
                    return dve.do(lambda e: e.tensor_scalar(prob[:, z, 0:w0 + 2 * w1], prob[:, z, 0:w0 + 2 * w1],
                                                            st[:, 7:8], None, ALU.mult), r)

                pending_values = {"do": None}

                def dilated_values(u, s, blk, prob_w):
                    z, po = u % 2, 64 * (s % 2)
                    first = max(blk - 1, 0)
                    w0 = (blk + 1 - first) * P
                    batches = [(1, 0, w0), (2, 0, w0 + (blk + 1) * P), (0, first, 0)]
                    for g, k0, at in batches:
                        t, nb, y = next_t(), blk + 1 - k0, pt["n"] % 2
                        pt["n"] += 1
                        for j in range(nb):
                            m = pe.do(lambda e, t=t, j=j, a=at: e.transpose(
                                bank_t[t][:, j * P:(j + 1) * P], prob[:, z, a + j * P:a + (j + 1) * P],
                                ident[:, :]), prob_w, free_t[t])
                        prob_read[z] = m
                        if pending_values["do"]:
                            pending_values["do"]()
                        if g == 1:
                            w = act.do(lambda e, t=t, y=y, nb=nb: e.activation(
                                prob_t[:, y, 0:nb * P], bank_t[t][:, 0:nb * P], ACT.Copy), m, pt_read[y])
                        else:
                            w = dve.do(lambda e, t=t, y=y, nb=nb: e.tensor_copy(
                                prob_t[:, y, 0:nb * P], bank_t[t][:, 0:nb * P]), m, pt_read[y])
                        free_t[t] = w

                        def rest(g=g, k0=k0, nb=nb, y=y, w=w):
                            head = (g * SLOTS + s) * HEAD
                            for j in range(nb):
                                m2 = pe.do(lambda e, j=j: e.matmul(
                                    bank_o[po:po + 64, 0:P], v_tok[:, k0 + j, head:head + HEAD],
                                    prob_t[:, y, j * P:(j + 1) * P], start=(g == 1 and j == 0),
                                    stop=(g == 0 and j == nb - 1)), w, v_w, free_o[0])
                            pt_read[y] = m2
                            if g == 0:
                                free_o[0] = dve.do(lambda e: e.tensor_copy(
                                    o_f[po:po + 64, s // 2, blk * P:(blk + 1) * P], bank_o[po:po + 64, 0:P]), m2)
                                o_w.append(free_o[0])
                        pending_values["do"] = rest

                units = [(s, blk) for blk in range(TB) for s in range(SLOTS)]
                marks = {}
                for u in range(len(units) + 1):
                    if u < len(units):
                        marks[u] = dilated_scores(u, *units[u])
                        if u < 12:
                            gate_panel()
                    if u:
                        dilated_values(u - 1, *units[u - 1], marks[u - 1])

                pending_values["do"]()
                place = [(0, 0), (1, 0), (2, 0), (1, 384)]
                flat = [0, 512, 1024, 896]

                def stick_scores(h):
                    z, po, ch = h % 2, 64 * (h % 2), h // 2
                    for kb in range(TB):
                        bk, c0 = place[kb]
                        w = T - kb * P
                        m = pe.do(lambda e, bk=bk, c0=c0, w=w, kb=kb: e.matmul(
                            bank_s[:, bk, c0:c0 + w], qk[po:po + 64, 14 + ch, kb * P:(kb + 1) * P],
                            qk[po:po + 64, 12 + ch, kb * P:T], start=(c0 == 0), stop=False,
                            skip_group_check=True), qk_w[12 + ch], qk_w[14 + ch], free_s[bk])
                    sizes = (512, 512, 256)
                    for bk, n in enumerate(sizes):
                        a = act.do(lambda e, bk=bk, n=n: e.activation(
                            prob[:, z, bk * 512:bk * 512 + n], bank_s[:, bk, 0:n], ACT.Abs), m, prob_read[z])
                    a = act.do(lambda e: e.activation(prob[:, z, :], prob[:, z, :], ACT.Exp, scale=-1.0), a)
                    a = act.do(lambda e: e.activation(prob[:, z, :], prob[:, z, :], ACT.Ln, bias=1.0), a)
                    done = []
                    for bk, n in enumerate(sizes):
                        done.append(dve.do(lambda e, bk=bk, n=n: e.scalar_tensor_tensor(
                            prob[:, z, bk * 512:bk * 512 + n], bank_s[:, bk, 0:n], 0.0,
                            prob[:, z, bk * 512:bk * 512 + n], ALU.max, ALU.add), a))
                    for kb in range(TB):
                        done.append(dve.do(lambda e, f=flat[kb]: e.tensor_tensor(
                            prob[:, z, f:f + P], prob[:, z, f:f + P], strict[:, :], ALU.mult),
                            done[0:3], loads["strict"]))
                    return done

                def stick_weights(h, nlk):
                    z = h % 2
                    for kb in range(TB):
                        bk, c0 = place[kb]
                        w = T - kb * P
                        pe.run(lambda e, bk=bk, c0=c0: e.matmul(
                            bank_s[:, bk, c0:c0 + P], ident_bf[:, :], masks_f[:, 10 * P:11 * P],
                            start=False, stop=False, skip_group_check=True), nlk)
                        pe.run(lambda e, bk=bk, c0=c0, w=w, f=flat[kb]: e.matmul(
                            bank_s[:, bk, c0:c0 + w], suffix[:, :], prob[:, z, f:f + w],
                            start=False, stop=False, skip_group_check=True), loads["suffix"], loads["minus"])
                        for k2 in range(kb + 1, TB):
                            w2, f2 = T - k2 * P, flat[k2]
                            c2 = c0 + (k2 - kb) * P
                            pe.run(lambda e, bk=bk, c=c2, w=w2, f=f2: e.matmul(
                                bank_s[:, bk, c:c + w], minus[:, :], prob[:, z, f:f + w],
                                start=False, stop=False, skip_group_check=True))
                    m = pe.do(lambda e: e.matmul(bank_s[:, 2, 0:1], ident_bf[:, :], masks_f[:, 0:1], start=False,
                                                 stop=True, skip_group_check=True))
                    for bk, n in enumerate((512, 512, 256)):
                        a = act.do(lambda e, bk=bk, n=n: e.activation(
                            prob[:, z, bk * 512:bk * 512 + n], bank_s[:, bk, 0:n], ACT.Exp), m)
                        free_s[bk] = a
                    return a

                def stick_values(h, weights):
                    z, po = h % 2, 64 * (h % 2)
                    for kb in range(TB):
                        f, w = flat[kb], T - kb * P
                        m = pe.do(lambda e, kb=kb, f=f, w=w: e.matmul(
                            bank_o[po:po + 64, kb * P:T], v_tok[:, kb, 768 + h * HEAD:768 + (h + 1) * HEAD],
                            prob[:, z, f:f + w], start=(kb == 0), stop=(kb == TB - 1),
                            skip_group_check=True), weights, free_o[0], v_w)
                    prob_read[z] = m
                    free_o[0] = dve.do(lambda e: e.tensor_copy(o_f[po:po + 64, 2 + h // 2, :],
                                                               bank_o[po:po + 64, :]), m)
                    o_w.append(free_o[0])

                prev = None
                for h in range(4):
                    nlk = stick_scores(h)
                    gate_panel()
                    if prev:
                        stick_values(*prev)
                    prev = (h, stick_weights(h, nlk))
                stick_values(*prev)
                fence()
                work.close()
                att.close()

                o_hi = sb(phase, f"o_hi_{l}", [P, 4, T], F32R)
                o_lo = sb(phase, f"o_lo_{l}", [P, 4, T], F32R)
                y_hi = sb(phase, f"y_hi_{l}", [P, DC, T], F32R)
                y_lo = sb(phase, f"y_lo_{l}", [P, DC, T], F32R)
                part = sb(phase, f"part_{l}", [P, 2, 2, T])
                o_ready = [split_value(o_hi[:, c, :], o_lo[:, c, :], o_f[:, c, :], o_w) for c in range(4)]
                part_read = [None, None]
                y_w = [None] * DC

                def split_y(m, w):
                    y_w[m] = part_read[m % 2] = split_value(y_hi[:, m, :], y_lo[:, m, :], part[:, m % 2, 0, :], w)

                for m in range(DC):
                    for f in range(2):
                        sg = act.do(lambda e, i=8 * f + m: e.activation(gates[:, i, :], gates[:, i, :], ACT.Sigmoid),
                                    gate_w[8 * f + m])
                        b = next_l()
                        done = product(f"proj_{('dil', 'sb')[f]}_{l}", lambda c, f=f: o_hi[:, 2 * f + c, :],
                                       lambda c, f=f: o_lo[:, 2 * f + c, :], bank_l[b][:, :],
                                       o_ready[2 * f:2 * f + 2], free_l[b])
                        z = m % 2
                        free_l[b] = dve.do(lambda e, b=b, z=z, f=f, i=8 * f + m: e.tensor_tensor(
                            part[:, z, f, :], bank_l[b][:, :], gates[:, i, :], ALU.mult),
                            done, sg, part_read[z])
                    w = pool.do(lambda e, z=z: e.tensor_tensor(part[:, z, 0, :], part[:, z, 0, :],
                                                               part[:, z, 1, :], ALU.add), dve.last)
                    if m:
                        split_y(m - 1, summed)
                    summed = w
                split_y(DC - 1, summed)
                for m in range(DC):
                    b = next_l()
                    done = product(f"out_{l}", lambda c: y_hi[:, c, :], lambda c: y_lo[:, c, :],
                                   bank_l[b][:, :], y_w, free_l[b])
                    add_to_x(m, b, done, 1.0, g_out)
                token_rstd()

        mixer_1()
        router()
        feed_forward("moe", "moe_gate", "moe_up", "moe_down", (8,) * 4, 1.0, None, expert_scales)
        normalise(2, 3)
        for l in range(DEPTH_2):
            feed_forward(f"ff1_{l}", f"ff1_gate_{l}", f"ff1_up_{l}", f"ff1_down_{l}", FF_GROUPS, 0.5, 4 + 3 * l)
            mixer_2(l)
            last = l == DEPTH_2 - 1
            feed_forward(f"ff2_{l}", f"ff2_gate_{l}", f"ff2_up_{l}", f"ff2_down_{l}", FF_GROUPS, 0.5,
                         None if last else 3 + 3 * (l + 1))
        normalise(3 + 3 * DEPTH_2, store=True)
        sync.wait((stored, 16 * DC))

        block = stack.enter_context(nc.Block())

        def body(engine):
            def emit(e):
                for op in engine.ops:
                    op(e)
            return emit
        block.sync(body(sync))
        block.scalar(body(act))
        block.gpsimd(body(pool))
        block.vector(body(dve))
        block.tensor(body(pe))


def constants():
    i = np.arange(P)
    causal = i[:, None] >= i[None, :]
    masks = []
    for w, d in zip(WINDOWS, DILATIONS):
        near = (i[:, None] - i[None, :]) % d == 0
        diag = near & causal
        far = near & (i[:, None] + P - i[None, :] <= w) if w == P else near
        masks += [far] * (1 if w == P else 3) + [diag]
    masks.append(i[:, None] < i[None, :])
    masks = np.where(np.concatenate(masks, 1), 0.0, MASKED)
    pos = np.arange(T, dtype=np.float32)
    inv = np.float32(ROPE_THETA) ** (-np.arange(0, ROPE_DIM, 2, dtype=np.float32) / np.float32(ROPE_DIM))
    ang = (pos[:, None] * inv[None, :]).astype(np.float32)
    half = ROPE_DIM // 2
    cos, sin = np.ones((P, T), np.float32), np.zeros((P, T), np.float32)
    rotate = np.zeros((P, P), np.float32)
    for h in range(0, P, HEAD):
        cos[h:h + half] = cos[h + half:h + ROPE_DIM] = np.cos(ang).T
        sin[h:h + half], sin[h + half:h + ROPE_DIM] = -np.sin(ang).T, np.sin(ang).T
        for a in range(half):
            rotate[h + a, h + half + a] = rotate[h + half + a, h + a] = 1.0
    resets = np.ones((P, META + T), np.float32)
    resets[:, META::CHUNK] = 0.0
    same = (i[:, None] // CHUNK) == (i[None, :] // CHUNK)
    gla_mask = np.tile((same & (i[:, None] <= i[None, :])).astype(np.int32), (1, TB))
    picks = np.zeros((N_EXPERTS, N_EXPERTS, P), np.float32)
    picks[np.arange(N_EXPERTS), np.arange(N_EXPERTS)] = 1.0
    return {
        "ident": np.eye(P, dtype=np.float32), "ones": np.ones((P, P), np.float32),
        "rotate": rotate, "cos": cos, "sin": sin,
        "suffix": np.where(i[:, None] >= i[None, :], -1.0, 0.0).astype(np.float32),
        "minus": np.full((P, P), -1.0, np.float32),
        "strict": (i[:, None] < i[None, :]).astype(np.float32),
        "masks": masks, "resets": resets, "gla_mask": gla_mask, "picks": picks,
        "rank": np.broadcast_to(np.arange(4, 0, -1, dtype=np.float32), (P, TB, 4)).copy(),
    }


def kernel(**a):
    import ml_dtypes
    import concourse.bacc as bacc
    from concourse.bass_utils import run_bass_kernel_spmd

    a = {k: np.asarray(v) for k, v in a.items()}

    def chunks(v):
        return v.reshape(-1, P).T

    def feature_major(v):
        return np.ascontiguousarray(v.T.reshape(DC, P, -1).transpose(1, 0, 2))

    def padded(w):
        return np.pad(w, ((0, 0), (0, P - w.shape[1])))

    w_in = a["w_in"][0]
    source = {
        "pool": w_in[:, 0:512], "q": w_in[:, 512:768], "k": w_in[:, 768:1024], "v": w_in[:, 1024:1536],
        "r": w_in[:, 1536:2048], "g": padded(w_in[:, 2048:2064]), "out": a["w_out"][0],
        "route": padded(np.concatenate([a["w_router_group"][0], a["w_router_expert"][0]], 1)),
        "moe_gate": a["w_expert_gate"][0].transpose(1, 0, 2).reshape(D, 4096),
        "moe_up": a["w_expert_up"][0].transpose(1, 0, 2).reshape(D, 4096),
        "moe_down": a["w_expert_down"][0].reshape(4096, D),
    }
    for l in range(DEPTH_2):
        for f in (1, 2):
            for part in ("gate", "up", "down"):
                source[f"ff{f}_{part}_{l}"] = a[f"ffn{f}_w_{part}_2"][l]
        source[f"in_{l}"] = a["w_in_2"][l]
        source[f"proj_dil_{l}"] = a["w_proj_dil_2"][l]
        source[f"proj_sb_{l}"] = a["w_proj_sb_2"][l]
        source[f"out_{l}"] = a["w_out_2"][l]
    arrays = {}
    for name, panels in weight_matrices().items():
        w = source[name]
        arrays[name] = np.concatenate([
            w[r:r + rows, c:c + cols].reshape(rows // P, P, cols).transpose(1, 0, 2).ravel()
            for r, rows, c, cols in panels])
    gains = [a["norm_mix_w"][0], a["norm_ffn_w"][0], a["final_norm_w"]]
    for l in range(DEPTH_2):
        gains += [a["norm_ffn1_2"][l], a["norm_mix_2"][l], a["norm_ffn2_2"][l]]
    gains.append(a["norm_final_2"])
    arrays.update(constants())
    arrays["masks"] = arrays["masks"].astype(ml_dtypes.bfloat16)
    arrays.update({
        "x_t": feature_major(a["x"][0]), "meta_t": feature_major(a["meta_tokens"]),
        "gains": np.ascontiguousarray(np.concatenate([chunks(g) for g in gains], 1)),
        "w_gate_up": a["w_gate_up"][0],
        "vecs": np.ascontiguousarray(np.concatenate(
            [chunks(a["b_gate"][0]), chunks(a["pool_scale"][0]), chunks(a["gla_norm_w"][0])], 1)),
        "pool_w": np.ascontiguousarray(a["pool_w"][0].transpose(1, 0, 2)),
        "router_bias": np.concatenate([a["b_router_group"][0], a["b_router_expert"][0]])[:, None].copy(),
    })

    nc = bacc.Bacc("TRN2", target_bir_lowering=False, num_devices=1)
    dram = {n: nc.dram_tensor(f"in_{n}", v.shape, mybir.dt.from_np(v.dtype), kind="ExternalInput").ap()
            for n, v in arrays.items()}
    out = nc.dram_tensor("out_t", (P, DC, T), F32, kind="ExternalOutput").ap()
    build(nc, dram, out)
    r = run_bass_kernel_spmd(nc, [{f"in_{n}": v for n, v in arrays.items()}], core_ids=[0])
    got = r.results[0]["out_t"]
    return got.transpose(2, 1, 0).reshape(1, T, D)
```

```python
from contextlib import ExitStack

import numpy as np

import concourse.bass as bass
from concourse import mybir

F32 = mybir.dt.float32
F32R = mybir.dt.float32r
BF16 = mybir.dt.bfloat16
I32 = mybir.dt.int32
U32 = mybir.dt.uint32
ALU = mybir.AluOpType
ACT = mybir.ActivationFunctionType
AX = mybir.AxisListType.X

P = 128
T = 512
D = 1024
DC = D // P
TB = T // P
META = 16
L = META + T
POOL_WINDOWS = (2, 4, 8, 16)
GATE_RANK = 16
GLA_HEADS, GLA_K, GLA_V, CHUNK = 4, 64, 128, 64
N_CHUNK = T // CHUNK
N_GROUPS, PER_GROUP = 4, 4
N_EXPERTS = N_GROUPS * PER_GROUP
ROUTES = N_GROUPS + N_EXPERTS
TOP_K = 2
EXPERT_HIDDEN = D // 4
OVERFLOW = (T * TOP_K) // (P + 1)
TILES = N_EXPERTS + OVERFLOW
GU_PANELS = 4
TILE_PANELS = GU_PANELS + EXPERT_HIDDEN // P
EPS = 1e-6
DEPTH_2 = 2
HEAD = 64
SLOTS = 4
DILATIONS = (1, 4, 16)
WINDOWS = (128, 512, 2048)
ROPE_DIM = HEAD // 4
ROPE_THETA = 500000.0
D_FF = 2816
FF_GROUPS = (8, 8, 6)
MASKED = -1e30

RAW = 3
SPLIT = 3
AHEAD = 2
EXPERT_OWN = 16
EXPERT_RAW = EXPERT_OWN + RAW
PANEL = DC * P


def matrix_panels(rows, cols, k_groups=None, width=P):
    out, r = [], 0
    for kc in k_groups or (rows // P,):
        for c in range(0, cols, width):
            out.append((r, kc * P, c, min(width, cols - c)))
        r += kc * P
    return out


def weight_matrices():
    m = {
        "pool": matrix_panels(D, 512), "q": matrix_panels(D, 256), "k": matrix_panels(D, 256),
        "v": matrix_panels(D, 512), "r": matrix_panels(D, 512), "g": matrix_panels(D, P),
        "out": matrix_panels(D, D), "route": matrix_panels(D, P),
    }
    for l in range(DEPTH_2):
        for f in (1, 2):
            m[f"ff{f}_gate_{l}"] = matrix_panels(D, D_FF)
            m[f"ff{f}_up_{l}"] = matrix_panels(D, D_FF)
            m[f"ff{f}_down_{l}"] = matrix_panels(D_FF, D, FF_GROUPS)
        m[f"in_{l}"] = matrix_panels(D, 5120)
        m[f"proj_dil_{l}"] = matrix_panels(256, D)
        m[f"proj_sb_{l}"] = matrix_panels(256, D)
        m[f"out_{l}"] = matrix_panels(D, D)
    return m


def ffn_order(gate, up, down, groups):
    out, j = [], 0
    for g, n in enumerate(groups):
        for i in range(n):
            out += [(gate, j), (up, j)]
            j += 1
        out += [(down, g * DC + m) for m in range(DC)]
    return out


def weight_order():
    o = [("g", 0)] + [("k", i) for i in range(2)] + [("v", i) for i in range(4)]
    o += [("q", i) for i in range(2)]
    for i in range(4):
        o += [("pool", i), ("r", i)]
    o += [("out", i) for i in range(DC)]
    o += [("route", 0)]
    for i in range(N_EXPERTS + 1):
        o += [("experts", (i, j)) for j in range(GU_PANELS) if i < N_EXPERTS]
        o += [("experts", (i - 1, j)) for j in range(GU_PANELS, TILE_PANELS) if i]
    for l in range(DEPTH_2):
        o += ffn_order(f"ff1_gate_{l}", f"ff1_up_{l}", f"ff1_down_{l}", FF_GROUPS)
        o += [(f"in_{l}", i) for i in (*range(18), 22, 23, *range(18, 22), *range(24, 40))]
        for m in range(DC):
            o += [(f"proj_dil_{l}", m), (f"proj_sb_{l}", m)]
        o += [(f"out_{l}", m) for m in range(DC)]
        o += ffn_order(f"ff2_gate_{l}", f"ff2_up_{l}", f"ff2_down_{l}", FF_GROUPS)
    return o


class Engine:

    def __init__(self, sem):
        self.sem, self.count, self.ops, self.reached = sem, 0, [], {}
        self.last = None

    def wait(self, *marks):
        for m in marks:
            if m is None:
                continue
            if isinstance(m, list):
                self.wait(*m)
                continue
            sem, value = m
            if self.reached.get(id(sem), 0) < value:
                self.reached[id(sem)] = value
                self.ops.append(lambda e, s=sem, v=value: e.wait_ge(s, v))

    def run(self, make, *marks):
        self.wait(*marks)
        self.ops.append(make)

    def do(self, make, *marks):
        self.wait(*marks)
        self.count += 1
        self.ops.append(lambda e: make(e).then_inc(self.sem, 1))
        self.last = (self.sem, self.count)
        return self.last

    def only_if(self, condition, others):
        def emit(e):
            with e.If(condition(e)):
                for op in others.ops:
                    op(e)
        self.ops.append(emit)


def build(nc, dram, out):
    matrices, order = weight_matrices(), weight_order()
    stack = ExitStack()
    with stack:
        def sb(where, name, shape, dt=F32):
            return where.enter_context(nc.sbuf_tensor(name, shape, dt))

        def sem(name):
            return stack.enter_context(nc.semaphore(name))

        pe, act, dve, pool = (Engine(sem(f"{n}_done")) for n in ("pe", "act", "dve", "pool"))
        sync = Engine(None)

        bank_l = [stack.enter_context(nc.psum_tensor(f"bank_l{i}", [P, 512], F32)) for i in range(2)]
        bank_s = stack.enter_context(nc.psum_tensor("bank_s", [P, 3, 512], F32))
        bank_t = [stack.enter_context(nc.psum_tensor(f"bank_t{i}", [P, 512], F32)) for i in range(2)]
        bank_o = stack.enter_context(nc.psum_tensor("bank_o", [P, 512], F32))
        free_l, free_s, free_t, free_o = [[], []], [[], [], []], [[], []], [[]]

        x = sb(stack, "x", [P, DC, T])
        xg_hi = sb(stack, "xg_hi", [P, DC, L], F32R)
        xg_lo = sb(stack, "xg_lo", [P, DC, L], F32R)
        rstd = sb(stack, "rstd", [P, T])
        squares = sb(stack, "squares", [P, 2, T])
        square_sum = sb(stack, "square_sum", [P, T])
        w_raw = sb(stack, "w_raw", [P, RAW, PANEL])
        w_hi = sb(stack, "w_hi", [P, SPLIT, PANEL], F32R)
        w_lo = sb(stack, "w_lo", [P, SPLIT, PANEL], F32R)
        n_gain = 3 + 3 * DEPTH_2 + 1
        gains = sb(stack, "gains", [P, n_gain * DC])
        ident = sb(stack, "ident", [P, P])
        ident_bf = sb(stack, "ident_bf", [P, P], BF16)
        ones = sb(stack, "ones", [P, P])
        strict = sb(stack, "strict", [P, P])

        loads = {}
        late_loads = []

        def load(name, dst, src, late=False, queue=None):
            s = sem(f"load_{name}")
            ops = late_loads if late else (queue or sync).ops
            ops.append(lambda e: e.dma_start(dst, src).then_inc(s, 16))
            loads[name] = (s, 16)
            return loads[name]

        load("gains", gains[:, :], dram["gains"])
        load("ident", ident[:, :], dram["ident"], late=True)
        load("strict", strict[:, :], dram["strict"], late=True)

        def gain(g, c):
            return gains[:, g * DC + c:g * DC + c + 1]

        raw_arrived = [sem(f"raw_arrived{i}") for i in range(RAW)]
        raw_split = [None] * RAW
        slot_used = [None] * SPLIT
        split_ready = {}
        stream = {"split": 0, "next": 0}
        experts_ring = {"memory": None, "issued": 0, "open": False}
        expert_arrived = [sem(f"expert_arrived{i}") for i in range(EXPERT_RAW)]
        expert_split = [None] * EXPERT_RAW
        expert_panels = [i for i in range(len(order)) if order[i][0] == "experts"]
        ring_turn, n = {}, 0
        for i in range(len(order)):
            if order[i][0] != "experts":
                ring_turn[i], n = n, n + 1
        ring_turn.update({i: k for k, i in enumerate(expert_panels)})

        def expert_slot(slot):
            if slot < EXPERT_OWN:
                return experts_ring["memory"][:, slot, :]
            return w_raw[:, slot - EXPERT_OWN, :]

        def load_expert_panel(k, *marks):
            slot = k % EXPERT_RAW
            if k < EXPERT_RAW and slot >= EXPERT_OWN:
                sync.wait(raw_split[slot - EXPERT_OWN])
            sync.wait(expert_split[slot], *marks)
            memory = expert_slot(slot)
            sync.ops.append(lambda e: e.dma_start(
                memory, dram["experts"][order[expert_panels[k]][1]]).then_inc(expert_arrived[slot], 16))
            experts_ring["issued"] = k + 1
            return expert_arrived[slot], 16 * (k // EXPERT_RAW + 1)

        def panel_shape(i):
            name, j = order[i]
            r, rows, c, cols = matrices[name][j]
            return rows // P, cols

        def split_panel():
            i = stream["split"]
            if i == len(order):
                return
            stream["split"] += 1
            name, j = order[i]
            slot, at_turn = i % SPLIT, ring_turn[i]
            if name == "experts":
                n, raw, splits = PANEL, at_turn % EXPERT_RAW, expert_split
                value = expert_slot(raw)
                if at_turn >= experts_ring["issued"]:
                    load_expert_panel(at_turn)
                arrived = (expert_arrived[raw], 16 * (at_turn // EXPERT_RAW + 1))
            else:
                kc, cols = panel_shape(i)
                n, raw, splits = kc * cols, at_turn % RAW, raw_split
                value = w_raw[:, raw, 0:n]
                at = sum(p[1] * p[3] for p in matrices[name][:j])
                src = dram[name][at:at + P * n].rearrange("(p w) -> p w", p=P)
                sync.wait(raw_split[raw])
                sync.ops.append(lambda e: e.dma_start(value, src).then_inc(raw_arrived[raw], 16))
                arrived = (raw_arrived[raw], 16 * (at_turn // RAW + 1))
            rounded = act.do(lambda e: e.activation(w_hi[:, slot, 0:n], value, ACT.Copy),
                             arrived, slot_used[slot], split_ready.get(i - SPLIT))
            split_ready[i] = dve.do(
                lambda e: e.tensor_tensor(w_lo[:, slot, 0:n], value, w_hi[:, slot, 0:n].bitcast(F32),
                                          ALU.subtract),
                arrived, rounded, slot_used[slot])
            splits[raw] = split_ready[i]
            if name == "experts" and raw >= EXPERT_OWN:
                raw_split[raw - EXPERT_OWN] = split_ready[i]

        def split_ahead(i):
            while stream["split"] <= min(i + AHEAD, len(order) - 1) and (
                    order[stream["split"]][0] != "experts" or experts_ring["open"]):
                split_panel()

        def product(name, hi, lo, outs, ready, bank_free):
            i = stream["next"]
            assert order[i][0] == name, (order[i], name)
            stream["next"] += 1
            split_ahead(i)
            kc, cols = panel_shape(i)
            slot = i % SPLIT
            pe.wait(split_ready[i])
            pe.wait(bank_free)
            parts = [(w_hi, 0), (w_hi, 1), (w_lo, 0)]
            for c in range(kc):
                pe.wait(ready[c] if ready else None)
                for n, (w, part) in enumerate(parts):
                    lhs = w[:, slot, c * cols:(c + 1) * cols]
                    for dst, src_hi, src_lo in [(outs, hi, lo)] if not isinstance(outs, list) else [
                            (o, h, g) for o, h, g in zip(outs, hi, lo)]:
                        src = (src_hi if part == 0 else src_lo)(c)
                        first, last = c == 0 and n == 0, c == kc - 1 and n == 2
                        op = (lambda e, d=dst, a=lhs, b=src, f=first, z=last:
                              e.matmul(d, a, b, start=f, stop=z))
                        if last and (not isinstance(outs, list) or dst is outs[-1]):
                            done = pe.do(op)
                        else:
                            pe.run(op)
            slot_used[slot] = done
            return done

        turn = {"l": 0, "t": 0, "s": 0}

        def next_l():
            turn["l"] ^= 1
            return turn["l"]

        def next_t():
            turn["t"] ^= 1
            return turn["t"]

        xg_ready = [None] * DC
        x_written = [None] * DC
        x_read = [None] * DC
        state = {"xg_used": None, "sum_used": None, "rstd": None, "owed": None, "rstd_read": None}
        square_read = [None, None]
        sum_mark = [None]

        def fence():
            marks = [e.last for e in (pe, act, dve, pool)]
            for e in (act, dve, pool):
                e.wait(*marks)

        def x_product(name, bank=None):
            b = next_l() if bank is None else bank
            kc, cols = panel_shape(stream["next"])
            done = product(name, lambda c: xg_hi[:, c, META:], lambda c: xg_lo[:, c, META:],
                           bank_l[b][0:cols, :], xg_ready, free_l[b])
            state["xg_used"] = done
            settle()
            return b, done

        def settle():
            if state["owed"]:
                owed, state["owed"] = state["owed"], None
                owed()

        def add_square(c, written):
            if c == 0:
                sum_mark[0] = act.do(lambda e: e.activation(square_sum[:, :], x[:, 0, :], ACT.Square),
                                     written, state["sum_used"], sum_mark[0])
                x_read[0] = [sum_mark[0]]
                return
            half = c % 2
            squared = act.do(lambda e: e.activation(squares[:, half, :], x[:, c, :], ACT.Square),
                             written, square_read[half])
            sum_mark[0] = dve.do(lambda e: e.tensor_tensor(square_sum[:, :], square_sum[:, :],
                                                           squares[:, half, :], ALU.add),
                                 squared, sum_mark[0])
            square_read[half] = sum_mark[0]
            x_read[c] = [squared]

        def split_x(c, g, written):
            rounded = act.do(lambda e: e.activation(xg_hi[:, c, META:], x[:, c, :], ACT.Copy, scale=gain(g, c)),
                             written, state["xg_used"], xg_ready[c], loads["gains"])
            xg_ready[c] = dve.do(
                lambda e: e.scalar_tensor_tensor(xg_lo[:, c, META:], x[:, c, :], gain(g, c),
                                                 xg_hi[:, c, META:].bitcast(F32), ALU.mult, ALU.subtract),
                written, rounded, state["xg_used"], loads["gains"])
            x_read[c] = (x_read[c] or []) + [rounded, xg_ready[c]]

        def token_rstd():
            summed = pe.do(lambda e: e.matmul(bank_o[:, :], ones[:, :], square_sum[:, :],
                                              start=True, stop=True),
                           sum_mark[0], free_o[0], loads["ones"])
            state["sum_used"] = summed
            logged = act.do(lambda e: e.activation(rstd[:, :], bank_o[:, :], ACT.Ln,
                                                   scale=1.0 / D, bias=eps_col[:, 0:1]),
                            summed, state["rstd_read"] or dve.last, eps_ready)
            state["rstd_read"] = None
            free_o[0] = logged
            state["rstd"] = act.do(lambda e: e.activation(rstd[:, :], rstd[:, :], ACT.Exp, scale=-0.5), logged)

        eps_col = sb(stack, "eps_col", [P, 1])
        eps_ready = dve.do(lambda e: e.memset(eps_col[:, :], EPS))

        def add_to_x(c, bank, done, factor, g=None, stats=True):
            written = dve.do(
                lambda e: e.scalar_tensor_tensor(x[:, c, :], bank_l[bank][:, :], factor, x[:, c, :],
                                                 ALU.mult, ALU.add),
                done, x_read[c], x_written[c])
            free_l[bank] = written
            x_written[c] = written
            x_read[c] = None
            if stats:
                add_square(c, written)
            if g is not None:
                split_x(c, g, written)

        def split_value(hi, lo, value, marks, free=None):
            rounded = act.do(lambda e: e.activation(hi, value, ACT.Copy), marks, free)
            return dve.do(lambda e: e.tensor_tensor(lo, value, hi.bitcast(F32), ALU.subtract), rounded, free)

        def feed_forward(tag, gate, up, down, groups, factor, g):
            fence()
            with ExitStack() as phase:
                hid_hi = sb(phase, f"hid_hi_{tag}", [P, 8, T], F32R)
                hid_lo = sb(phase, f"hid_lo_{tag}", [P, 8, T], F32R)
                gated = sb(phase, f"gated_{tag}", [P, 2, T])
                silu = sb(phase, f"silu_{tag}", [P, 2, T])
                val = sb(phase, f"val_{tag}", [P, 2, T])
                hid_used, j = None, 0
                silu_read, val_read, gated_read = [None] * 2, [None] * 2, [None] * 2
                val_written = [None] * 2
                silu_w, gated_w = [None] * 2, [None] * 2
                for n_group, n in enumerate(groups):
                    hid_ready = [None] * n
                    for i in range(n):
                        h = j % 2
                        bg, gate_done = x_product(gate)
                        gated_w[h] = dve.do(lambda e, h=h, b=bg: e.tensor_tensor(
                            gated[:, h, :], bank_l[b][:, :], rstd[:, :], ALU.mult),
                            gate_done, state["rstd"], gated_read[h])
                        free_l[bg] = gated_w[h]
                        silu_w[h] = act.do(lambda e, h=h: e.activation(silu[:, h, :], gated[:, h, :], ACT.Silu),
                                           gated_w[h], silu_read[h])
                        gated_read[h] = silu_w[h]
                        bu, up_done = x_product(up)
                        product_w = dve.do(lambda e, h=h, b=bu: e.tensor_tensor(
                            val[:, h, :], bank_l[b][:, :], silu[:, h, :], ALU.mult),
                            up_done, silu_w[h], val_read[h])
                        free_l[bu] = product_w
                        silu_read[h] = product_w
                        val_w = dve.do(lambda e, h=h: e.tensor_tensor(
                            val[:, h, :], val[:, h, :], rstd[:, :], ALU.mult), product_w)
                        hid_ready[i] = split_value(hid_hi[:, i, :], hid_lo[:, i, :], val[:, h, :],
                                                   val_w, hid_used)
                        val_read[h] = hid_ready[i]
                        j += 1
                    last = n_group == len(groups) - 1
                    for m in range(DC):
                        b = next_l()
                        hid_used = product(down, lambda c: hid_hi[:, c, :], lambda c: hid_lo[:, c, :],
                                           bank_l[b][:, :], hid_ready, free_l[b])
                        add_to_x(m, b, hid_used, factor, g if last else None, last)
                        if last and m == DC - 1:
                            state["owed"], state["rstd_read"] = token_rstd, dve.last

        def transpose_to(dst, src, n_out, n_in, t, at, marks):
            return pe.do(lambda e: e.transpose(bank_t[t][0:n_out, at:at + n_in], src, ident[0:n_in, 0:n_in]),
                         marks, loads["ident"])

        def mixer_1():
            with ExitStack() as phase:
                meta = sb(phase, "meta", [P, DC, META])
                meta_sq = sb(phase, "meta_sq", [P, DC, META])
                meta_sum = sb(phase, "meta_sum", [P, META])
                all_rstd = sb(phase, "all_rstd", [P, L])
                meta_g = sb(phase, "meta_g", [P, DC, META])
                gate_up = sb(phase, "gate_up", [GATE_RANK, 256])
                vecs = sb(phase, "vecs", [P, 2 + 4 + 1])
                pool_w = sb(phase, "pool_w", [P, 4, P])
                resets = sb(phase, "resets", [P, L])
                gla_mask = sb(phase, "gla_mask", [P, T], I32)
                y_hi = sb(phase, "y1_hi", [P, DC, T], F32R)
                y_lo = sb(phase, "y1_lo", [P, DC, T], F32R)
                load("gate_up", gate_up[:, :], dram["w_gate_up"], late=True)
                load("vecs", vecs[:, :], dram["vecs"], late=True)
                load("resets", resets[:, :], dram["resets"], late=True)
                load("gla_mask", gla_mask[:, :], dram["gla_mask"], late=True)
                load("pool_w", pool_w[:, :, :], dram["pool_w"], late=True)

                load("meta", meta[:, :, :], dram["meta_t"])
                for c in range(DC):
                    load(f"x{c}", x[:, c, :], dram["x_t"][:, c, :])
                load("ones", ones[:, :], dram["ones"])

                mg = dve.do(lambda e: e.tensor_tensor(
                    meta_g[:, :, :], meta[:, :, :],
                    gains[:, 0:DC].rearrange("p (c o) -> p c o", o=1).to_broadcast([P, DC, META]), ALU.mult),
                    loads["meta"], loads["gains"])
                meta_ready = split_value(xg_hi[:, :, 0:META], xg_lo[:, :, 0:META], meta_g[:, :, :], mg)
                for c in range(DC):
                    split_x(c, 0, loads[f"x{c}"])
                split_panel()
                split_panel()
                sync.ops += late_loads
                sq = act.do(lambda e: e.activation(meta_sq[:, :, :], meta[:, :, :], ACT.Square), loads["meta"])
                for c in range(DC):
                    add_square(c, loads[f"x{c}"])
                meta_summed = dve.do(lambda e: e.tensor_reduce(
                    meta_sum[:, :], meta_sq[:, :, :].rearrange("p c t -> p t c"), AX, ALU.add), sq)

                def owed_rstd():
                    mm = pe.do(lambda e: e.matmul(bank_s[:, 0, 0:META], ones[:, :], meta_sum[:, :],
                                                  start=True, stop=True), meta_summed, loads["ones"])
                    free_s[0] = act.do(lambda e: e.activation(all_rstd[:, 0:META], bank_s[:, 0, 0:META], ACT.Ln,
                                                              scale=1.0 / D, bias=eps_col[:, 0:1]), mm, eps_ready)
                    token_rstd()
                    meta_rstd_w = act.do(lambda e: e.activation(all_rstd[:, 0:META], all_rstd[:, 0:META],
                                                                ACT.Exp, scale=-0.5), free_s[0])
                    state["all_rstd"] = dve.do(lambda e: e.tensor_copy(all_rstd[:, META:], rstd[:, :]),
                                               state["rstd"], meta_rstd_w)
                state["owed"] = owed_rstd

                half = L // 2

                def both(name, dst, rows=P, dst_free=None):
                    b, t = next_l(), next_t()
                    done = product(name, [lambda c: xg_hi[:, c, 0:half], lambda c: xg_hi[:, c, half:]],
                                   [lambda c: xg_lo[:, c, 0:half], lambda c: xg_lo[:, c, half:]],
                                   [bank_l[b][:, 0:half], bank_t[t][:, 0:half]],
                                   [[r, meta_ready] for r in xg_ready], [free_l[b], free_t[t]])
                    state["xg_used"] = done
                    settle()
                    free_l[b] = dve.do(lambda e: e.tensor_tensor(dst[0:rows, 0:half], bank_l[b][0:rows, 0:half],
                                                                 all_rstd[0:rows, 0:half], ALU.mult),
                                       done, state["all_rstd"], dst_free)
                    free_t[t] = dve.do(lambda e: e.tensor_tensor(dst[0:rows, half:], bank_t[t][0:rows, 0:half],
                                                                 all_rstd[0:rows, half:], ALU.mult),
                                       done, state["all_rstd"], dst_free)
                    return [free_l[b], free_t[t]]

                with ExitStack() as gla:
                    g_low = sb(gla, "g_low", [GATE_RANK, L])
                    k_f = sb(gla, "k_f", [P, 2, L])
                    q_f = sb(gla, "q_f", [P, 2, T])
                    v_f = sb(gla, "v_f", [P, 2, L])
                    v_tok = sb(gla, "v_tok", [P, TB, 512])
                    v_meta = sb(gla, "v_meta", [META, 512])
                    la = sb(gla, "la", [P, 2, L])
                    e1 = sb(gla, "e1", [P, L])
                    bsum = sb(gla, "bsum", [P, 2, L])
                    k_end = sb(gla, "k_end", [P, 2, L])
                    ke_tok = sb(gla, "ke_tok", [P, TB, 256])
                    ke_meta = sb(gla, "ke_meta", [META, 256])
                    decay = sb(gla, "decay", [P, 2, N_CHUNK])
                    carry = sb(gla, "carry", [P, 2, N_CHUNK, GLA_V])
                    scores = sb(gla, "scores", [P, 2, T])
                    pool_u = sb(gla, "pool_u", [P, L])
                    pool_s = sb(gla, "pool_s", [P, 2, L])
                    o_f, o_square, head_rstd, r_f = (k_end[:, :, 0:T], e1[:, 0:T], v_f[:, 0, 0:T],
                                                     bsum[:, :, 0:T])

                    g_ready = both("g", g_low, GATE_RANK)
                    k_w = [both("k", k_f[:, 0, :])]
                    la_w = []
                    for hp in range(2):
                        t = next_t()
                        b = next_l()
                        w = gate_up[:, hp * P:(hp + 1) * P]
                        pe.run(lambda e, b=b, w=w: e.matmul(bank_l[b][:, :], w, g_low[:, META:], start=True, stop=True),
                               g_ready, free_l[b], loads["gate_up"])
                        m = pe.do(lambda e, t=t, w=w: e.matmul(bank_t[t][:, 0:META], w, g_low[:, 0:META],
                                                               start=True, stop=True), free_t[t])
                        bias = vecs[:, hp:hp + 1]
                        w1 = dve.do(lambda e, b=b, hp=hp, s=bias: e.tensor_scalar(
                            la[:, hp, META:], bank_l[b][:, :], s, None, ALU.add), m, loads["vecs"])
                        free_l[b] = w1
                        w2 = dve.do(lambda e, t=t, hp=hp, s=bias: e.tensor_scalar(
                            la[:, hp, 0:META], bank_t[t][:, 0:META], s, None, ALU.add), m)
                        free_t[t] = w2
                        a = act.do(lambda e, hp=hp: e.activation(e1[:, :], la[:, hp, :], ACT.Abs), w1, w2,
                                   la_w[-1] if la_w else None)
                        a = act.do(lambda e: e.activation(e1[:, :], e1[:, :], ACT.Exp, scale=-1.0), a)
                        a = act.do(lambda e: e.activation(e1[:, :], e1[:, :], ACT.Ln, bias=1.0), a)
                        la_w.append(dve.do(lambda e, hp=hp: e.scalar_tensor_tensor(
                            la[:, hp, :], la[:, hp, :], 0.0, e1[:, :], ALU.min, ALU.subtract), a))
                    sums = [dve.do(lambda e, hp=hp: e.tensor_tensor_scan(
                        bsum[:, hp, :], resets[:, :], la[:, hp, :], 0.0, ALU.mult, ALU.add),
                        la_w[hp], loads["resets"]) for hp in range(2)]

                    k_w.append(both("k", k_f[:, 1, :]))

                    ke_w, decay_w = [], []
                    for hp in range(2):
                        blocks = bsum[:, hp, META:].rearrange("p (n c) -> p n c", c=CHUNK)
                        a1 = dve.do(lambda e, hp=hp, v=blocks: e.tensor_tensor(
                            k_end[:, hp, META:].rearrange("p (n c) -> p n c", c=CHUNK),
                            v[:, :, CHUNK - 1:CHUNK].to_broadcast([P, N_CHUNK, CHUNK]), v, ALU.subtract), sums[hp])
                        a2 = dve.do(lambda e, hp=hp: e.tensor_scalar(
                            k_end[:, hp, 0:META], bsum[:, hp, 0:META], bsum[:, hp, META - 1:META], -1.0,
                            ALU.subtract, ALU.mult), sums[hp])
                        ex = act.do(lambda e, hp=hp: e.activation(k_end[:, hp, :], k_end[:, hp, :], ACT.Exp,
                                                                  scale=1.0 / 16), a1, a2)
                        decay_w.append(act.do(lambda e, hp=hp, v=blocks: e.activation(
                            decay[:, hp, :], v[:, :, CHUNK - 1], ACT.Exp, scale=1.0 / 16), sums[hp]))
                        ke_w.append(dve.do(lambda e, hp=hp: e.tensor_tensor(
                            k_end[:, hp, :], k_end[:, hp, :], k_f[:, hp, :], ALU.mult), ex, k_w[hp]))
                    exps = []
                    for hp in range(2):
                        p1 = act.do(lambda e, hp=hp: e.activation(la[:, hp, :], bsum[:, hp, :], ACT.Exp,
                                                                  scale=1.0 / 16), sums[hp])
                        p2 = act.do(lambda e, hp=hp: e.activation(bsum[:, hp, :], bsum[:, hp, :], ACT.Exp,
                                                                  scale=-1.0 / 16), p1, decay_w[hp], ke_w[hp])
                        exps.append((p1, p2))
                    kt_w = [dve.do(lambda e, hp=hp: e.tensor_tensor(k_f[:, hp, :], k_f[:, hp, :],
                                                                    bsum[:, hp, :], ALU.mult), exps[hp][1], ke_w[hp])
                            for hp in range(2)]

                    def to_tokens(src, dst, dst_meta, col, marks):
                        t = next_t()
                        for blk in range(TB):
                            m = pe.do(lambda e, blk=blk: e.transpose(
                                bank_t[t][:, blk * P:(blk + 1) * P],
                                src[:, META + blk * P:META + (blk + 1) * P], ident[:, :]),
                                marks, free_t[t], loads["ident"])
                        free_t[t] = act.do(lambda e: e.activation(
                            dst[:, :, col:col + P], bank_t[t][:, :].rearrange("p (b c) -> p b c", c=P), ACT.Copy), m)
                        r1 = free_t[t]
                        t2 = next_t()
                        m = pe.do(lambda e: e.transpose(bank_t[t2][0:META, 0:P], src[:, 0:META], ident[:, :]),
                                  free_t[t2])
                        free_t[t2] = act.do(lambda e: e.activation(dst_meta[:, col:col + P],
                                                                   bank_t[t2][0:META, 0:P], ACT.Copy), m)
                        return [r1, free_t[t2]], m

                    v_w, v_read, w = [], [None, None], None
                    for i in range(4):
                        w_next = both("v", v_f[:, i % 2, :], dst_free=v_read[i % 2])
                        if i:
                            r, v_read[(i - 1) % 2] = to_tokens(v_f[:, (i - 1) % 2, :], v_tok, v_meta, (i - 1) * P, w)
                            v_w += r
                        w = w_next
                    to_q = x_product("q")
                    r, _ = to_tokens(v_f[:, 1, :], v_tok, v_meta, 3 * P, w)
                    v_w += r
                    ke_ready = []
                    for hp in range(2):
                        r, _ = to_tokens(k_end[:, hp, :], ke_tok, ke_meta, hp * P, ke_w[hp])
                        ke_ready += r

                    qt_w = []

                    def scale_q(hp, b, done):
                        w = free_l[b] = dve.do(lambda e: e.scalar_tensor_tensor(
                            q_f[:, hp, :], bank_l[b][:, :], GLA_K ** -0.5, rstd[:, :], ALU.mult, ALU.mult),
                            done, state["rstd"])
                        qt_w.append(dve.do(lambda e: e.tensor_tensor(
                            q_f[:, hp, :], q_f[:, hp, :], la[:, hp, META:], ALU.mult), w, exps[hp][0]))

                    scale_q(0, *to_q)

                    carry_w = [[None] * N_CHUNK, [None] * N_CHUNK]

                    def carry_step(n):
                        s = (n + 1) % 3
                        po = 64 * (n % 2)
                        for h in range(GLA_HEADS):
                            if n < 0:
                                lhs, rhs = ke_meta[:, h * 64:(h + 1) * 64], v_meta[:, h * P:(h + 1) * P]
                            else:
                                lhs = ke_tok[po:po + 64, n // 2, h * 64:(h + 1) * 64]
                                rhs = v_tok[po:po + 64, n // 2, h * P:(h + 1) * P]
                            d = bank_s[64 * (h % 2):64 * (h % 2) + 64, s, (h // 2) * P:(h // 2 + 1) * P]
                            m = pe.do(lambda e, d=d, a=lhs, b=rhs, h=h: e.matmul(
                                d, a, b, start=(h < 2), stop=True, skip_group_check=True),
                                ke_ready, v_w, free_s[s])
                        for hp in range(2):
                            src = bank_s[:, s, hp * P:(hp + 1) * P]
                            if n < 0:
                                carry_w[hp][0] = dve.do(lambda e, hp=hp, v=src: e.tensor_copy(
                                    carry[:, hp, 0, :], v), m)
                            else:
                                carry_w[hp][n + 1] = dve.do(lambda e, hp=hp, v=src: e.scalar_tensor_tensor(
                                    carry[:, hp, n + 1, :], carry[:, hp, n, :], decay[:, hp, n:n + 1], v,
                                    ALU.mult, ALU.add), m, carry_w[hp][n], decay_w[hp])
                            free_s[s] = carry_w[hp][n + 1]

                    for n in range(-1, 2):
                        carry_step(n)
                    to_q = x_product("q")
                    for n in range(2, 5):
                        carry_step(n)
                    scale_q(1, *to_q)
                    for n in range(5, N_CHUNK - 1):
                        carry_step(n)
                    zeroed = pool.do(lambda e: e.memset(scores[:, :, :], 0.0))

                    y_w = [None] * DC
                    scores_read = [None, None]
                    o_read, r_read, sq_read = [ke_ready, ke_ready], [kt_w, kt_w], la_w
                    u_read, p_read = None, None

                    def finish_head(h, o_w, o_sq, r_w):
                        z, t = h % 2, next_t()
                        m = pe.do(lambda e: e.matmul(bank_t[t][:, :], ones[:, :], o_square[:, :],
                                                     start=True, stop=True), o_sq, free_t[t])
                        a = act.do(lambda e: e.activation(head_rstd[:, :], bank_t[t][:, :], ACT.Ln,
                                                          scale=1.0 / GLA_V, bias=eps_col[:, 0:1]), m, marks["norm"])
                        free_t[t] = a
                        a = act.do(lambda e: e.activation(head_rstd[:, :], head_rstd[:, :], ACT.Exp, scale=-0.5), a)
                        v = dve.do(lambda e: e.scalar_tensor_tensor(
                            o_f[:, z, :], o_f[:, z, :], vecs[:, 6:7], head_rstd[:, :], ALU.mult, ALU.mult), a, o_w)
                        marks["norm"] = v
                        v = dve.do(lambda e: e.tensor_tensor(o_f[:, z, :], o_f[:, z, :], r_f[:, z, :], ALU.mult),
                                   v, r_w)
                        r_read[z] = v
                        y_w[4 + h] = o_read[z] = split_value(y_hi[:, 4 + h, :], y_lo[:, 4 + h, :], o_f[:, z, :], v)
                        return m

                    marks = {"norm": v_w}
                    pending = None
                    for h in range(GLA_HEADS):
                        hp, po, z = h // 2, 64 * (h % 2), h % 2
                        u_w = both("pool", pool_u[:, :], dst_free=u_read)
                        width, src, cur, flip = 1, pool_u[:, :], u_w, 0
                        while width < POOL_WINDOWS[h]:
                            dst = pool_s[:, flip, :]
                            cur = (pool if width < 4 else dve).do(lambda e, d=dst, s=src, w=width: e.tensor_tensor(
                                d[:, 2 * w - 1:L], s[:, 2 * w - 1:L], s[:, w - 1:L - w], ALU.add),
                                cur, p_read, zeroed)
                            src, width, flip = dst, 2 * width, flip ^ 1
                        dst = pool_s[:, flip, META:L]
                        pooled = dve.do(lambda e, d=dst, s=src, h=h: e.scalar_tensor_tensor(
                            d, s[:, META:L], 1.0 / POOL_WINDOWS[h], pool_u[:, META:L], ALU.mult, ALU.subtract),
                            cur, u_w)

                        t = next_t()
                        for blk in range(TB):
                            m = pe.do(lambda e, a=blk * P, b=(blk + 1) * P, hp=hp, po=po, t=t: e.matmul(
                                bank_t[t][:, a:b], k_f[po:po + 64, hp, META + a:META + b],
                                q_f[po:po + 64, hp, a:b], start=True, stop=True),
                                kt_w[hp], qt_w[hp], free_t[t])
                        scores_w = free_t[t] = dve.do(lambda e, z=z, t=t: e.copy_predicated(
                            scores[:, z, :], gla_mask[:, :], bank_t[t][:, :]),
                            m, zeroed, scores_read[z], loads["gla_mask"])
                        if pending:
                            sq_read = finish_head(*pending)

                        b, done = x_product("r")
                        r_w = free_l[b] = dve.do(lambda e, b=b, z=z: e.tensor_tensor(
                            r_f[:, z, :], bank_l[b][:, :], rstd[:, :], ALU.mult), done, state["rstd"], r_read[z])
                        r_w = act.do(lambda e, z=z: e.activation(r_f[:, z, :], r_f[:, z, :], ACT.Silu), r_w)

                        b = next_l()
                        m = pe.do(lambda e, b=b, d=dst, h=h: e.matmul(bank_l[b][:, :], pool_w[:, h, :], d,
                                                                      start=True, stop=True),
                                  pooled, free_l[b], loads["pool_w"])
                        u_read, p_read = pooled, m
                        sc = vecs[:, 2 + h:3 + h]
                        hi = act.do(lambda e, b=b, h=h, s=sc: e.activation(y_hi[:, h, :], bank_l[b][:, :],
                                                                           ACT.Copy, scale=s), m, loads["vecs"])
                        y_w[h] = free_l[b] = dve.do(lambda e, b=b, h=h, s=sc: e.scalar_tensor_tensor(
                            y_lo[:, h, :], bank_l[b][:, :], s, y_hi[:, h, :].bitcast(F32),
                            ALU.mult, ALU.subtract), hi)

                        for blk in range(TB):
                            pe.run(lambda e, blk=blk, h=h, z=z: e.matmul(
                                bank_o[:, blk * P:(blk + 1) * P], v_tok[:, blk, h * P:(h + 1) * P],
                                scores[:, z, blk * P:(blk + 1) * P], start=(blk == 0), stop=False,
                                skip_group_check=True), scores_w, free_o[0], v_w)
                        for n in range(N_CHUNK):
                            m = pe.do(lambda e, n=n, hp=hp, po=po: e.matmul(
                                bank_o[:, n * CHUNK:(n + 1) * CHUNK], carry[po:po + 64, hp, n, :],
                                q_f[po:po + 64, hp, n * CHUNK:(n + 1) * CHUNK], start=False,
                                stop=(n == N_CHUNK - 1), skip_group_check=True), carry_w[hp][n])
                        scores_read[z] = m
                        o_w = act.do(lambda e, z=z: e.activation(o_f[:, z, :], bank_o[:, :], ACT.Copy), m, o_read[z])
                        o_sq = free_o[0] = act.do(lambda e: e.activation(o_square[:, :], bank_o[:, :], ACT.Square),
                                                  m, sq_read)
                        pending = (h, o_w, o_sq, r_w)
                    finish_head(*pending)
                for m in range(DC):
                    b = next_l()
                    done = product("out", lambda c: y_hi[:, c, :], lambda c: y_lo[:, c, :],
                                   bank_l[b][:, :], y_w, free_l[b])
                    add_to_x(m, b, done, 1.0, 1)
                token_rstd()

        router_bias = sb(stack, "router_bias", [ROUTES, 1])
        load("router_bias", router_bias[:, :], dram["router_bias"], late=True)
        x_rows = nc.dram_tensor("x_rows", (T, D), F32, kind="Internal").ap()
        y_rows = nc.dram_tensor("y_rows", (TILES * P, D), F32, kind="Internal").ap()
        table = sb(stack, "overflow_expert", [1, OVERFLOW + 1], I32)

        def mixture():
            fence()
            with ExitStack() as phase:
                slot_of = sb(phase, "slot_of", [P, TB, TOP_K], U32)
                token_of = sb(phase, "token_of", [P, TILES], U32)
                weight = sb(phase, "weight", [P, TOP_K, TB, 1])
                ring_stack = ExitStack()
                experts_ring["memory"] = sb(ring_stack, "expert_raw", [P, EXPERT_OWN, PANEL])

                with ExitStack() as routing:
                    lt = sb(routing, "logits_t", [P, T])
                    gain_diag = sb(routing, "gain_diag", [P, DC, P])
                    token_rms = sb(routing, "token_rms", [P, TB, 2])
                    rows = sb(routing, "rows", [P, TB, D])
                    lg = sb(routing, "logits", [P, TB, ROUTES])
                    rank = sb(routing, "rank", [P, TB, 4])
                    hot_g = sb(routing, "hot_g", [P, TB, 4])
                    hot = [sb(routing, f"hot{i}", [P, TB, 4]) for i in range(TOP_K)]
                    tmp4 = sb(routing, "tmp4", [P, TB, 4])
                    tmp16 = sb(routing, "tmp16", [P, TB, 4, 4])
                    el = sb(routing, "el", [P, TB, 4])
                    pick = sb(routing, "pick", [P, TB, 4])
                    col = sb(routing, "col", [P, 8, TB, 1])
                    chosen = [sb(routing, f"chosen{i}", [P, TB, N_EXPERTS]) for i in range(TOP_K)]
                    both_c = sb(routing, "both_chosen", [P, TB, N_EXPERTS])
                    slots = sb(routing, "slots", [P, TB, N_EXPERTS])
                    tile_n = sb(routing, "tile_n", [P, 3, N_EXPERTS])
                    numbers = sb(routing, "numbers", [1, OVERFLOW, N_EXPERTS])
                    upto = sb(routing, "upto", [1, OVERFLOW, N_EXPERTS])
                    owner = sb(routing, "owner", [1, OVERFLOW])
                    first_slot = sb(routing, "first_slot", [P, N_EXPERTS])
                    behind = sb(routing, "behind", [P, TB, N_EXPERTS])
                    slot_f = sb(routing, "slot_f", [P, TOP_K, TB, 1])
                    token_id = sb(routing, "token_id", [P, TB])
                    bounds = sb(routing, "bounds", [P, 1, TILES + 1])
                    columns = sb(routing, "columns", [P, P])
                    reached = sb(routing, "reached", [P, TOP_K * TB, TILES + 1])
                    tile_hot = sb(routing, "tile_hot", [P, TOP_K * TB, TILES])
                    slot_hot = sb(routing, "slot_hot", [P, TOP_K * TB, P])
                    in_tile = sb(routing, "in_tile", [P, TOP_K * TB, 1])
                    ones16 = sb(routing, "ones16", [P, N_EXPERTS])
                    pool.wait(pe.last)
                    sync.wait(*[e.last for e in (pe, act, dve, pool)])
                    load("rank", rank[:, :, :], dram["rank"], queue=pool)
                    load("numbers", numbers[:, :, :], dram["numbers"], queue=pool)
                    load("token_id", token_id[:, :], dram["token_id"], queue=pool)
                    load("bounds", bounds[:, :, :], dram["bounds"], queue=pool)
                    load("columns", columns[:, :], dram["columns"], queue=pool)
                    load("first_slot", first_slot[:, :], dram["first_slot"], queue=pool)

                    b_route, done = x_product("route")
                    arrivals = []
                    for k in range(experts_ring["issued"], EXPERT_RAW):
                        arrivals.append(load_expert_panel(k, arrivals[-2] if k >= 2 and len(arrivals) > 1 else None))
                    diag_w = []
                    for c in range(DC):
                        diag_w.append(dve.do(lambda e, c=c: e.tensor_scalar(
                            gain_diag[:, c, :], ident[:, :], gain(1, c), None, ALU.mult), loads["ident"]))
                    m = free_l[b_route] = dve.do(lambda e: e.tensor_tensor(
                        lt[0:ROUTES, :], bank_l[b_route][0:ROUTES, :], rstd[0:ROUTES, :], ALU.mult),
                        done, state["rstd"])
                    logits_w = dve.do(lambda e: e.tensor_scalar(
                        lt[0:ROUTES, :], lt[0:ROUTES, :], router_bias[:, 0:1], None, ALU.add),
                        m, loads["router_bias"])
                    for blk in range(TB):
                        p = pe.do(lambda e, blk=blk: e.matmul(
                            bank_o[:, 2 * blk:2 * blk + 2], square_sum[:, blk * P:(blk + 1) * P], ones[:, 0:2],
                            start=True, stop=True), sum_mark[0], free_o[0])
                    state["sum_used"] = p
                    m = free_o[0] = act.do(lambda e: e.activation(
                        token_rms[:, :, :], bank_o[:, 0:2 * TB].rearrange("p (b o) -> p b o", o=2), ACT.Ln,
                        scale=1.0 / D, bias=eps_col[:, 0:1]), p)
                    token_rms_w = act.do(lambda e: e.activation(token_rms[:, :, :], token_rms[:, :, :], ACT.Exp,
                                                                scale=-0.5), m)

                    rows_written = sem("rows_written")
                    for blk in range(TB):
                        marks = []
                        for h in range(2):
                            t = next_t()
                            for c in range(4):
                                m = pe.do(lambda e, t=t, c=4 * h + c, at=c * P, blk=blk: e.matmul(
                                    bank_t[t][:, at:at + P], x[:, c, blk * P:(blk + 1) * P], gain_diag[:, c, :],
                                    start=True, stop=True), x_written[4 * h + c], diag_w[4 * h + c], free_t[t])
                                x_read[4 * h + c] = (x_read[4 * h + c] or []) + [m]
                            marks.append(act.do(lambda e, t=t, h=h, blk=blk: e.activation(
                                rows[:, blk, h * 512:(h + 1) * 512], bank_t[t][:, :], ACT.Copy,
                                scale=token_rms[:, blk, 0:1]), m, token_rms_w))
                            free_t[t] = marks[-1]
                        act.wait(*marks)
                        act.ops.append(lambda e, blk=blk: e.dma_start(
                            x_rows[blk * P:(blk + 1) * P, :], rows[:, blk, :]).then_inc(rows_written, 16))
                        if blk == 0:
                            for k in range(TB):
                                p = pe.do(lambda e, k=k: e.transpose(
                                    bank_s[:, 0, k * 32:k * 32 + ROUTES], lt[0:ROUTES, k * P:(k + 1) * P],
                                    ident[0:ROUTES, 0:ROUTES]), logits_w, free_s[0])
                            free_s[0] = dve.do(lambda e: e.tensor_copy(
                                lg[:, :, :], bank_s[:, 0, 0:TB * 32].rearrange("p (b r) -> p b r", r=32)[
                                    :, :, 0:ROUTES]), p)

                    def chain(make, *marks):
                        return dve.do(make, dve.last, *marks)

                    def wide(v):
                        return v.to_broadcast([P, TB, 4])

                    def first_of(values, peak, dst):
                        chain(lambda e: e.tensor_tensor(tmp4[:, :, :], values, wide(peak), ALU.is_equal))
                        chain(lambda e: e.tensor_tensor(tmp4[:, :, :], tmp4[:, :, :], rank[:, :, :], ALU.mult),
                              loads["rank"])
                        chain(lambda e: e.tensor_reduce(col[:, 7, :, :], tmp4[:, :, :], AX, ALU.max))
                        chain(lambda e: e.tensor_tensor(dst, tmp4[:, :, :], wide(col[:, 7, :, :]), ALU.is_equal))

                    g_l = lg[:, :, 0:N_GROUPS]
                    chain(lambda e: e.tensor_reduce(col[:, 0, :, :], g_l, AX, ALU.max))
                    first_of(g_l, col[:, 0, :, :], hot_g[:, :, :])
                    m = chain(lambda e: e.tensor_tensor(pick[:, :, :], g_l, wide(col[:, 0, :, :]), ALU.subtract))
                    exp_g = act.do(lambda e: e.activation(pick[:, :, :], pick[:, :, :], ACT.Exp), m)
                    e_l = lg[:, :, N_GROUPS:].rearrange("p b (g e) -> p b g e", e=4)

                    def by_group(v):
                        return v.rearrange("p b (g o) -> p b g o", o=1).to_broadcast([P, TB, 4, 4])

                    def by_expert(v):
                        return v.rearrange("p b (o e) -> p b o e", o=1).to_broadcast([P, TB, 4, 4])

                    chain(lambda e: e.tensor_tensor(tmp16[:, :, :, :], e_l, by_group(hot_g[:, :, :]), ALU.mult))
                    chain(lambda e: e.tensor_reduce(el[:, :, :], tmp16[:, :, :, :].rearrange("p b g e -> p b e g"),
                                                    AX, ALU.add))
                    chain(lambda e: e.tensor_reduce(col[:, 2, :, :], el[:, :, :], AX, ALU.max))
                    first_of(el[:, :, :], col[:, 2, :, :], hot[0][:, :, :])
                    chain(lambda e: e.tensor_reduce(col[:, 1, :, :], pick[:, :, :], AX, ALU.add), exp_g)
                    m = chain(lambda e: e.tensor_tensor(pick[:, :, :], el[:, :, :], wide(col[:, 2, :, :]),
                                                        ALU.subtract))
                    exp_e = act.do(lambda e: e.activation(pick[:, :, :], pick[:, :, :], ACT.Exp), m)
                    chain(lambda e: e.scalar_tensor_tensor(el[:, :, :], hot[0][:, :, :], -3e38, el[:, :, :],
                                                           ALU.mult, ALU.add))
                    chain(lambda e: e.tensor_reduce(col[:, 3, :, :], el[:, :, :], AX, ALU.max))
                    first_of(el[:, :, :], col[:, 3, :, :], hot[1][:, :, :])
                    for i in range(TOP_K):
                        chain(lambda e, i=i: e.tensor_tensor(
                            chosen[i][:, :, :].rearrange("p b (g e) -> p b g e", e=4),
                            by_group(hot_g[:, :, :]), by_expert(hot[i][:, :, :]), ALU.mult))
                    m = chain(lambda e: e.tensor_tensor(both_c[:, :, :], chosen[0][:, :, :], chosen[1][:, :, :],
                                                        ALU.add))
                    places = [bank_s[:, 1, k * N_EXPERTS:(k + 1) * N_EXPERTS] for k in range(TB + 1)]
                    for blk in range(TB + 1):
                        for k in range(min(blk, TB - 1) + 1):
                            lhs = strict if k == blk else ones
                            p = pe.do(lambda e, blk=blk, k=k, w=lhs: e.matmul(
                                places[blk], w[:, :], both_c[:, k, :], start=(blk == 0),
                                stop=(k == min(blk, TB - 1)), skip_group_check=True),
                                m, free_s[1], loads["strict"])
                    count = places[TB]
                    for i in range(TOP_K):
                        chain(lambda e, i=i: e.tensor_tensor(tmp4[:, :, :], hot[i][:, :, :], pick[:, :, :],
                                                             ALU.mult), exp_e)
                        chain(lambda e, i=i: e.tensor_reduce(weight[:, i, :, :], tmp4[:, :, :], AX, ALU.add))
                    chain(lambda e: e.tensor_tensor(col[:, 4, :, :], weight[:, 0, :, :], weight[:, 1, :, :], ALU.add))
                    chain(lambda e: e.tensor_tensor(col[:, 5, :, :], col[:, 4, :, :], col[:, 1, :, :], ALU.mult))
                    chain(lambda e: e.reciprocal(col[:, 6, :, :], col[:, 5, :, :]))
                    for i in range(TOP_K):
                        weight_w = chain(lambda e, i=i: e.tensor_tensor(weight[:, i, :, :], weight[:, i, :, :],
                                                                        col[:, 6, :, :], ALU.mult))
                    chain(lambda e: e.memset(ones16[:, :], 1.0))
                    chain(lambda e: e.tensor_scalar(tile_n[:, 0, :], count, float(P), None, ALU.is_gt), p)
                    for k in range(2, TB):
                        chain(lambda e, k=k: e.scalar_tensor_tensor(tile_n[:, 0, :], count, float(k * P),
                                                                    tile_n[:, 0, :], ALU.is_gt, ALU.add))
                    chain(lambda e: e.tensor_tensor_scan(tile_n[:, 1, :], ones16[:, :], tile_n[:, 0, :], 0.0,
                                                         ALU.mult, ALU.add))
                    chain(lambda e: e.tensor_tensor(
                        upto[:, :, :], numbers[:, :, :],
                        tile_n[0:1, 1:2, :].to_broadcast([1, OVERFLOW, N_EXPERTS]), ALU.is_ge), loads["numbers"])
                    chain(lambda e: e.tensor_reduce(owner[:, :], upto[:, :, :], AX, ALU.add))
                    chain(lambda e: e.tensor_scalar(
                        table[:, 0:OVERFLOW], owner[:, :], float(N_EXPERTS - 1), None, ALU.min))
                    table_w = chain(lambda e: e.tensor_copy(table[:, OVERFLOW:OVERFLOW + 1],
                                                            tile_n[0:1, 1, N_EXPERTS - 1:N_EXPERTS]))
                    chain(lambda e: e.tensor_tensor(tile_n[:, 2, :], tile_n[:, 1, :], tile_n[:, 0, :], ALU.subtract))
                    chain(lambda e: e.tensor_scalar(tile_n[:, 2, :], tile_n[:, 2, :], float(N_EXPERTS - 1), float(P),
                                                    ALU.add, ALU.mult))
                    chain(lambda e: e.tensor_tensor(tile_n[:, 2, :], tile_n[:, 2, :], first_slot[:, :],
                                                    ALU.subtract), loads["first_slot"])
                    place = bank_s[:, 1, 0:TB * N_EXPERTS].rearrange("p (b e) -> p b e", e=N_EXPERTS)
                    chain(lambda e: e.tensor_scalar(behind[:, :, :], place, float(P), None, ALU.is_ge))
                    chain(lambda e: e.tensor_tensor(behind[:, :, :], behind[:, :, :],
                                                    tile_n[:, 2:3, :].to_broadcast([P, TB, N_EXPERTS]), ALU.mult))
                    free_s[1] = chain(lambda e: e.tensor_tensor(
                        slots[:, :, :], place, behind[:, :, :], ALU.add))
                    chain(lambda e: e.tensor_tensor(
                        slots[:, :, :], slots[:, :, :], first_slot[:, :].rearrange("p (o e) -> p o e", o=1).to_broadcast(
                            [P, TB, N_EXPERTS]), ALU.add))
                    for i in range(TOP_K):
                        chain(lambda e, i=i: e.tensor_tensor(chosen[i][:, :, :], chosen[i][:, :, :],
                                                             slots[:, :, :], ALU.mult))
                        chain(lambda e, i=i: e.tensor_reduce(slot_f[:, i, :, :], chosen[i][:, :, :], AX, ALU.add))
                    pairs = TOP_K * TB
                    slot_c = slot_f[:, :, :, :].rearrange("p k b o -> p (k b) o")
                    chain(lambda e: e.tensor_tensor(
                        reached[:, :, :], slot_c.to_broadcast([P, pairs, TILES + 1]),
                        bounds[:, :, :].to_broadcast([P, pairs, TILES + 1]), ALU.is_ge), loads["bounds"])
                    chain(lambda e: e.tensor_reduce(in_tile[:, :, :], reached[:, :, :], AX, ALU.add))
                    chain(lambda e: e.tensor_scalar(in_tile[:, :, :], in_tile[:, :, :], -float(P), float(P),
                                                    ALU.mult, ALU.add))
                    chain(lambda e: e.tensor_tensor(in_tile[:, :, :], in_tile[:, :, :], slot_c, ALU.add))
                    tile_hot_w = chain(lambda e: e.tensor_tensor(
                        tile_hot[:, :, :], reached[:, :, 0:TILES], reached[:, :, 1:], ALU.subtract))
                    for k in range(pairs):
                        blk = k % TB
                        hot_w = dve.do(lambda e, k=k, blk=blk: e.tensor_scalar(
                            slot_hot[:, k, :], columns[:, :], in_tile[:, k, :], token_id[:, blk:blk + 1],
                            ALU.is_equal, ALU.mult), tile_hot_w, loads["columns"], loads["token_id"])
                        p = pe.do(lambda e, k=k: e.matmul(
                            bank_s[:, 0, 0:TILES], slot_hot[:, k, :], tile_hot[:, k, :],
                            start=(k == 0), stop=(k == pairs - 1)), hot_w, free_s[0])
                    token_w = free_s[0] = chain(lambda e: e.tensor_copy(token_of[:, :], bank_s[:, 0, 0:TILES]), p)
                    slot_w = chain(lambda e: e.tensor_copy(
                        slot_of[:, :, :], slot_f[:, :, :, :].rearrange("p k b o -> p (b o) k")))
                    experts_ring["open"] = True
                    split_panel()
                    split_panel()
                    pool.wait(token_w, (rows_written, 16 * TB))
                    act.wait((rows_written, 16 * TB))
                    dve.wait((rows_written, 16 * TB))
                    fence()

                def stream_panel(products, *marks):
                    i = stream["next"]
                    assert order[i][0] == "experts"
                    stream["next"] += 1
                    split_ahead(i)
                    slot = i % SPLIT
                    pe.wait(split_ready[i], *marks)
                    slot_used[slot] = panel_products(pe, products, w_hi[:, slot, :], w_lo[:, slot, :])
                    return slot_used[slot]

                def panel_products(tensor, products, hi_w, lo_w):
                    for dst, hi, lo, at, first, last in products:
                        for n, (lhs, w) in enumerate(((hi, hi_w), (hi, lo_w), (lo, hi_w))):
                            op = (lambda e, d=dst, a=lhs, v=w[:, at:at + 512], f=first and n == 0,
                                  z=last and n == 2: e.matmul(d, a, v, start=f, stop=z))
                            done = tensor.do(op) if n == 2 else tensor.run(op)
                    return done

                def run_tiles(tag, engines, banks, first_tile, tiles, tile_panel):
                    pe, act, dve, pool = engines
                    free_l, free_s, free_t = banks
                    hid = EXPERT_HIDDEN
                    x_slot = sb(stage, f"x_slot_{tag}", [P, 2, D])
                    xt_hi = sb(stage, f"xt_hi_{tag}", [P, 2, DC, P], F32R)
                    xt_lo = sb(stage, f"xt_lo_{tag}", [P, 2, DC, P], F32R)
                    act_g = sb(stage, f"act_g_{tag}", [P, 2, hid])
                    hidden = sb(stage, f"hidden_{tag}", [P, 2, hid])
                    ht_hi = sb(stage, f"ht_hi_{tag}", [P, 2, 2, P], F32R)
                    ht_lo = sb(stage, f"ht_lo_{tag}", [P, 2, 2, P], F32R)
                    y_slot = sb(stage, f"y_slot_{tag}", [P, 2, D])
                    gathered = [sem(f"gathered_{tag}{i}") for i in range(2)]
                    y_stored = [sem(f"y_stored_{tag}{i}") for i in range(2)]
                    slot_read, xt_read, ht_read = [None] * 2, [None] * 2, [None] * 2
                    xt_w, hidden_w, ht_w = [None] * 2, [None] * 2, [None] * 2
                    hidden_read, act_read = [None] * 2, [None] * 2

                    def split(hi, lo, value, marks, free):
                        rounded = act.do(lambda e: e.activation(hi, value, ACT.Copy), marks, free)
                        return dve.do(lambda e: e.tensor_tensor(lo, value, hi.bitcast(F32), ALU.subtract),
                                      rounded, free)

                    def gather(i):
                        z = i % 2
                        pool.wait(slot_read[z])
                        at = first_tile + i
                        pool.ops.append(lambda e: e.indirect_dma_start(
                            out=x_slot[:, z, :], out_offset=None, in_=x_rows,
                            in_offset=bass.IndirectOffsetOnAxis(ap=token_of[:, at:at + 1], axis=0)
                        ).then_inc(gathered[z], 16))

                    def transpose_tokens(i):
                        z, marks = i % 2, []
                        for h in range(2):
                            t = next_t()
                            for c in range(4):
                                m = pe.do(lambda e, t=t, c=c, h=h: e.transpose(
                                    bank_t[t][:, c * P:(c + 1) * P],
                                    x_slot[:, z, (4 * h + c) * P:(4 * h + c + 1) * P],
                                    ident[:, :]), (gathered[z], 16 * (i // 2 + 1)), free_t[t])
                            marks.append(split(xt_hi[:, z, 4 * h:4 * h + 4, :], xt_lo[:, z, 4 * h:4 * h + 4, :],
                                               bank_t[t][:, :].rearrange("p (c s) -> p c s", s=P), m, xt_read[z]))
                            free_t[t] = marks[-1]
                        slot_read[z], xt_w[z] = m, marks

                    def gate_up(i, j, b):
                        z = i % 2
                        return tile_panel([(bank_l[b][:, :], xt_hi[:, z, c, :], xt_lo[:, z, c, :],
                                            512 * (c % 2), c == 0, c == DC - 1) for c in (2 * j, 2 * j + 1)],
                                          xt_w[z], free_l[b])

                    def transpose_hidden(i):
                        z = i % 2
                        for c in range(2):
                            m = pe.do(lambda e, c=c: e.transpose(bank_s[:, 2, c * P:(c + 1) * P],
                                                                 hidden[:, z, c * P:(c + 1) * P], ident[:, :]),
                                      hidden_w[z], free_s[2])
                        ht_w[z] = free_s[2] = split(ht_hi[:, z, :, :], ht_lo[:, z, :, :],
                                                    bank_s[:, 2, 0:2 * P].rearrange("p (c s) -> p c s", s=P),
                                                    m, ht_read[z])
                        hidden_read[z] = m

                    def down(i):
                        z = i % 2
                        for c in range(2):
                            done = tile_panel([(bank_s[:, h, :], ht_hi[:, z, c, :], ht_lo[:, z, c, :], 512 * h,
                                                c == 0, c == 1) for h in range(2)], ht_w[z], free_s[0], free_s[1])
                        ht_read[z] = done
                        stored_before = (y_stored[z], 16 * (i // 2)) if i >= 2 else None
                        free_s[0] = act.do(lambda e: e.activation(y_slot[:, z, 0:512], bank_s[:, 0, :], ACT.Copy),
                                           done, stored_before)
                        free_s[1] = dve.do(lambda e: e.tensor_copy(y_slot[:, z, 512:], bank_s[:, 1, :]),
                                           done, stored_before)
                        pool.wait(free_s[0], free_s[1])
                        at = (first_tile + i) * P
                        pool.ops.append(lambda e: e.dma_start(y_rows[at:at + P, :],
                                                              y_slot[:, z, :]).then_inc(y_stored[z], 16))

                    gather(0)
                    gather(1)
                    transpose_tokens(0)
                    for i in range(tiles + 1):
                        z = i % 2
                        if i < tiles:
                            b = next_l()
                            gate_up(i, 0, b)
                        if i:
                            transpose_hidden(i - 1)
                        if i < tiles:
                            gate_up(i, 1, b)
                            if i + 1 < tiles:
                                transpose_tokens(i + 1)
                            if i + 2 < tiles:
                                gather(i + 2)
                            gate_up(i, 2, b)
                            done = gate_up(i, 3, b)
                            xt_read[z] = done
                            g = act.do(lambda e, z=z, b=b: e.activation(act_g[:, z, :], bank_l[b][:, 0:hid],
                                                                        ACT.Silu), done, act_read[z])
                            hidden_w[z] = free_l[b] = act_read[z] = dve.do(lambda e, z=z, b=b: e.tensor_tensor(
                                hidden[:, z, :], bank_l[b][:, hid:], act_g[:, z, :], ALU.mult), g, hidden_read[z])
                        if i:
                            down(i - 1)
                    return [(y_stored[0], 16 * ((tiles + 1) // 2)), (y_stored[1], 16 * (tiles // 2))]

                with ExitStack() as stage:
                    y_all_stored = run_tiles("tile", (pe, act, dve, pool), (free_l, free_s, free_t),
                                             0, N_EXPERTS, stream_panel)
                ring_stack.close()

                before = [e.last for e in (pe, act, dve, pool)] + y_all_stored
                mains = (pe, act, dve, pool, sync)
                subs = [Engine(sem(f"overflow_{n}")) for n in ("pe", "act", "dve", "pool", "sync")]
                for sub in subs:
                    sub.wait(before)
                with ExitStack() as stage:
                    o_raw = sb(stage, "o_raw", [P, 2, PANEL])
                    o_hi = sb(stage, "o_hi", [P, 2, PANEL], F32R)
                    o_lo = sb(stage, "o_lo", [P, 2, PANEL], F32R)
                    o_arrived = [sem("overflow_arrived0"), sem("overflow_arrived1")]
                    o_order = []
                    for i in range(OVERFLOW + 1):
                        o_order += [(i, j) for j in range(GU_PANELS) if i < OVERFLOW]
                        o_order += [(i - 1, j) for j in range(GU_PANELS, TILE_PANELS) if i]
                    o_state = {"n": 0, "ready": [], "used": [None, None]}
                    o_registers = {}
                    s_pe, s_act, s_dve, s_pool, s_sync = subs

                    def overflow_load(k):
                        tile, part = o_order[k]
                        r = k % 2

                        def dma(e):
                            if tile not in o_registers:
                                o_registers[tile] = e.value_load(table[0:1, tile:tile + 1], min_val=0,
                                                                 max_val=N_EXPERTS - 1)
                            return e.dma_start(o_raw[:, r, :], dram["experts"][
                                bass.ds(o_registers[tile], 1), part, :, :].rearrange("o p w -> (o p) w")
                            ).then_inc(o_arrived[r], 16)
                        if k >= 2:
                            s_sync.wait(o_state["ready"][k - 2])
                        s_sync.ops.append(dma)
                        arrived = (o_arrived[r], 16 * (k // 2 + 1))
                        rounded = s_act.do(lambda e: e.activation(o_hi[:, r, :], o_raw[:, r, :], ACT.Copy),
                                           arrived, o_state["used"][r])
                        o_state["ready"].append(s_dve.do(lambda e: e.tensor_tensor(
                            o_lo[:, r, :], o_raw[:, r, :], o_hi[:, r, :].bitcast(F32), ALU.subtract),
                            arrived, rounded, o_state["used"][r]))

                    def overflow_panel(products, *marks):
                        k = o_state["n"]
                        o_state["n"] += 1
                        while len(o_state["ready"]) <= min(k + 1, len(o_order) - 1):
                            overflow_load(len(o_state["ready"]))
                        s_pe.wait(o_state["ready"][k], *marks)
                        o_state["used"][k % 2] = panel_products(s_pe, products, o_hi[:, k % 2, :], o_lo[:, k % 2, :])
                        return o_state["used"][k % 2]

                    overflow_stored = run_tiles("overflow", subs[:4], ([None] * 2, [None] * 3, [None] * 2),
                                                N_EXPERTS, OVERFLOW, overflow_panel)
                    after = [sub.last for sub in subs[:4]] + overflow_stored
                    for sub in subs:
                        sub.wait([m for m in after if m])

                def overflow_tiles(e):
                    return e.value_load(table[0:1, OVERFLOW:OVERFLOW + 1], min_val=0, max_val=OVERFLOW)

                for main, sub in zip(mains, subs):
                    main.wait(table_w)
                    main.only_if(lambda e: overflow_tiles(e) > 0, sub)

                y_pair = sb(phase, "y_pair", [P, TB, TOP_K, D])
                fetched = [sem(f"y_fetched{i}") for i in range(TB)]
                pool.wait(y_all_stored)
                pool.wait(*[e.last for e in (pe, act, dve)])
                sources = [(Engine(None), y_rows, lambda e: overflow_tiles(e) > 0),
                           (Engine(None), y_rows[0:N_EXPERTS * P, :], lambda e: overflow_tiles(e) == 0)]
                for blk in range(TB):
                    z = blk
                    for fetch, y_source, _ in sources:
                        for i in range(TOP_K):
                            fetch.ops.append(lambda e, blk=blk, i=i, z=z, source=y_source: e.indirect_dma_start(
                                out=y_pair[:, z, i, :], out_offset=None, in_=source,
                                in_offset=bass.IndirectOffsetOnAxis(ap=slot_of[:, blk, i:i + 1], axis=0)
                            ).then_inc(fetched[z], 16))
                    m = act.do(lambda e, blk=blk, z=z: e.activation(
                        y_pair[:, z, 0, :], y_pair[:, z, 0, :], ACT.Copy, scale=weight[:, 0, blk, :]),
                        (fetched[z], 16 * TOP_K), weight_w)
                    m = dve.do(lambda e, blk=blk, z=z: e.scalar_tensor_tensor(
                        y_pair[:, z, 0, :], y_pair[:, z, 1, :], weight[:, 1, blk, :], y_pair[:, z, 0, :],
                        ALU.mult, ALU.add), m)
                    for h in range(2):
                        t = next_t()
                        for c in range(4):
                            p = pe.do(lambda e, t=t, c=c, h=h, z=z: e.transpose(
                                bank_t[t][:, c * P:(c + 1) * P], y_pair[:, z, 0, (4 * h + c) * P:(4 * h + c + 1) * P],
                                ident[:, :]), m, free_t[t])
                        cs = slice(4 * h, 4 * h + 4)
                        w = free_t[t] = dve.do(lambda e, t=t, cs=cs, blk=blk: e.tensor_tensor(
                            x[:, cs, blk * P:(blk + 1) * P], x[:, cs, blk * P:(blk + 1) * P],
                            bank_t[t][:, :].rearrange("p (c s) -> p c s", s=P), ALU.add),
                            p, x_read[cs], x_written[cs])
                        if blk == TB - 1:
                            for c in range(4 * h, 4 * h + 4):
                                x_written[c], x_read[c] = w, None
                for fetch, _, condition in sources:
                    pool.only_if(condition, fetch)

        def normalise_between(g, g_next):
            both_gains = [gains[:, k * DC:(k + 1) * DC] for k in (g, g_next)]
            pair_w = [dve.do(lambda e, k=k: e.tensor_tensor(gain_pair[:, k * DC:(k + 1) * DC], both_gains[0],
                                                            both_gains[k], ALU.mult), loads["gains"])
                      for k in range(2)]
            for c in range(DC):
                factor = gain_pair[:, DC + c:DC + c + 1]
                rounded = act.do(lambda e, c=c, f=factor: e.activation(xg_hi[:, c, META:], x[:, c, :], ACT.Copy,
                                                                       scale=f),
                                 x_written[c], state["xg_used"], xg_ready[c], pair_w)
                xg_ready[c] = dve.do(lambda e, c=c, f=factor: e.scalar_tensor_tensor(
                    xg_lo[:, c, META:], x[:, c, :], f, xg_hi[:, c, META:].bitcast(F32), ALU.mult, ALU.subtract),
                    x_written[c], rounded, state["xg_used"])
                x_read[c] = (x_read[c] or []) + [rounded, xg_ready[c]]
            plain, gained = None, None
            for c in range(DC):
                half = c % 2
                target = square_sum[:, :] if c == 0 else squares[:, half, :]
                squared = act.do(lambda e, c=c, t=target: e.activation(t, x[:, c, :], ACT.Square),
                                 x_written[c], square_read[half] if c else state["sum_used"])
                x_read[c].append(squared)
                f = gain_pair[:, c:c + 1]
                if c == 0:
                    gained = dve.do(lambda e, f=f: e.tensor_scalar(gained_sum[:, :], square_sum[:, :], f, None,
                                                                   ALU.mult), squared)
                    plain = gained
                else:
                    gained = dve.do(lambda e, f=f, half=half: e.scalar_tensor_tensor(
                        gained_sum[:, :], squares[:, half, :], f, gained_sum[:, :], ALU.mult, ALU.add),
                        squared, gained)
                    plain = pool.do(lambda e, half=half: e.tensor_tensor(
                        square_sum[:, :], square_sum[:, :], squares[:, half, :], ALU.add), squared, plain)
                    square_read[half] = [gained, plain]
            def owed():
                summed = pe.do(lambda e: e.matmul(bank_o[:, :], ones[:, :], square_sum[:, :], start=True, stop=True),
                               plain, free_o[0])
                t = next_t()
                gained_summed = pe.do(lambda e: e.matmul(bank_t[t][:, :], ones[:, :], gained_sum[:, :],
                                                         start=True, stop=True), gained, free_t[t])
                state["sum_used"] = summed
                m = free_o[0] = act.do(lambda e: e.activation(first_rstd[:, :], bank_o[:, :], ACT.Ln, scale=1.0 / D,
                                                              bias=eps_col[:, 0:1]), summed)
                first = act.do(lambda e: e.activation(first_rstd[:, :], first_rstd[:, :], ACT.Exp, scale=-0.5), m)
                m = dve.do(lambda e: e.tensor_tensor(rstd[:, :], first_rstd[:, :], first_rstd[:, :], ALU.mult), first)
                m = free_t[t] = dve.do(lambda e: e.tensor_tensor(rstd[:, :], rstd[:, :], bank_t[t][:, :], ALU.mult),
                                       m, gained_summed)
                m = act.do(lambda e: e.activation(rstd[:, :], rstd[:, :], ACT.Ln, scale=1.0 / D,
                                                  bias=eps_col[:, 0:1]), m)
                m = act.do(lambda e: e.activation(rstd[:, :], rstd[:, :], ACT.Exp, scale=-0.5), m)
                state["rstd"] = dve.do(lambda e: e.tensor_tensor(rstd[:, :], rstd[:, :], first_rstd[:, :], ALU.mult), m)
                for c in range(DC):
                    x_written[c] = pool.do(lambda e, c=c: e.tensor_tensor(
                        x[:, c, :], x[:, c, :], first_rstd[:, :], ALU.mult), first, x_read[c], x_written[c])
                    x_written[c] = pool.do(lambda e, c=c: e.tensor_scalar(
                        x[:, c, :], x[:, c, :], gain(g, c), None, ALU.mult), x_written[c])
                    x_read[c] = None
            state["owed"] = owed

        def normalise(g):
            for c in range(DC):
                w = x_written[c] = dve.do(lambda e, c=c: e.scalar_tensor_tensor(
                    x[:, c, :], x[:, c, :], gain(g, c), rstd[:, :], ALU.mult, ALU.mult),
                    state["rstd"], x_read[c], x_written[c])
                sync.wait(w)
                sync.ops.append(lambda e, c=c: e.dma_start(out[:, c, :], x[:, c, :]).then_inc(stored, 16))

        stored = sem("stored")


        rotate = sb(stack, "rotate", [P, P])
        suffix = sb(stack, "suffix", [P, P])
        minus = sb(stack, "minus", [P, P])
        masks_f = sb(stack, "masks_bf", [P, 2 * P + 4 * P + 4 * P + P], BF16)
        load("rotate", rotate[:, :], dram["rotate"], late=True)
        load("suffix", suffix[:, :], dram["suffix"], late=True)
        load("minus", minus[:, :], dram["minus"], late=True)
        load("masks", masks_f[:, :], dram["masks"], late=True)
        MASK_END = (2 * P, 6 * P, 10 * P)

        def mixer_2(l):
            g_out = 3 + 3 * l + 2
            name = f"in_{l}"
            fence()
            with ExitStack() as phase:
                o_f = sb(phase, f"o_f_{l}", [P, 4, T])
                gates = sb(phase, f"gates_{l}", [P, 16, T])
                att = ExitStack()
                qk = sb(att, f"qk_{l}", [P, 16, T])
                v_tok = sb(att, f"vt_{l}", [P, TB, D])
                rope = ExitStack()
                cos = sb(rope, f"cos_{l}", [P, T])
                sin = sb(rope, f"sin_{l}", [P, T])
                rot = sb(rope, f"rot_{l}", [P, 2, T])
                val = sb(rope, f"values_{l}", [P, 2, T])
                pool.wait(pe.last)
                load(f"cos_{l}", cos[:, :], dram["cos"], queue=pool)
                load(f"sin_{l}", sin[:, :], dram["sin"], queue=pool)
                rot_read = [None, None]
                qk_w = [None] * 16
                pending = []

                def next_panel():
                    b, done = x_product(name)
                    if len(pending) == 2:
                        pending.pop(0)()
                    return b, done

                def rotated_panel(i):
                    b, done = next_panel()
                    scale = HEAD ** -0.5 if i < 6 else 1.0
                    w = free_l[b] = dve.do(lambda e: e.scalar_tensor_tensor(
                        qk[:, i, :], bank_l[b][:, :], scale, rstd[:, :], ALU.mult, ALU.mult), done, state["rstd"])

                    def rest():
                        t, r = next_t(), i % 2
                        m = pe.do(lambda e: e.matmul(bank_t[t][:, :], rotate[:, :], qk[:, i, :],
                                                     start=True, stop=True), w, free_t[t], loads["rotate"])
                        free_t[t] = dve.do(lambda e: e.tensor_tensor(
                            rot[:, r, :], bank_t[t][:, :], sin[:, :], ALU.mult), m, rot_read[r], loads[f"sin_{l}"])
                        a = pool.do(lambda e: e.tensor_tensor(qk[:, i, :], qk[:, i, :], cos[:, :], ALU.mult),
                                    w, m, loads[f"cos_{l}"])
                        qk_w[i] = rot_read[r] = pool.do(lambda e: e.tensor_tensor(
                            qk[:, i, :], qk[:, i, :], rot[:, r, :], ALU.add), a, free_t[t])
                    pending.append(rest)

                v_w = []

                def value_panel(i):
                    b, done = next_panel()
                    r = i % 2
                    w = free_l[b] = dve.do(lambda e: e.tensor_tensor(val[:, r, :], bank_l[b][:, :],
                                                                     rstd[:, :], ALU.mult),
                                           done, state["rstd"], val_read[r])

                    def rest():
                        t = next_t()
                        for blk in range(TB):
                            m = pe.do(lambda e, blk=blk: e.transpose(
                                bank_t[t][:, blk * P:(blk + 1) * P], val[:, r, blk * P:(blk + 1) * P], ident[:, :]),
                                w, free_t[t])
                        val_read[r] = m
                        free_t[t] = act.do(lambda e: e.activation(
                            v_tok[:, :, i * P:(i + 1) * P], bank_t[t][:, :].rearrange("p (b c) -> p b c", c=P),
                            ACT.Copy), m)
                        v_w.append(free_t[t])
                    pending.append(rest)

                val_read = [None, None]
                for i in range(12):
                    rotated_panel(i)
                for i in range(8):
                    value_panel(i)
                for rest in pending:
                    rest()
                fence()
                rope.close()

                work = ExitStack()
                prob = sb(work, f"prob_{l}", [P, 2, 1280])
                prob_t = sb(work, f"prob_t_{l}", [P, 2, T])
                stat = sb(work, f"stat_{l}", [P, 2, 8])
                prob_read, pt_read = [None, None], [None, None]
                pt = {"n": 0}
                o_w = []
                gate_n = {"i": 0}

                def gate_panel():
                    i = gate_n["i"]
                    if i == 16:
                        return
                    gate_n["i"] += 1
                    b, done = x_product(name)
                    free_l[b] = gate_w[i] = dve.do(lambda e: e.tensor_tensor(
                        gates[:, i, :], bank_l[b][:, :], rstd[:, :], ALU.mult), done)

                gate_w = [None] * 16

                def stick_panel(i):
                    b, done = x_product(name)
                    scale = HEAD ** -0.5 if i < 14 else 1.0
                    qk_w[i] = free_l[b] = dve.do(lambda e: e.scalar_tensor_tensor(
                        qk[:, i, :], bank_l[b][:, :], scale, rstd[:, :], ALU.mult, ALU.mult), done)

                def dilated_scores(u, s, blk):
                    z, po = u % 2, 64 * (s % 2)
                    first = max(blk - 1, 0)
                    k0 = (first, 0, 0)
                    width = [(blk + 1 - k) * P for k in k0]
                    for g in range(3):
                        ch = (g * SLOTS + s) // 2
                        pe.run(lambda e, g=g: e.matmul(
                            bank_s[:, g, 0:width[g]], ident_bf[:, :], masks_f[:, MASK_END[g] - width[g]:MASK_END[g]],
                            start=True, stop=False), free_s[g], ident_bf_ready, loads["masks"])
                        m = pe.do(lambda e, g=g, ch=ch: e.matmul(
                            bank_s[:, g, 0:width[g]], qk[po:po + 64, ch, blk * P:(blk + 1) * P],
                            qk[po:po + 64, 6 + ch, k0[g] * P:(blk + 1) * P], start=False, stop=True),
                            qk_w[ch], qk_w[6 + ch])
                    w0, w1 = width[0], width[1]
                    st = stat[:, z, :]
                    r1 = dve.do(lambda e: e.tensor_reduce(st[:, 0:1], bank_s[:, 0, 0:w0], AX, ALU.max),
                                m)
                    r2 = dve.do(lambda e: e.tensor_reduce(st[:, 1:3], bank_s[:, 1:3, 0:w1], AX, ALU.max), m)
                    r = dve.do(lambda e: e.tensor_reduce(st[:, 3:4], st[:, 0:3], AX, ALU.max), r1, r2)
                    r = dve.do(lambda e: e.tensor_scalar(st[:, 4:5], st[:, 3:4], -1.0, None, ALU.mult), r)
                    a1 = act.do(lambda e: e.activation(prob[:, z, 0:w0], bank_s[:, 0, 0:w0], ACT.Exp,
                                                       bias=st[:, 4:5], accum_out=st[:, 5:6]), r, prob_read[z])
                    a2 = act.do(lambda e: e.activation(
                        prob[:, z, w0:w0 + 2 * w1].rearrange("p (g k) -> p g k", g=2), bank_s[:, 1:3, 0:w1],
                        ACT.Exp, bias=st[:, 4:5], accum_out=st[:, 6:7]), r)
                    free_s[0] = [a1]
                    free_s[1] = free_s[2] = [a2]
                    r = dve.do(lambda e: e.tensor_tensor(st[:, 7:8], st[:, 5:6], st[:, 6:7], ALU.add), a1, a2)
                    r = dve.do(lambda e: e.reciprocal(st[:, 7:8], st[:, 7:8]), r)
                    return dve.do(lambda e: e.tensor_scalar(prob[:, z, 0:w0 + 2 * w1], prob[:, z, 0:w0 + 2 * w1],
                                                            st[:, 7:8], None, ALU.mult), r)

                pending_values = {"do": None}

                def dilated_values(u, s, blk, prob_w):
                    z, po = u % 2, 64 * (s % 2)
                    first = max(blk - 1, 0)
                    w0 = (blk + 1 - first) * P
                    batches = [(1, 0, w0), (2, 0, w0 + (blk + 1) * P), (0, first, 0)]
                    for g, k0, at in batches:
                        t, nb, y = next_t(), blk + 1 - k0, pt["n"] % 2
                        pt["n"] += 1
                        for j in range(nb):
                            m = pe.do(lambda e, t=t, j=j, a=at: e.transpose(
                                bank_t[t][:, j * P:(j + 1) * P], prob[:, z, a + j * P:a + (j + 1) * P],
                                ident[:, :]), prob_w, free_t[t])
                        prob_read[z] = m
                        if pending_values["do"]:
                            pending_values["do"]()
                        if g == 1:
                            w = act.do(lambda e, t=t, y=y, nb=nb: e.activation(
                                prob_t[:, y, 0:nb * P], bank_t[t][:, 0:nb * P], ACT.Copy), m, pt_read[y])
                        else:
                            w = dve.do(lambda e, t=t, y=y, nb=nb: e.tensor_copy(
                                prob_t[:, y, 0:nb * P], bank_t[t][:, 0:nb * P]), m, pt_read[y])
                        free_t[t] = w

                        def rest(g=g, k0=k0, nb=nb, y=y, w=w):
                            head = (g * SLOTS + s) * HEAD
                            for j in range(nb):
                                m2 = pe.do(lambda e, j=j: e.matmul(
                                    bank_o[po:po + 64, 0:P], v_tok[:, k0 + j, head:head + HEAD],
                                    prob_t[:, y, j * P:(j + 1) * P], start=(g == 1 and j == 0),
                                    stop=(g == 0 and j == nb - 1)), w, v_w, free_o[0])
                            pt_read[y] = m2
                            if g == 0:
                                free_o[0] = dve.do(lambda e: e.tensor_copy(
                                    o_f[po:po + 64, s // 2, blk * P:(blk + 1) * P], bank_o[po:po + 64, 0:P]), m2)
                                o_w.append(free_o[0])
                        pending_values["do"] = rest

                units = [(s, blk) for blk in range(TB) for s in range(SLOTS)]
                marks = {}
                for u in range(len(units) + 1):
                    if u < len(units):
                        marks[u] = dilated_scores(u, *units[u])
                        if u < 4:
                            stick_panel(12 + u)
                        else:
                            gate_panel()
                    if u:
                        dilated_values(u - 1, *units[u - 1], marks[u - 1])

                pending_values["do"]()
                place = [(0, 0), (1, 0), (2, 0), (1, 384)]
                flat = [0, 512, 1024, 896]

                def stick_scores(h):
                    z, po, ch = h % 2, 64 * (h % 2), h // 2
                    for kb in range(TB):
                        bk, c0 = place[kb]
                        w = T - kb * P
                        m = pe.do(lambda e, bk=bk, c0=c0, w=w, kb=kb: e.matmul(
                            bank_s[:, bk, c0:c0 + w], qk[po:po + 64, 14 + ch, kb * P:(kb + 1) * P],
                            qk[po:po + 64, 12 + ch, kb * P:T], start=(c0 == 0), stop=False,
                            skip_group_check=True), qk_w[12 + ch], qk_w[14 + ch], free_s[bk])
                    sizes = (512, 512, 256)
                    for bk, n in enumerate(sizes):
                        a = act.do(lambda e, bk=bk, n=n: e.activation(
                            prob[:, z, bk * 512:bk * 512 + n], bank_s[:, bk, 0:n], ACT.Abs), m, prob_read[z])
                    a = act.do(lambda e: e.activation(prob[:, z, :], prob[:, z, :], ACT.Exp, scale=-1.0), a)
                    a = act.do(lambda e: e.activation(prob[:, z, :], prob[:, z, :], ACT.Ln, bias=1.0), a)
                    done = []
                    for bk, n in enumerate(sizes):
                        done.append(dve.do(lambda e, bk=bk, n=n: e.scalar_tensor_tensor(
                            prob[:, z, bk * 512:bk * 512 + n], bank_s[:, bk, 0:n], 0.0,
                            prob[:, z, bk * 512:bk * 512 + n], ALU.max, ALU.add), a))
                    for kb in range(TB):
                        done.append(dve.do(lambda e, f=flat[kb]: e.tensor_tensor(
                            prob[:, z, f:f + P], prob[:, z, f:f + P], strict[:, :], ALU.mult),
                            done[0:3], loads["strict"]))
                    return done

                def stick_weights(h, nlk):
                    z = h % 2
                    for kb in range(TB):
                        bk, c0 = place[kb]
                        w = T - kb * P
                        pe.run(lambda e, bk=bk, c0=c0: e.matmul(
                            bank_s[:, bk, c0:c0 + P], ident_bf[:, :], masks_f[:, 10 * P:11 * P],
                            start=False, stop=False, skip_group_check=True), nlk)
                        pe.run(lambda e, bk=bk, c0=c0, w=w, f=flat[kb]: e.matmul(
                            bank_s[:, bk, c0:c0 + w], suffix[:, :], prob[:, z, f:f + w],
                            start=False, stop=False, skip_group_check=True), loads["suffix"], loads["minus"])
                        for k2 in range(kb + 1, TB):
                            w2, f2 = T - k2 * P, flat[k2]
                            c2 = c0 + (k2 - kb) * P
                            pe.run(lambda e, bk=bk, c=c2, w=w2, f=f2: e.matmul(
                                bank_s[:, bk, c:c + w], minus[:, :], prob[:, z, f:f + w],
                                start=False, stop=False, skip_group_check=True))
                    m = pe.do(lambda e: e.matmul(bank_s[:, 2, 0:1], ident_bf[:, :], masks_f[:, 0:1], start=False,
                                                 stop=True, skip_group_check=True))
                    for bk, n in enumerate((512, 512, 256)):
                        a = act.do(lambda e, bk=bk, n=n: e.activation(
                            prob[:, z, bk * 512:bk * 512 + n], bank_s[:, bk, 0:n], ACT.Exp), m)
                        free_s[bk] = a
                    return a

                def stick_values(h, weights):
                    z, po = h % 2, 64 * (h % 2)
                    for kb in range(TB):
                        f, w = flat[kb], T - kb * P
                        m = pe.do(lambda e, kb=kb, f=f, w=w: e.matmul(
                            bank_o[po:po + 64, kb * P:T], v_tok[:, kb, 768 + h * HEAD:768 + (h + 1) * HEAD],
                            prob[:, z, f:f + w], start=(kb == 0), stop=(kb == TB - 1),
                            skip_group_check=True), weights, free_o[0], v_w)
                    prob_read[z] = m
                    free_o[0] = dve.do(lambda e: e.tensor_copy(o_f[po:po + 64, 2 + h // 2, :],
                                                               bank_o[po:po + 64, :]), m)
                    o_w.append(free_o[0])

                prev = None
                for h in range(4):
                    nlk = stick_scores(h)
                    gate_panel()
                    if prev:
                        stick_values(*prev)
                    prev = (h, stick_weights(h, nlk))
                stick_values(*prev)
                fence()
                work.close()
                att.close()

                o_hi = sb(phase, f"o_hi_{l}", [P, 4, T], F32R)
                o_lo = sb(phase, f"o_lo_{l}", [P, 4, T], F32R)
                y_hi = sb(phase, f"y_hi_{l}", [P, DC, T], F32R)
                y_lo = sb(phase, f"y_lo_{l}", [P, DC, T], F32R)
                part = sb(phase, f"part_{l}", [P, 2, 2, T])
                o_ready = [split_value(o_hi[:, c, :], o_lo[:, c, :], o_f[:, c, :], o_w) for c in range(4)]
                part_read = [None, None]
                y_w = [None] * DC

                def split_y(m, w):
                    y_w[m] = part_read[m % 2] = split_value(y_hi[:, m, :], y_lo[:, m, :], part[:, m % 2, 0, :], w)

                for m in range(DC):
                    for f in range(2):
                        sg = act.do(lambda e, i=8 * f + m: e.activation(gates[:, i, :], gates[:, i, :], ACT.Sigmoid),
                                    gate_w[8 * f + m])
                        b = next_l()
                        done = product(f"proj_{('dil', 'sb')[f]}_{l}", lambda c, f=f: o_hi[:, 2 * f + c, :],
                                       lambda c, f=f: o_lo[:, 2 * f + c, :], bank_l[b][:, :],
                                       o_ready[2 * f:2 * f + 2], free_l[b])
                        z = m % 2
                        free_l[b] = dve.do(lambda e, b=b, z=z, f=f, i=8 * f + m: e.tensor_tensor(
                            part[:, z, f, :], bank_l[b][:, :], gates[:, i, :], ALU.mult),
                            done, sg, part_read[z])
                    w = pool.do(lambda e, z=z: e.tensor_tensor(part[:, z, 0, :], part[:, z, 0, :],
                                                               part[:, z, 1, :], ALU.add), dve.last)
                    if m:
                        split_y(m - 1, summed)
                    summed = w
                split_y(DC - 1, summed)
                for m in range(DC):
                    b = next_l()
                    done = product(f"out_{l}", lambda c: y_hi[:, c, :], lambda c: y_lo[:, c, :],
                                   bank_l[b][:, :], y_w, free_l[b])
                    add_to_x(m, b, done, 1.0, g_out)
                state["owed"], state["rstd_read"] = token_rstd, dve.last

        mixer_1()
        ident_bf_ready = act.do(lambda e: e.activation(ident_bf[:, :], ident[:, :], ACT.Copy),
                                loads["ident"])
        gained_sum = sb(stack, "gained_sum", [P, T])
        first_rstd = sb(stack, "first_rstd", [P, T])
        gain_pair = sb(stack, "gain_pair", [P, 2 * DC])
        mixture()
        normalise_between(2, 3)
        for l in range(DEPTH_2):
            feed_forward(f"ff1_{l}", f"ff1_gate_{l}", f"ff1_up_{l}", f"ff1_down_{l}", FF_GROUPS, 0.5, 4 + 3 * l)
            mixer_2(l)
            last = l == DEPTH_2 - 1
            feed_forward(f"ff2_{l}", f"ff2_gate_{l}", f"ff2_up_{l}", f"ff2_down_{l}", FF_GROUPS, 0.5,
                         None if last else 3 + 3 * (l + 1))
        settle()
        normalise(3 + 3 * DEPTH_2)
        sync.wait((stored, 16 * DC))

        block = stack.enter_context(nc.Block())

        def body(engine):
            def emit(e):
                for op in engine.ops:
                    op(e)
            return emit
        block.sync(body(sync))
        block.scalar(body(act))
        block.gpsimd(body(pool))
        block.vector(body(dve))
        block.tensor(body(pe))


def constants():
    i = np.arange(P)
    causal = i[:, None] >= i[None, :]
    masks = []
    for w, d in zip(WINDOWS, DILATIONS):
        near = (i[:, None] - i[None, :]) % d == 0
        diag = near & causal
        far = near & (i[:, None] + P - i[None, :] <= w) if w == P else near
        masks += [far] * (1 if w == P else 3) + [diag]
    masks.append(i[:, None] < i[None, :])
    masks = np.where(np.concatenate(masks, 1), 0.0, MASKED)
    pos = np.arange(T, dtype=np.float32)
    inv = np.float32(ROPE_THETA) ** (-np.arange(0, ROPE_DIM, 2, dtype=np.float32) / np.float32(ROPE_DIM))
    ang = (pos[:, None] * inv[None, :]).astype(np.float32)
    half = ROPE_DIM // 2
    cos, sin = np.ones((P, T), np.float32), np.zeros((P, T), np.float32)
    rotate = np.zeros((P, P), np.float32)
    for h in range(0, P, HEAD):
        cos[h:h + half] = cos[h + half:h + ROPE_DIM] = np.cos(ang).T
        sin[h:h + half], sin[h + half:h + ROPE_DIM] = -np.sin(ang).T, np.sin(ang).T
        for a in range(half):
            rotate[h + a, h + half + a] = rotate[h + half + a, h + a] = 1.0
    resets = np.ones((P, META + T), np.float32)
    resets[:, META::CHUNK] = 0.0
    same = (i[:, None] // CHUNK) == (i[None, :] // CHUNK)
    gla_mask = np.tile((same & (i[:, None] <= i[None, :])).astype(np.int32), (1, TB))
    return {
        "ident": np.eye(P, dtype=np.float32), "ones": np.ones((P, P), np.float32),
        "rotate": rotate, "cos": cos, "sin": sin,
        "suffix": np.where(i[:, None] >= i[None, :], -1.0, 0.0).astype(np.float32),
        "minus": np.full((P, P), -1.0, np.float32),
        "strict": (i[:, None] < i[None, :]).astype(np.float32),
        "masks": masks, "resets": resets, "gla_mask": gla_mask,
        "token_id": (np.arange(TB)[None, :] * P + i[:, None]).astype(np.float32),
        "columns": np.broadcast_to(i[None, :].astype(np.float32), (P, P)).copy(),
        "bounds": np.broadcast_to(np.arange(TILES + 1, dtype=np.float32) * P, (P, 1, TILES + 1)).copy(),
        "numbers": np.broadcast_to(np.arange(OVERFLOW, dtype=np.float32)[None, :, None],
                                   (1, OVERFLOW, N_EXPERTS)).copy(),
        "first_slot": np.broadcast_to(np.arange(N_EXPERTS, dtype=np.float32) * P, (P, N_EXPERTS)).copy(),
        "rank": np.broadcast_to(np.arange(4, 0, -1, dtype=np.float32), (P, TB, 4)).copy(),
    }


def kernel(**a):
    import ml_dtypes
    import concourse.bacc as bacc
    from concourse.bass_utils import run_bass_kernel_spmd

    a = {k: np.asarray(v) for k, v in a.items()}

    def chunks(v):
        return v.reshape(-1, P).T

    def feature_major(v):
        return np.ascontiguousarray(v.T.reshape(DC, P, -1).transpose(1, 0, 2))

    def padded(w):
        return np.pad(w, ((0, 0), (0, P - w.shape[1])))

    w_in = a["w_in"][0]
    source = {
        "pool": w_in[:, 0:512], "q": w_in[:, 512:768], "k": w_in[:, 768:1024], "v": w_in[:, 1024:1536],
        "r": w_in[:, 1536:2048], "g": padded(w_in[:, 2048:2064]), "out": a["w_out"][0],
        "route": padded(np.concatenate([a["w_router_group"][0], a["w_router_expert"][0]], 1)),
    }
    for l in range(DEPTH_2):
        for f in (1, 2):
            for part in ("gate", "up", "down"):
                source[f"ff{f}_{part}_{l}"] = a[f"ffn{f}_w_{part}_2"][l]
        source[f"in_{l}"] = a["w_in_2"][l]
        source[f"proj_dil_{l}"] = a["w_proj_dil_2"][l]
        source[f"proj_sb_{l}"] = a["w_proj_sb_2"][l]
        source[f"out_{l}"] = a["w_out_2"][l]
    arrays = {}
    for name, panels in weight_matrices().items():
        w = source[name]
        arrays[name] = np.concatenate([
            w[r:r + rows, c:c + cols].reshape(rows // P, P, cols).transpose(1, 0, 2).ravel()
            for r, rows, c, cols in panels])
    gate_up = np.concatenate([a["w_expert_gate"][0], a["w_expert_up"][0]], 2)
    arrays["experts"] = np.concatenate([
        gate_up.reshape(N_EXPERTS, GU_PANELS, 2, P, 512).transpose(0, 1, 3, 2, 4).reshape(
            N_EXPERTS, GU_PANELS, P, PANEL),
        a["w_expert_down"][0].reshape(N_EXPERTS, 2, P, D)], 1)
    gains = [a["norm_mix_w"][0], a["norm_ffn_w"][0], a["final_norm_w"]]
    for l in range(DEPTH_2):
        gains += [a["norm_ffn1_2"][l], a["norm_mix_2"][l], a["norm_ffn2_2"][l]]
    gains.append(a["norm_final_2"])
    arrays.update(constants())
    arrays["masks"] = arrays["masks"].astype(ml_dtypes.bfloat16)
    arrays.update({
        "x_t": feature_major(a["x"][0]), "meta_t": feature_major(a["meta_tokens"]),
        "gains": np.ascontiguousarray(np.concatenate([chunks(g) for g in gains], 1)),
        "w_gate_up": a["w_gate_up"][0],
        "vecs": np.ascontiguousarray(np.concatenate(
            [chunks(a["b_gate"][0]), chunks(a["pool_scale"][0]), chunks(a["gla_norm_w"][0])], 1)),
        "pool_w": np.ascontiguousarray(a["pool_w"][0].transpose(1, 0, 2)),
        "router_bias": np.concatenate([a["b_router_group"][0], a["b_router_expert"][0]])[:, None].copy(),
    })

    nc = bacc.Bacc("TRN2", target_bir_lowering=False, num_devices=1)
    dram = {n: nc.dram_tensor(f"in_{n}", v.shape, mybir.dt.from_np(v.dtype), kind="ExternalInput").ap()
            for n, v in arrays.items()}
    out = nc.dram_tensor("out_t", (P, DC, T), F32, kind="ExternalOutput").ap()
    build(nc, dram, out)
    r = run_bass_kernel_spmd(nc, [{f"in_{n}": v for n, v in arrays.items()}], core_ids=[0])
    got = r.results[0]["out_t"]
    return got.transpose(2, 1, 0).reshape(1, T, D)
```
